# Optimizing a Trainium2 kernel written in Bass

```python
import math
import jax, jax.numpy as jnp
from jax import lax
import numpy as np

D_MODEL = 1024
BATCH = 1
SEQ = 256
DEPTH = 1
DEC_BATCH = 8
DEC_SEQ = 1
PAST_LEN = 2048
PAGE_SIZE = 128

RET_HEADS = 8
RET_DV = D_MODEL // RET_HEADS
RET_DK = RET_DV
RET_WIDTH = RET_HEADS * RET_DV
RET_CHUNK = 128
ROPE_BASE = 10000.0
RET_GN_EPS = 1e-5
RWKV_HEAD = 64
RWKV_HEADS = D_MODEL // RWKV_HEAD
RWKV_WIDTH = RWKV_HEADS * RWKV_HEAD
LORA_DECAY = max(32, int(round(D_MODEL ** 0.5 * 1.8 / 32)) * 32)
LORA_A = max(32, int(round(D_MODEL ** 0.5 * 1.8 / 32)) * 32)
LORA_G = max(32, int(round(D_MODEL ** 0.8 * 0.6 / 32)) * 32)
RWKV_GN_EPS = 64e-5
OFF_Q = 0
OFF_K = OFF_Q + RET_HEADS * RET_DK
OFF_V = OFF_K + RET_HEADS * RET_DK
OFF_GSW = OFF_V + RET_WIDTH
OFF_SHIFT = OFF_GSW + RET_WIDTH
N_SHIFT = 3 * RWKV_WIDTH + LORA_DECAY + LORA_A + LORA_G
OFF_GATE_A = OFF_SHIFT + N_SHIFT
OFF_GATE_B = OFF_GATE_A + D_MODEL
N_IN = OFF_GATE_B + D_MODEL
SHIFT_SPLITS = (RWKV_WIDTH, 2 * RWKV_WIDTH, 3 * RWKV_WIDTH,
                3 * RWKV_WIDTH + LORA_DECAY, 3 * RWKV_WIDTH + LORA_DECAY + LORA_A)
N_GROUPS = 4
EXPERTS_PER_GROUP = 8
N_EXPERTS = N_GROUPS * EXPERTS_PER_GROUP
TOP_K = 2
D_EXPERT = 256
RMS_EPS = 1e-6

kernel_name = 'retnet_rwkv7_gated_hier_moe_step'

F32 = jnp.float32

def _rmsnorm(x, g):
    xf = x.astype(F32)
    y = xf * lax.rsqrt(jnp.mean(xf * xf, axis=-1, keepdims=True) + RMS_EPS)
    return (y * g.astype(F32)).astype(x.dtype)

def _head_norm(x, eps):
    mu = jnp.mean(x, axis=-1, keepdims=True)
    xc = x - mu
    return xc * lax.rsqrt(jnp.mean(xc * xc, axis=-1, keepdims=True) + eps)

def _rope(x, pos):
    half = x.shape[-1] // 2
    inv = ROPE_BASE ** (-jnp.arange(half, dtype=F32) / half)
    ang = pos[:, None] * inv[None, :]
    cos = jnp.cos(ang)[None, :, None, :]
    sin = jnp.sin(ang)[None, :, None, :]
    x1, x2 = x[..., :half], x[..., half:]
    return jnp.concatenate([x1 * cos - x2 * sin, x1 * sin + x2 * cos], axis=-1)

def _retention(q, k, v, s0):
    B, L, H, DK = q.shape
    DV = v.shape[-1]
    C = math.gcd(L, RET_CHUNK)
    n = L // C
    log_gamma = jnp.log1p(-jnp.exp2(-5.0 - jnp.arange(H, dtype=F32)))
    idx = jnp.arange(C, dtype=F32)
    rel = idx[:, None] - idx[None, :]
    intra = jnp.where(rel[None] >= 0, jnp.exp(jnp.maximum(rel, 0.0)[None] * log_gamma[:, None, None]), 0.0)
    q_dec = jnp.exp((idx[:, None] + 1.0) * log_gamma[None, :])
    k_dec = jnp.exp((C - 1.0 - idx)[None, :] * log_gamma[:, None])
    chunk_dec = jnp.exp(C * log_gamma)

    def blocks(t):
        return t.reshape(B, n, C, H, t.shape[-1]).transpose(1, 0, 2, 3, 4)

    def step(S, inp):
        qc, kc, vc = inp
        scores = jnp.einsum('bihd,bjhd->bhij', qc, kc) * intra[None]
        inner = jnp.einsum('bhij,bjhe->bihe', scores, vc)
        cross = jnp.einsum('bihd,bhde->bihe', qc, S) * q_dec[None, :, :, None]
        S_new = S * chunk_dec[None, :, None, None] + jnp.einsum('bjhd,bjhe,hj->bhde', kc, vc, k_dec)
        return S_new, inner + cross

    S, out = lax.scan(step, s0, (blocks(q), blocks(k), blocks(v)))
    return out.transpose(1, 0, 2, 3, 4).reshape(B, L, H, DV), S

def _rwkv7_recurrence(r, w, k, v, a, b, s0):
    def step(S, inp):
        r_t, w_t, k_t, v_t, a_t, b_t = inp
        sa = jnp.einsum('bhij,bhj->bhi', S, a_t)
        S = S * w_t[:, :, None, :] + sa[..., None] * b_t[:, :, None, :] + v_t[..., None] * k_t[:, :, None, :]
        return S, jnp.einsum('bhij,bhj->bhi', S, r_t)

    seq = (r.transpose(1, 0, 2, 3), w.transpose(1, 0, 2, 3), k.transpose(1, 0, 2, 3),
           v.transpose(1, 0, 2, 3), a.transpose(1, 0, 2, 3), b.transpose(1, 0, 2, 3))
    S, y = lax.scan(step, s0, seq)
    return y.transpose(1, 0, 2, 3), S

def _mixer(xn, prev_row, pos, s_ret, s_rwkv, p):
    B, L, _ = xn.shape
    proj = jnp.concatenate([prev_row[:, None, :].astype(xn.dtype), xn], axis=1) @ p['w_in']
    cur, prev = proj[:, 1:], proj[:, :-1]

    def heads(t, h):
        return t.reshape(B, L, h, -1).astype(F32)

    q = _rope(heads(cur[..., OFF_Q:OFF_K], RET_HEADS), pos)
    k = _rope(heads(cur[..., OFF_K:OFF_V], RET_HEADS), pos) * (RET_DK ** -0.5)
    v = heads(cur[..., OFF_V:OFF_GSW], RET_HEADS)
    o_ret, s_ret_new = _retention(q, k, v, s_ret.astype(F32))
    o_ret = (_head_norm(o_ret, RET_GN_EPS).reshape(B, L, RET_WIDTH) * p['ret_gn_w'].astype(F32)
             * jax.nn.silu(cur[..., OFF_GSW:OFF_SHIFT].astype(F32)))

    sh = cur[..., OFF_SHIFT:OFF_GATE_A].astype(F32)
    sh = sh + (prev[..., OFF_SHIFT:OFF_GATE_A].astype(F32) - sh) * p['mu_shift'].astype(F32)
    r_, k_, v_, w_lo, a_lo, g_lo = jnp.split(sh, SHIFT_SPLITS, axis=-1)
    w_log = -jax.nn.softplus(-(p['rwkv_w0'].astype(F32) + jnp.tanh(w_lo) @ p['rwkv_w2'].astype(F32))) - 0.5
    decay = jnp.exp(-jnp.exp(w_log))
    a = jax.nn.sigmoid(p['rwkv_a0'].astype(F32) + a_lo @ p['rwkv_a2'].astype(F32))
    g = jax.nn.sigmoid(g_lo) @ p['rwkv_g2'].astype(F32)
    kk = heads(k_ * p['rwkv_k_k'].astype(F32), RWKV_HEADS)
    kk = kk / jnp.maximum(jnp.sqrt(jnp.sum(kk * kk, axis=-1, keepdims=True)), 1e-12)
    kmod = k_ * (1.0 + (a - 1.0) * p['rwkv_k_a'].astype(F32))
    rh = heads(r_, RWKV_HEADS)
    kh = heads(kmod, RWKV_HEADS)
    vh = heads(v_, RWKV_HEADS)
    ah = heads(a, RWKV_HEADS)
    y, s_rwkv_new = _rwkv7_recurrence(rh, heads(decay, RWKV_HEADS), kh, vh, -kk, kk * ah, s_rwkv.astype(F32))
    y = (_head_norm(y, RWKV_GN_EPS).reshape(B, L, RWKV_WIDTH) * p['rwkv_lnx_w'].astype(F32)
         + p['rwkv_lnx_b'].astype(F32))
    bonus = (jnp.sum(rh * kh * p['rwkv_r_k'].astype(F32), axis=-1, keepdims=True) * vh).reshape(B, L, RWKV_WIDTH)
    o_rwkv = (y + bonus) * g

    gate_a = jax.nn.sigmoid(cur[..., OFF_GATE_A:OFF_GATE_B].astype(F32))
    gate_b = jax.nn.sigmoid(cur[..., OFF_GATE_B:N_IN].astype(F32))
    merged = (gate_a * o_ret + gate_b * o_rwkv).astype(xn.dtype)
    return merged @ p['w_out'], s_ret_new.astype(s_ret.dtype), s_rwkv_new.astype(s_rwkv.dtype)

def _hier_moe(x, p):
    B, L, D = x.shape
    T = B * L
    xf = x.reshape(T, D)
    g_logit = (xf @ p['router_group_w'] + p['router_group_b']).astype(F32)
    g_prob = jax.nn.softmax(g_logit, axis=-1)
    g_sel = jnp.argmax(g_logit, axis=-1)
    g_w = jnp.take_along_axis(g_prob, g_sel[:, None], axis=-1)
    e_logit = (xf @ p['router_expert_w'] + p['router_expert_b']).astype(F32).reshape(T, N_GROUPS, EXPERTS_PER_GROUP)
    e_logit = jnp.take_along_axis(e_logit, g_sel[:, None, None], axis=1)[:, 0]
    e_prob = jax.nn.softmax(e_logit, axis=-1)
    top_p, top_i = lax.top_k(e_prob, TOP_K)
    top_w = g_w * top_p / jnp.sum(top_p, axis=-1, keepdims=True)
    expert_id = g_sel[:, None] * EXPERTS_PER_GROUP + top_i
    combine = jnp.sum(jax.nn.one_hot(expert_id, N_EXPERTS, dtype=F32) * top_w[..., None], axis=1)
    h = (jax.nn.silu(jnp.einsum('td,edf->tef', xf, p['expert_w_gate']))
         * jnp.einsum('td,edf->tef', xf, p['expert_w_up']))
    h = h * combine[..., None].astype(h.dtype)
    y = jnp.einsum('tef,efd->td', h, p['expert_w_down'])
    return y.reshape(B, L, D).astype(x.dtype)

def _trunk(x, pos, s_ret, s_rwkv, s_shift, layers, norm_final):
    new_ret, new_rwkv, new_shift = [], [], []
    for l in range(DEPTH):
        p = layers[l]
        xn = _rmsnorm(x, p['norm_mix'])
        m, sr, sw = _mixer(xn, s_shift[l], pos, s_ret[l], s_rwkv[l], p)
        x = x + m.astype(x.dtype)
        x = x + _hier_moe(_rmsnorm(x, p['norm_ffn']), p)
        new_ret.append(sr)
        new_rwkv.append(sw)
        new_shift.append(xn[:, -1].astype(s_shift.dtype))
    return _rmsnorm(x, norm_final), jnp.stack(new_ret), jnp.stack(new_rwkv), jnp.stack(new_shift)

def setup_inputs(seed: int = 0) -> dict:
    key = jax.random.key(seed)
    ks = iter(jax.random.split(key, 32))
    L = DEPTH

    def nrm(shape, s):
        return jax.random.normal(next(ks), shape, F32) * s

    def unif(shape, lo, hi):
        return jax.random.uniform(next(ks), shape, F32, lo, hi)

    return {
        'x_prompt': nrm((BATCH, SEQ, D_MODEL), 1.0),
        'x_sample': nrm((DEC_BATCH, DEC_SEQ, D_MODEL), 1.0),
        'state_ret': nrm((L, DEC_BATCH, RET_HEADS, RET_DK, RET_DV), 0.5),
        'state_rwkv': nrm((L, DEC_BATCH, RWKV_HEADS, RWKV_HEAD, RWKV_HEAD), 0.1),
        'state_shift': nrm((L, DEC_BATCH, D_MODEL), 1.0),
        'norm_mix': 1.0 + nrm((L, D_MODEL), 0.1),
        'w_in': nrm((L, D_MODEL, N_IN), D_MODEL ** -0.5),
        'mu_shift': unif((L, N_SHIFT), 0.0, 1.0),
        'ret_gn_w': 1.0 + nrm((L, D_MODEL), 0.1),
        'rwkv_w0': unif((L, D_MODEL), -6.0, -1.0),
        'rwkv_w2': nrm((L, LORA_DECAY, D_MODEL), 0.1),
        'rwkv_a0': nrm((L, D_MODEL), 0.1),
        'rwkv_a2': nrm((L, LORA_A, D_MODEL), 0.1),
        'rwkv_g2': nrm((L, LORA_G, D_MODEL), LORA_G ** -0.5),
        'rwkv_k_k': 0.85 + nrm((L, D_MODEL), 0.05),
        'rwkv_k_a': 1.0 + nrm((L, D_MODEL), 0.05),
        'rwkv_r_k': nrm((L, RWKV_HEADS, RWKV_HEAD), 0.1),
        'rwkv_lnx_w': 1.0 + nrm((L, D_MODEL), 0.1),
        'rwkv_lnx_b': nrm((L, D_MODEL), 0.02),
        'w_out': nrm((L, D_MODEL, D_MODEL), D_MODEL ** -0.5),
        'norm_ffn': 1.0 + nrm((L, D_MODEL), 0.1),
        'router_group_w': nrm((L, D_MODEL, N_GROUPS), D_MODEL ** -0.5),
        'router_group_b': nrm((L, N_GROUPS), 0.01),
        'router_expert_w': nrm((L, D_MODEL, N_EXPERTS), D_MODEL ** -0.5),
        'router_expert_b': nrm((L, N_EXPERTS), 0.01),
        'expert_w_gate': nrm((L, N_EXPERTS, D_MODEL, D_EXPERT), D_MODEL ** -0.5),
        'expert_w_up': nrm((L, N_EXPERTS, D_MODEL, D_EXPERT), D_MODEL ** -0.5),
        'expert_w_down': nrm((L, N_EXPERTS, D_EXPERT, D_MODEL), D_EXPERT ** -0.5),
        'norm_final': 1.0 + nrm((D_MODEL,), 0.1),
    }

def reference(x_prompt, x_sample, state_ret, state_rwkv, state_shift,
              norm_mix, w_in, mu_shift, ret_gn_w,
              rwkv_w0, rwkv_w2, rwkv_a0, rwkv_a2, rwkv_g2, rwkv_k_k, rwkv_k_a, rwkv_r_k,
              rwkv_lnx_w, rwkv_lnx_b, w_out, norm_ffn,
              router_group_w, router_group_b, router_expert_w, router_expert_b,
              expert_w_gate, expert_w_up, expert_w_down, norm_final):
    layers = [dict(norm_mix=norm_mix[l], w_in=w_in[l], mu_shift=mu_shift[l], ret_gn_w=ret_gn_w[l],
                   rwkv_w0=rwkv_w0[l], rwkv_w2=rwkv_w2[l], rwkv_a0=rwkv_a0[l], rwkv_a2=rwkv_a2[l],
                   rwkv_g2=rwkv_g2[l], rwkv_k_k=rwkv_k_k[l], rwkv_k_a=rwkv_k_a[l], rwkv_r_k=rwkv_r_k[l],
                   rwkv_lnx_w=rwkv_lnx_w[l], rwkv_lnx_b=rwkv_lnx_b[l], w_out=w_out[l], norm_ffn=norm_ffn[l],
                   router_group_w=router_group_w[l], router_group_b=router_group_b[l],
                   router_expert_w=router_expert_w[l], router_expert_b=router_expert_b[l],
                   expert_w_gate=expert_w_gate[l], expert_w_up=expert_w_up[l],
                   expert_w_down=expert_w_down[l])
              for l in range(DEPTH)]
    Bp, Lp, _ = x_prompt.shape
    pos_p = jnp.arange(Lp, dtype=F32)
    ret0 = jnp.zeros((DEPTH, Bp, RET_HEADS, RET_DK, RET_DV), state_ret.dtype)
    rwkv0 = jnp.zeros((DEPTH, Bp, RWKV_HEADS, RWKV_HEAD, RWKV_HEAD), state_rwkv.dtype)
    shift0 = jnp.zeros((DEPTH, Bp, D_MODEL), state_shift.dtype)
    y_prompt, ret_p, rwkv_p, shift_p = _trunk(x_prompt, pos_p, ret0, rwkv0, shift0, layers, norm_final)
    pos_s = PAST_LEN + jnp.arange(x_sample.shape[1], dtype=F32)
    y_sample, ret_s, rwkv_s, shift_s = _trunk(x_sample, pos_s, state_ret, state_rwkv, state_shift, layers, norm_final)
    return (y_prompt, y_sample, ret_p, rwkv_p, shift_p, ret_s, rwkv_s, shift_s)


_drawn_inputs = setup_inputs


def setup_inputs(seed=0):
    import zlib

    import numpy as np

    out = dict(_drawn_inputs(seed))
    spreads = {}
    factors = {'rwkv_lnx_b': 4.655, 'router_group_b': 3.383, 'router_expert_b': 4.911}
    for name, (base, spread) in spreads.items():
        noise = np.random.default_rng([zlib.crc32(name.encode()), seed]).standard_normal(out[name].shape)
        drawn = base * np.exp(spread * noise) if base else spread * noise
        out[name] = __import__('jax').numpy.asarray(drawn.astype(out[name].dtype))
    for name, factor in factors.items():
        out[name] = (out[name] * factor).astype(out[name].dtype)
    return out
```

```python
from contextlib import ExitStack

import numpy as np

import concourse.bass as bass
from concourse import mybir

ALU = mybir.AluOpType
ACT = mybir.ActivationFunctionType
F32 = mybir.dt.float32
I32 = mybir.dt.int32
AX_X = mybir.AxisListType.X

P = 128
D = 1024
KT = D // P
TP = 256
TT = TP // P
B = 8
T = TP + B
TX = T + B
HEADS = 8
RH = 16
HD = 64
C = 64
NCH = TP // C
PAST = 2048
NG, EPG = 4, 8
NE = NG * EPG
DE = 256
SLOTS = 96
LORA = 64
LORA_G = 160
RMS_EPS, RET_EPS, RWKV_EPS = 1e-6, 1e-5, 64e-5

O_Q, O_K, O_V, O_GS = 0, D, 2 * D, 3 * D
O_SH = 4 * D
O_R, O_RK, O_RV = O_SH, O_SH + D, O_SH + 2 * D
O_LORA = O_SH + 3 * D
N_LORA = 2 * LORA + LORA_G
O_GA = O_LORA + N_LORA
O_GB = O_GA + D
N_IN = O_GB + D
SECTIONS = [O_R, O_RK, O_RV, O_Q, O_K, O_V, O_GS, O_GA, O_GB]

PAR = ["mu_r", "mu_k", "mu_v", "w0", "a0", "k_k", "k_a", "r_k", "lnx_w", "lnx_b", "gn_w"]
NPAR = len(PAR)
DERIVED = ["om_r", "om_k", "om_v", "w0h", "a0h", "om_ka"]
PX = {n: i for i, n in enumerate(PAR + DERIVED)}
NPX = len(PX)
LOGW_C = -0.5 * float(np.exp(-0.5))


def constants():
    out = {}
    half = P // 2
    inv = (10000.0 ** (-np.arange(half, dtype=np.float32) / np.float32(half))).astype(np.float32)
    pos = np.concatenate([np.arange(TP), np.full(B, PAST)]).astype(np.float32)
    ang = (inv[:, None] * pos[None, :]).astype(np.float32).astype(np.float64)
    cos, sin = np.cos(ang), np.sin(ang)
    cs = np.concatenate([cos, cos], 0)
    sn = np.concatenate([sin, -sin], 0)
    scale = P ** -0.5
    out["rope"] = np.stack([cs, sn, cs * scale, sn * scale], 1)
    lg = np.log1p(-np.exp2(-5.0 - np.arange(HEADS)))
    j = np.arange(P)[:, None]
    i0 = np.arange(TP)[None, :]
    dec = np.zeros((P, HEADS, TP + P))
    kd = np.zeros((P, HEADS, 3))
    for h in range(HEADS):
        dec[:, h, :TP] = np.where(i0 >= j, np.exp(np.maximum(i0 - j, 0) * lg[h]), 0)
        i1 = np.arange(P)[None, :]
        dec[:, h, TP:] = np.where(i1 >= j, np.exp(np.maximum(i1 - j, 0) * lg[h]), 0)
        for tt in range(TT):
            kd[:, h, tt] = np.exp((TP - 1 - tt * P - np.arange(P)) * lg[h])
        kd[:, h, 2] = np.exp(lg[h])
    out["retdec"] = dec
    out["retcol"] = kd
    s, t = np.meshgrid(np.arange(P), np.arange(P), indexing="ij")
    same64 = s // C == t // C
    same16 = s // 16 == t // 16
    m = np.zeros((P, 4, P))
    m[:, 0] = same16 & (s < t)
    m[:, 1] = same64 & (s <= t)
    m[:, 2] = same64 & (s < t)
    m[:, 3] = same64 & (s <= t)
    out["mk"] = m
    lo = np.zeros((P, 2, P))
    lo[:, 0] = same16 & (t < s)
    lo[:, 1] = same64 & ~same16 & (t < s)
    out["mlo"] = lo
    out["ident"] = np.eye(P)
    out["one64"] = (s // HD == t // HD).astype(np.float64)
    out["mean64"] = out["one64"] / HD
    out["mean128"] = np.ones((P, P)) / P
    sm = np.ones((P, T))
    sm[:, 0:TP:C] = 0
    sm[:, TP:] = 0
    out["scanm"] = sm
    out["tri"] = (s < t).astype(np.float64)
    out["ones"] = np.ones((P, P))
    out["id64"] = np.concatenate([np.eye(HD), np.eye(HD)], 0)
    out["slot"] = np.tile(np.arange(SLOTS)[None, :], (P, 1)).astype(np.float64)
    d8 = np.zeros((B, B, P))
    for b in range(B):
        d8[b, b] = 1
    out["diag8"] = d8
    return {k: np.ascontiguousarray(v.astype(np.float32)) for k, v in out.items()}


class Semaphores:

    def __init__(self, nc):
        self.nc = nc
        self.named = {}
        self.stack = ExitStack()

    def __call__(self, name):
        if name not in self.named:
            self.named[name] = self.stack.enter_context(self.nc.semaphore(name))
        return self.named[name]

    def next_phase(self):
        with self.nc.Block() as block:

            @block.gpsimd
            def _(pool):
                for handle in self.named.values():
                    pool.sem_clear(handle)

        self.named = {}
        self.stack.close()


def hybrid_moe_step(nc, a, o, k):
    w_in = a["w_in"][0].rearrange("(k p) c -> p k c", p=P)

    with ExitStack() as top:
        keep = {}

        def alloc(ctx, table, name, shape, dt=F32):
            table[name] = ctx.enter_context(nc.sbuf_tensor(name, shape, dt))
            return table[name]

        sem = Semaphores(nc)

        psum = [top.enter_context(nc.psum_tensor(f"bank{n}", [P, 512], F32)) for n in range(8)]
        cst = {}
        for n in ("ident", "one64", "mean64", "mean128", "tri", "ones", "slot", "id64"):
            alloc(top, cst, "c_" + n, list(k[n].shape))
        merged = alloc(top, keep, "merged", [P, KT, T])
        svec = alloc(top, keep, "svec", [P, KT, 6, B])
        spost = alloc(top, keep, "spost", [P, 3, KT, B])
        parc = alloc(top, keep, "parc", [P, NPX, KT])
        gbc = alloc(top, keep, "gbc", [P, D])
        eps = alloc(top, keep, "eps", [P, 4])

        mixer_phase(nc, a, o, k, w_in, alloc, sem, psum, cst, keep)
        sem.next_phase()
        sample_phase(nc, a, o, k, alloc, sem, psum, cst, keep)
        sem.next_phase()
        moe_phase(nc, a, o, k, alloc, sem, psum, cst, keep)
        sem.next_phase()


def mixer_phase(nc, a, o, k, w_in, alloc, sem, psum, cst, keep):
    with ExitStack() as ctx:
        sb = {}

        def buf(name, shape):
            return alloc(ctx, sb, name, shape)

        ident, one64, mean64, mean128 = (cst["c_" + n] for n in ("ident", "one64", "mean64", "mean128"))
        merged, svec, spost, parc, gbc, eps = (keep[n] for n in ("merged", "svec", "spost", "parc", "gbc", "eps"))
        rope = buf("rope", [P, 4, T])
        retdec = buf("retdec", [P, HEADS, TP + P])
        retcol = buf("retcol", [P, HEADS, 3])
        mk = buf("mk", [P, 4, P])
        mlo = buf("mlo", [P, 2, P])
        scanm = buf("scanm", [P, T])
        diag8 = buf("diag8", [B, B, P])

        xt = buf("xt", [P, KT, TX])
        wslot = [buf(f"wslot{n}", [P, KT, P]) for n in range(9)]
        lowa = buf("lowa", [P, D])
        g2a = buf("g2a", [P, D])
        g2b = buf("g2b", [LORA_G - P, D])
        lwa = buf("lwa", [P, T])
        lga = buf("lga", [P, T])
        lgb = buf("lgb", [LORA_G - P, T])
        mulora = buf("mulora", [P, 6])

        def tok(name):
            return buf(name, [P, T])

        pro = ExitStack()
        x_tok = alloc(pro, sb, "x_tok", [P, TT, D])
        xs_tok = alloc(pro, sb, "xs_tok", [2 * B, D])
        sq_junk = alloc(pro, sb, "sq_junk", [P, D])
        stat = alloc(pro, sb, "stat", [P, 3, 4])
        prow = alloc(pro, sb, "prow", [P, P])
        wlora = alloc(pro, sb, "wlora", [P, KT, N_LORA])
        mpro = alloc(pro, sb, "mpro", [P, 3, TX + 1])

        mult, add, sub = ALU.mult, ALU.add, ALU.subtract

        def mm(pe, out, lhsT, rhs, start, stop, loose=False):
            return nc.tensor.matmul(out, lhsT, rhs, start=start, stop=stop, skip_group_check=loose)

        with nc.Block() as block:

            @block.sync
            def _(sp):
                sp.dma_start(sb["x_tok"][:], a["x_prompt"][0].rearrange("(t p) d -> p t d", p=P)).then_inc(sem("x_in"), 16)
                sp.dma_start(sb["xs_tok"][0:B, :], a["x_sample"].rearrange("b t d -> (b t) d")).then_inc(sem("x_in"), 16)
                sp.dma_start(sb["xs_tok"][B:2 * B, :], a["state_shift"][0]).then_inc(sem("x_in"), 16)
                sp.dma_start(gbc[:], a["norm_mix"].partition_broadcast(P)).then_inc(sem("x_in"), 16)
                sp.dma_start(wlora[:], w_in[:, :, O_LORA:O_LORA + N_LORA]).then_inc(sem("wlora_in"), 16)
                sp.dma_start(lowa[0:LORA, :], a["rwkv_w2"][0]).then_inc(sem("lora_in"), 16)
                sp.dma_start(lowa[LORA:2 * LORA, :], a["rwkv_a2"][0]).then_inc(sem("lora_in"), 16)
                sp.dma_start(g2a[:], a["rwkv_g2"][0][0:P, :]).then_inc(sem("lora_in"), 16)
                sp.dma_start(g2b[:], a["rwkv_g2"][0][P:LORA_G, :]).then_inc(sem("lora_in"), 16)
                sp.wait_ge(sem("xn_ready"), 1)
                sp.dma_start(o["shift_p"][0, 0:1, :], sb["x_tok"][P - 1:P, TT - 1, :]).then_inc(sem("out_done"), 16)
                sp.dma_start(o["shift_s"][0], sb["xs_tok"][0:B, :]).then_inc(sem("out_done"), 16)
                sp.wait_ge(sem("out_done"), 32)
                sp.wait_ge(sem("lora_in"), 64)

            @block.scalar
            def _(act):
                act.wait_ge(sem("prow_zero"), 1)
                rows = [a["mu_shift"][0, n * D:(n + 1) * D] for n in range(3)]
                rows += [a[n][0] for n in ("rwkv_w0", "rwkv_a0", "rwkv_k_k", "rwkv_k_a")]
                rows += [a["rwkv_r_k"][0].rearrange("h c -> (h c)")]
                rows += [a[n][0] for n in ("rwkv_lnx_w", "rwkv_lnx_b", "ret_gn_w")]
                for n, row in enumerate(rows):
                    act.dma_start(prow[n * KT:(n + 1) * KT, :], row.rearrange("(k c) -> k c", c=P)).then_inc(sem("prow_in"), 16)
                lo = NPAR * KT
                mu = a["mu_shift"][0:1, :]
                act.dma_start(prow[lo:lo + 1, :], mu[:, 3 * D:3 * D + P]).then_inc(sem("prow_in"), 16)
                act.dma_start(prow[lo + 1:lo + 2, :], mu[:, 3 * D + P:3 * D + 2 * P]).then_inc(sem("prow_in"), 16)
                act.dma_start(prow[lo + 2:lo + 3, 0:LORA_G - P], mu[:, 3 * D + 2 * P:3 * D + N_LORA]).then_inc(sem("prow_in"), 16)
                for n in ("ident", "one64", "mean64", "mean128", "tri", "ones", "slot", "id64"):
                    act.dma_start(cst["c_" + n][:], k[n]).then_inc(sem("const_in"), 16)
                for n, t in (("rope", rope), ("retdec", retdec), ("retcol", retcol), ("mk", mk), ("mlo", mlo),
                             ("scanm", scanm), ("diag8", diag8)):
                    act.dma_start(t[:], k[n]).then_inc(sem("const_in"), 16)
                act.wait_ge(sem("x_in"), 64)
                act.wait_ge(sem("stat_zero"), 1)
                for t in range(TT):
                    act.activation(sq_junk[:], sb["x_tok"][:, t, :], ACT.Square, accum_out=stat[:, t, 0:1]).then_inc(sem("sq_done"), 1)
                    act.wait_ge(sem("sq_done"), t + 1)
                act.activation(sq_junk[0:B, :], sb["xs_tok"][0:B, :], ACT.Square, accum_out=stat[0:B, 2, 0:1]).then_inc(sem("sq_done"), 1)
                act.wait_ge(sem("ms_ready"), 1)
                act.activation(stat[:, :, 2:3], stat[:, :, 1:2], ACT.Sqrt).then_inc(sem("rms_ready"), 1)
                for kk in range(0, KT, 2):
                    act.wait_ge(sem("xt_mm"), kk + 1)
                    act.copy(xt[:, kk, :], psum[kk][:, 0:TX]).then_inc(sem("xt_act"), 1)
                for n, m in enumerate((P, P, LORA_G - P)):
                    act.wait_ge(sem("lora_mm"), n + 1)
                    act.wait_ge(sem("mulora_ready"), 2)
                    act.activation(mpro[0:m, n, 1:TX + 1], psum[n][0:m, 0:TX], ACT.Copy, scale=mulora[0:m, n:n + 1]).then_inc(sem("lora_mu"), 1)
                act.wait_ge(sem("lora_mix"), 1)
                act.activation(lwa[0:LORA, :], lwa[0:LORA, :], ACT.Tanh)
                act.wait_ge(sem("lora_mix"), 3)
                act.activation(lga[:], lga[:], ACT.Tanh, scale=0.5)
                act.activation(lgb[:], lgb[:], ACT.Tanh, scale=0.5).then_inc(sem("lora_tanh"), 1)

            @block.vector
            def _(dve):
                nc.vector.memset(prow[:], 0.0).then_inc(sem("prow_zero"), 1)
                nc.vector.memset(stat[:], 1.0).then_inc(sem("stat_zero"), 1)
                nc.vector.memset(mpro[:], 0.0).then_inc(sem("mpro_zero"), 1)
                nc.vector.memset(eps[:, 0:1], RET_EPS)
                nc.vector.memset(eps[:, 1:2], RWKV_EPS)
                nc.vector.memset(eps[:, 2:3], RMS_EPS)
                nc.vector.memset(eps[:, 3:4], 0.0).then_inc(sem("eps_ready"), 1)
                dve.wait_ge(sem("sq_done"), 3)
                nc.vector.tensor_scalar(stat[:, :, 1:2], stat[:, :, 0:1], 1.0 / D, RMS_EPS, mult, add).then_inc(sem("ms_ready"), 1)
                dve.wait_ge(sem("rms_ready"), 1)
                nc.vector.reciprocal(stat[:, :, 3:4], stat[:, :, 2:3]).then_inc(sem("rstd_ready"), 1)
                dve.wait_ge(sem("rstd_ready"), 1)
                for t in range(TT):
                    nc.vector.scalar_tensor_tensor(out=sb["x_tok"][:, t, :], in0=sb["x_tok"][:, t, :], scalar=stat[:, t, 3:4],
                                                   in1=gbc[:], op0=mult, op1=mult)
                nc.vector.scalar_tensor_tensor(out=sb["xs_tok"][0:B, :], in0=sb["xs_tok"][0:B, :], scalar=stat[0:B, 2, 3:4],
                                               in1=gbc[0:B, :], op0=mult, op1=mult).then_inc(sem("xn_ready"), 1)
                for kk in range(1, KT, 2):
                    dve.wait_ge(sem("xt_mm"), kk + 1)
                    nc.vector.tensor_copy(xt[:, kk, :], psum[kk][:, 0:TX]).then_inc(sem("xt_dve"), 1)
                dve.wait_ge(sem("par_mm"), 1)
                nc.vector.tensor_copy(parc[:, 0:NPAR, :], psum[7][:, 0:NPAR * KT].rearrange("p (n k) -> p n k", k=KT)).then_inc(sem("par_c"), 1)
                nc.vector.tensor_copy(mulora[:, 0:3], psum[7][:, NPAR * KT:NPAR * KT + 3]).then_inc(sem("mulora_ready"), 1)
                dve.wait_ge(sem("par_c"), 1)
                dve.wait_ge(sem("mulora_ready"), 1)
                nc.vector.tensor_scalar(mulora[:, 3:6], mulora[:, 0:3], -1.0, 1.0, mult, add).then_inc(sem("mulora_ready"), 1)
                nc.vector.tensor_scalar(parc[:, PX["om_r"]:PX["om_v"] + 1, :], parc[:, PX["mu_r"]:PX["mu_v"] + 1, :], -1.0, 1.0, mult, add)
                nc.vector.tensor_scalar(parc[:, PX["w0h"]:PX["a0h"] + 1, :], parc[:, PX["w0"]:PX["a0"] + 1, :], 0.5, None, mult)
                nc.vector.tensor_scalar(parc[:, PX["om_ka"], :], parc[:, PX["k_a"], :], -1.0, 1.0, mult, add).then_inc(sem("parc_ready"), 1)
                dve.wait_ge(sem("mulora_ready"), 2)
                for n, (m, dst) in enumerate(((P, lwa), (P, lga), (LORA_G - P, lgb))):
                    dve.wait_ge(sem("lora_mu"), n + 1)
                    om = mulora[0:m, 3 + n:4 + n]
                    nc.vector.scalar_tensor_tensor(out=dst[0:m, 0:TP], in0=psum[n][0:m, 0:TP], scalar=om, in1=mpro[0:m, n, 0:TP], op0=mult, op1=add)
                    nc.vector.scalar_tensor_tensor(out=dst[0:m, TP:T], in0=psum[n][0:m, TP:T], scalar=om, in1=mpro[0:m, n, T + 1:TX + 1],
                                                   op0=mult, op1=add).then_inc(sem("lora_mix"), 1)
                dve.wait_ge(sem("lora_tanh"), 1)
                nc.vector.tensor_scalar(lga[:], lga[:], 0.5, 0.5, mult, add)
                nc.vector.tensor_scalar(lgb[:], lgb[:], 0.5, 0.5, mult, add).then_inc(sem("lora_ready"), 1)

            @block.tensor
            def _(pe):
                pe.wait_ge(sem("const_in"), 16 * 15)
                pe.wait_ge(sem("prow_in"), 16 * 14)
                pe.wait_ge(sem("xn_ready"), 1)
                for kk in range(KT):
                    for t in range(TT):
                        nc.tensor.transpose(psum[kk][:, t * P:(t + 1) * P], sb["x_tok"][:, t, kk * P:(kk + 1) * P], ident[:])
                    nc.tensor.transpose(psum[kk][:, TP:TX], sb["xs_tok"][:, kk * P:(kk + 1) * P], ident[0:2 * B, 0:2 * B]).then_inc(sem("xt_mm"), 1)
                pe.wait_ge(sem("xt_dve"), 4)
                nrow = NPAR * KT + 3
                nc.tensor.transpose(psum[7][:, 0:nrow], prow[0:nrow, :], ident[0:nrow, 0:nrow]).then_inc(sem("par_mm"), 1)
                pe.wait_ge(sem("xt_act"), 4)
                pe.wait_ge(sem("wlora_in"), 16)
                for n, m in enumerate((P, P, LORA_G - P)):
                    for kk in range(KT):
                        last = mm(pe, psum[n][0:m, 0:TX], wlora[:, kk, n * P:n * P + m], xt[:, kk, :], kk == 0, kk == KT - 1)
                    last.then_inc(sem("lora_mm"), 1)
        pro.close()
        sem.next_phase()

        pt = buf("pt", [P, NPX])
        dcol = buf("dcol", [P, 3])
        ddec = buf("ddec", [P, TP + P])
        mshift = [buf(f"mshift{n}", [P, TX + 1]) for n in range(3)]
        r, kx, vx = tok("r"), tok("kx"), tok("vx")
        thw, tha, gg = tok("thw"), tok("tha"), tok("gg")
        kk0, kks, kkn = tok("kk0"), tok("kks"), tok("kkn")
        kk, ba, kmod, lp, lpx = tok("kk"), tok("ba"), tok("kmod"), tok("lp"), tok("lpx")
        ep, en, epx = tok("ep"), tok("en"), tok("epx")
        ar = buf("ar", [P, TT, 2, P])
        bt, kt = buf("bt", [P, TP]), buf("kt", [P, TP])
        rkk, bonus = tok("rkk"), tok("bonus")
        qr, kr, vr = tok("qr"), tok("kr"), tok("vr")
        ta, tb = tok("ta"), tok("tb")
        sg, thg = tok("sg"), tok("thg")
        ga, gb = tok("ga"), tok("gb")
        pr = buf("pr", [P, 4, 4, P])
        la = buf("la", [P, 4, 2, P])
        a2 = buf("a2", [P, 4, P])
        at2w = buf("at2w", [P, 4, 2, P])
        a4 = buf("a4", [P, 4, P])
        at4w = buf("at4w", [P, 4, 2, P])
        a8, w2s, w3 = buf("a8", [P, 4, P]), buf("w2s", [P, 4, P]), buf("w3", [P, 4, P])
        rhs = buf("rhs", [P, 4, 2, HD])
        nt, x0 = buf("nt", [P, 4, P]), buf("x0", [P, 4, P])
        z1, z2, zf = a2, a4, a8
        tmk = buf("tmk", [P, TT, 3, P])
        fts = buf("fts", [P, NCH, HD])
        q = buf("q", [P, TP])
        zst = [buf(f"zst{n}", [P, HD]) for n in range(NCH)]
        zout = buf("zout", [HD, 2, HD])
        ys, yc, ysq, yrs = tok("ys"), tok("yc"), tok("ysq"), tok("yrs")
        kvt = buf("kvt", [P, 4, P])
        vd = buf("vd", [P, TT, P])
        sc = buf("sc", [P, TP + P])
        ks8 = buf("ks8", [B, 2, P])
        vdiag = buf("vdiag", [B, B, P])
        sin_, snew = buf("sin_", [P, B, P]), buf("snew", [P, B, P])
        stp = buf("stp", [P, P])
        os_, osq, ors = ys, ysq, yrs
        oc = tok("oc")

        pj = [psum[0], psum[1]]
        M = psum[2:8]

        def v4(x):
            return x[:].rearrange("p (u c) -> p u c", u=4)

        def done(eng, name, i):
            eng.wait_ge(sem(name), i + 1)

        def settle(eng):
            eng.wait_ge(sem("mshift_zero"), 1)

        def last_pass(eng, name, i):
            if not (isinstance(i, int) and i == 0):
                eng.wait_ge(sem(name), i)

        emptied = ["r_mix", "k_mix", "v_mix", "w_tanh", "a_tanh", "g_copy", "q_rope", "k_rope", "v_copy", "gs_silu", "ga_tanh", "gb_tanh"]

        def pe_project(pe, i, use):
            if use >= 2:
                done(pe, emptied[use - 2], i)
            else:
                last_pass(pe, emptied[10 + use], i)
            bank = pj[use % 2]
            if 3 <= use < 6:
                return
            n = use if use < 3 else use - 3
            done_w = sem(f"w_in{n}")
            pe.wait_ge(done_w, 16 * (i + 1))
            width = TX if n < 3 else T
            for kk_ in range(KT):
                last = mm(pe, bank[:, 0:width], wslot[n][:, kk_, :], xt[:, kk_, 0:width], kk_ == 0, kk_ == KT - 1)
            last.then_inc(sem(f"proj{use}"), 1)

        def pe_pass(pe, i, wst):
            for use in range(3):
                pe_project(pe, i, use)
            pe_project(pe, i, 3)
            done(pe, "stage_lora", i)
            mm(pe, pj[1][:, 0:T], wst["w"][0:LORA, :], lwa[0:LORA, :], True, True).then_inc(sem("proj3"), 1)
            pe_project(pe, i, 4)
            mm(pe, pj[0][:, 0:T], wst["w"][LORA:P, :], lwa[LORA:P, :], True, True).then_inc(sem("proj4"), 1)
            pe_project(pe, i, 5)
            mm(pe, pj[1][:, 0:T], wst["ga"][:], lga[:], True, False)
            mm(pe, pj[1][:, 0:T], wst["gb"][:], lgb[:], False, True).then_inc(sem("proj5"), 1)
            done(pe, "kk_sq", i)
            mm(pe, M[0][:, 0:T], one64[:], kks[:], True, True).then_inc(sem("kk_sum"), 1)
            for use in range(6, 12):
                pe_project(pe, i, use)
            done(pe, "rkk_ready", i)
            mm(pe, M[1][:, 0:T], one64[:], rkk[:], True, True).then_inc(sem("rk_sum"), 1)
            done(pe, "abkr_ready", i)
            for t in range(TT):
                for n, src in enumerate((ar[:, t, 0, :], bt[:, t * P:(t + 1) * P], kt[:, t * P:(t + 1) * P], vx[:, t * P:(t + 1) * P])):
                    last = nc.tensor.transpose(M[4 + t][:, n * P:(n + 1) * P], src, ident[:])
                last.then_inc(sem(f"tok_mm{t}"), 1)
            done(pe, "bonus_ready", i)
            done(pe, "kk_norm", i)
            for t in range(TT):
                for h in range(2):
                    u = 2 * t + h
                    hs = slice(HD * h, HD * h + HD)
                    cols = slice(t * P, (t + 1) * P)
                    mm(pe, M[u][:, 0:2 * P], bt[hs, cols], ar[hs, t].rearrange("p a b -> p (a b)"), True, True)
                    mm(pe, M[u][:, 2 * P:4 * P], kt[hs, cols], ar[hs, t].rearrange("p a b -> p (a b)"), True, True).then_inc(sem(f"prod{u}"), 1)
            for h in range(2):
                done(pe, f"tok_copy{h}", i)
                for t in range(TT):
                    hs = slice(HD * h, HD * h + HD)
                    last = mm(pe, M[4 + h][:, t * P:(t + 1) * P], ar[hs, t, 0, :], bt[hs, t * P:(t + 1) * P], True, True)
                last.then_inc(sem(f"lmat{h}"), 1)
            done(pe, "masked", i)
            done(pe, "l_masked", i)
            for u in range(4):
                last = mm(pe, v4(M[0])[:, u, :], pr[:, u, 0, :], la[:, u, 0, :], True, True)
            last.then_inc(sem("a2_mm"), 1)
            for u in range(4):
                last = mm(pe, v4(M[1])[:, u, :], la[:, u, 0, :], pr[:, u, 0, :], True, True)
            last.then_inc(sem("at2_mm"), 1)
            for u in range(4):
                h = u % 2
                last = mm(pe, M[4][:, u * HD:(u + 1) * HD], pr[:, u, 2, :], tmk[:, u // 2, 2, HD * h:HD * h + HD], True, True)
            last.then_inc(sem("lakv_mm"), 1)
            done(pe, "a2_copy", i)
            done(pe, "w0_ready", i)
            done(pe, "at2_copy", i)
            for u in range(4):
                last = mm(pe, M[2 + u // 2][:, (u % 2) * 2 * P:(u % 2 + 1) * 2 * P], a2[:, u, :], at2w[:, u].rearrange("p a b -> p (a b)"), True, True)
            last.then_inc(sem("at4w1_mm"), 1)
            for u in range(4):
                last = mm(pe, v4(M[0])[:, u, :], at2w[:, u, 0, :], a2[:, u, :], True, True)
            last.then_inc(sem("a4_mm"), 1)
            done(pe, "at4_copy", i)
            done(pe, "w1_ready", i)
            done(pe, "a4_copy", i)
            for u in range(4):
                last = mm(pe, v4(M[5])[:, u, :], at4w[:, u, 0, :], a4[:, u, :], True, True)
            last.then_inc(sem("a8_mm"), 1)
            for u in range(4):
                last = mm(pe, v4(M[1])[:, u, :], a4[:, u, :], at4w[:, u, 1, :], True, True)
            last.then_inc(sem("w2_mm"), 1)
            done(pe, "a8_copy", i)
            done(pe, "w2_ready", i)
            for u in range(4):
                last = mm(pe, v4(M[2])[:, u, :], a8[:, u, :], w2s[:, u, :], True, True)
            last.then_inc(sem("w3_mm"), 1)
            done(pe, "w3_ready", i)
            done(pe, "rhs_ready", i)
            for u in range(4):
                last = mm(pe, v4(M[3])[:, u, :], la[:, u, 1, :], w3[:, u, :], True, True)
            last.then_inc(sem("nt_mm"), 1)
            for u in range(4):
                last = mm(pe, v4(M[4])[:, u, :], w3[:, u, :], rhs[:, u].rearrange("p a b -> p (a b)"), True, True)
            last.then_inc(sem("x0_mm"), 1)
            done(pe, "nt_copy", i)
            done(pe, "x0_copy", i)
            for n, (src, bank, wait) in enumerate(((x0, M[5], None), (z1, M[0], "z1_ready"), (z2, M[1], "z2_ready"))):
                if wait:
                    done(pe, wait, i)
                for u in range(4):
                    last = mm(pe, v4(bank)[:, u, :], nt[:, u, :], src[:, u, :], True, True)
                last.then_inc(sem(f"z{n + 1}_mm"), 1)
            done(pe, "zf_ready", i)
            for u in range(4):
                h, t = u % 2, u // 2
                hs = slice(HD * h, HD * h + HD)
                last = mm(pe, M[2][hs, t * P:(t + 1) * P], zf[:, u, 0:HD], pr[:, u, 1, :], True, True, True)
            last.then_inc(sem("q_mm"), 1)
            for u in range(4):
                h, t = u % 2, u // 2
                hs = slice(HD * h, HD * h + HD)
                mm(pe, M[3][hs, t * P:(t + 1) * P], zf[:, u, HD:P], pr[:, u, 1, :], t == 0, False, True)
                mm(pe, M[3][hs, t * P:(t + 1) * P], tmk[:, t, 2, HD * h:HD * h + HD], pr[:, u, 3, :], False, False, True)
            for par in range(2):
                ps = slice(C * par, C * par + C)
                for u in range(4):
                    h, t = u % 2, u // 2
                    hs = slice(HD * h, HD * h + HD)
                    hc = slice(HD * h, HD * h + HD)
                    mm(pe, M[4 + par][hs, t * P:t * P + HD], zf[ps, u, 0:HD], tmk[ps, t, 0, hc], t == 0, False, True)
                    mm(pe, M[4 + par][hs, t * P + HD:(t + 1) * P], tmk[ps, t, 0, hc], zf[ps, u, HD:P], False, False, True)
                    last = mm(pe, M[4 + par][hs, t * P + HD:(t + 1) * P], tmk[ps, t, 1, hc], tmk[ps, t, 2, hc], False, False, True)
                last.then_inc(sem(f"fg_mm{par}"), 1)
            for c in range(1, NCH):
                settle(pe)
                done(pe, f"state{c - 1}", i)
                if c == 1:
                    done(pe, "q_ready", i)
                    done(pe, "ft_ready", i)
                t, par = c // 2, c % 2
                for h in range(2):
                    hs = slice(HD * h, HD * h + HD)
                    last = mm(pe, M[4 + par][hs, t * P + HD:(t + 1) * P], fts[hs, c, :], zst[c - 1][hs, :], False, True, True)
                last.then_inc(sem(f"state_mm{c}"), 1)
                for h in range(2):
                    hs = slice(HD * h, HD * h + HD)
                    last = mm(pe, M[3][hs, c * C:(c + 1) * C], zst[c - 1][hs, :], q[hs, c * C:(c + 1) * C], False, True, True)
            last.then_inc(sem("y_mm"), 1)
            settle(pe)
            done(pe, f"state{NCH - 1}", i)
            nc.tensor.transpose(M[0][0:HD, 0:P], zst[NCH - 1][:], ident[:]).then_inc(sem("zt_mm"), 1)
            done(pe, "y_copy", i)
            mm(pe, M[1][:, 0:TP], mean64[:], ys[:, 0:TP], True, True).then_inc(sem("ymean_mm"), 1)
            done(pe, "y_sq", i)
            mm(pe, M[2][:, 0:TP], mean64[:], ysq[:, 0:TP], True, True).then_inc(sem("yvar_mm"), 1)
            done(pe, "zt_copy", i)
            done(pe, "q_rope", i)
            for n, src in enumerate((kr[:, 0:P], kr[:, P:TP], vr[:, 0:P], vr[:, P:TP])):
                last = nc.tensor.transpose(v4(M[3])[:, n, :], src, ident[:])
            last.then_inc(sem("kvt_mm"), 1)
            nc.tensor.transpose(M[0][0:B, 0:P], kr[:, TP:T], ident[:])
            nc.tensor.transpose(M[0][0:B, P:2 * P], vr[:, TP:T], ident[:]).then_inc(sem("kv8_mm"), 1)
            mm(pe, M[4][:, 0:TP], kr[:, 0:P], qr[:, 0:TP], True, True)
            mm(pe, M[4][:, TP:TP + P], kr[:, P:TP], qr[:, P:TP], True, True).then_inc(sem("sc_mm"), 1)
            done(pe, "sc_ready", i)
            done(pe, "kvt_copy", i)
            mm(pe, M[5][:, 0:TP], kvt[:, 2, :], sc[:, 0:TP], True, False, True)
            mm(pe, M[5][:, P:TP], kvt[:, 3, :], sc[:, TP:TP + P], False, True, True)
            done(pe, "vd_ready", i)
            mm(pe, M[4][:, 0:P], kvt[:, 0, :], vd[:, 0, :], True, False)
            mm(pe, M[4][:, 0:P], kvt[:, 1, :], vd[:, 1, :], False, True).then_inc(sem("stp_mm"), 1)
            done(pe, "vdiag_ready", i)
            vflat = vdiag[:].rearrange("b c d -> b (c d)")
            mm(pe, M[0][:, :], ks8[:, 0, :], vflat[:, 0:512], True, True)
            mm(pe, M[3][:, :], ks8[:, 0, :], vflat[:, 512:1024], True, True).then_inc(sem("kv_mm"), 1)
            done(pe, "snew_ready", i)
            for b in range(B):
                last = mm(pe, M[5][:, TP + b:TP + b + 1], snew[:, b, :], qr[:, TP + b:TP + b + 1], False, True, True)
            last.then_inc(sem("o_mm"), 1)
            done(pe, "o_copy", i)
            mm(pe, M[0][:, 0:T], mean128[:], os_[:], True, True).then_inc(sem("omean_mm"), 1)
            done(pe, "o_sq", i)
            mm(pe, M[3][:, 0:T], mean128[:], osq[:], True, True).then_inc(sem("ovar_mm"), 1)

        wst = {"w": buf("wst_w", [P, P]), "ga": buf("wst_ga", [P, P]), "gb": buf("wst_gb", [LORA_G - P, P])}

        def act_pass(act, i):
            A = nc.scalar
            ci = bass.ts(i, P)
            last_pass(act, "g_copy", i)
            A.copy(wst["w"][:], lowa[:, ci])
            A.copy(wst["ga"][:], g2a[:, ci])
            A.copy(wst["gb"][:], g2b[:, ci]).then_inc(sem("stage_lora"), 1)
            done(act, "pt_ready", i)
            for n, nm in enumerate(("r", "k", "v")):
                done(act, f"proj{n}", i)
                A.activation(mshift[n][:, 1:TX + 1], pj[n % 2][:, 0:TX], ACT.Copy, scale=pt[:, PX["mu_" + nm]:PX["mu_" + nm] + 1]).then_inc(sem(f"mu_{nm}"), 1)
            done(act, "proj3", i)
            A.activation(thw[:], pj[1][:, 0:T], ACT.Tanh, scale=0.5, bias=pt[:, PX["w0h"]:PX["w0h"] + 1]).then_inc(sem("w_tanh"), 1)
            done(act, "proj4", i)
            A.activation(tha[:], pj[0][:, 0:T], ACT.Tanh, scale=0.5, bias=pt[:, PX["a0h"]:PX["a0h"] + 1]).then_inc(sem("a_tanh"), 1)
            done(act, "proj5", i)
            A.copy(gg[:], pj[1][:, 0:T]).then_inc(sem("g_copy"), 1)
            done(act, "kk0_ready", i)
            A.activation(kks[:], kk0[:], ACT.Square).then_inc(sem("kk_sq"), 1)
            done(act, "lp_ready", i)
            A.activation(ep[:], lp[:], ACT.Exp)
            A.activation(en[:], lp[:], ACT.Exp, scale=-1.0)
            done(act, "lpx_ready", i)
            A.activation(epx[:], lpx[:], ACT.Exp).then_inc(sem("exp_ready"), 1)
            done(act, "kk_sum", i)
            A.activation(kkn[:], M[0][:, 0:T], ACT.Sqrt).then_inc(sem("kk_root"), 1)
            done(act, "proj8", i)
            A.copy(vr[:], pj[0][:, 0:T]).then_inc(sem("v_copy"), 1)
            done(act, "proj9", i)
            A.activation(thg[:], pj[1][:, 0:T], ACT.Tanh, scale=0.5).then_inc(sem("gs_tanh"), 1)
            done(act, "proj10", i)
            A.activation(ga[:], pj[0][:, 0:T], ACT.Tanh, scale=0.5).then_inc(sem("ga_tanh"), 1)
            done(act, "proj11", i)
            A.activation(gb[:], pj[1][:, 0:T], ACT.Tanh, scale=0.5).then_inc(sem("gb_tanh"), 1)
            for t in range(TT):
                done(act, f"tok_mm{t}", i)
                A.copy(rhs[:, 2 * t:2 * t + 2, 0, :], M[4 + t][:, 0:P].rearrange("p (h c) -> p h c", h=2))
                A.copy(tmk[:, t], M[4 + t][:, P:4 * P].rearrange("p (n c) -> p n c", n=3)).then_inc(sem(f"tok_copy{t}"), 1)
            done(act, "a2_mm", i)
            A.copy(a2[:], v4(M[0])).then_inc(sem("a2_copy"), 1)
            done(act, "lakv_mm", i)
            A.copy(rhs[:, :, 1, :], M[4][:, 0:4 * HD].rearrange("p (u c) -> p u c", u=4)).then_inc(sem("rhs_ready"), 1)
            done(act, "at4w1_mm", i)
            for half in range(2):
                last = A.copy(at4w[:, 2 * half:2 * half + 2, 0, :], M[2 + half][:].rearrange("p (u a c) -> p u a c", u=2, a=2)[:, :, 0, :])
            last.then_inc(sem("at4_copy"), 1)
            done(act, "a4_mm", i)
            A.copy(a4[:], v4(M[0])).then_inc(sem("a4_copy"), 1)
            done(act, "a8_mm", i)
            A.copy(a8[:], v4(M[5])).then_inc(sem("a8_copy"), 1)
            done(act, "nt_mm", i)
            A.copy(nt[:], v4(M[3])).then_inc(sem("nt_copy"), 1)
            done(act, "y_mm", i)
            A.copy(ys[:, 0:TP], M[3][:, 0:TP]).then_inc(sem("y_copy"), 1)
            done(act, "zt_mm", i)
            last_pass(act, "zout_sent", 16 * i if not isinstance(i, int) else i * 16)
            A.copy(zout[:], M[0][0:HD, 0:P].rearrange("p (h c) -> p h c", h=2)).then_inc(sem("zt_copy"), 1)
            done(act, "yc_ready", i)
            A.activation(ysq[:, 0:TP], yc[:, 0:TP], ACT.Square).then_inc(sem("y_sq"), 1)
            done(act, "yvar_mm", i)
            A.activation(yrs[:, 0:TP], M[2][:, 0:TP], ACT.Sqrt, bias=eps[:, 1:2]).then_inc(sem("y_root"), 1)
            done(act, "kvt_mm", i)
            A.copy(kvt[:], v4(M[3])).then_inc(sem("kvt_copy"), 1)
            done(act, "kv8_mm", i)
            A.copy(ks8[:], M[0][0:B, 0:2 * P].rearrange("p (n c) -> p n c", n=2)).then_inc(sem("ks8_ready"), 1)
            done(act, "stp_mm", i)
            last_pass(act, "stp_sent", 16 * i if not isinstance(i, int) else i * 16)
            A.copy(stp[:], M[4][:, 0:P]).then_inc(sem("stp_ready"), 1)
            done(act, "o_mm", i)
            A.copy(os_[:], M[5][:, 0:T]).then_inc(sem("o_copy"), 1)
            done(act, "oc_ready", i)
            A.activation(osq[:], oc[:], ACT.Square).then_inc(sem("o_sq"), 1)
            done(act, "ovar_mm", i)
            A.activation(ors[:], M[3][:, 0:T], ACT.Sqrt, bias=eps[:, 0:1]).then_inc(sem("o_root"), 1)

        def dve_pass(dve, i):
            V = nc.vector

            def par(n):
                return pt[:, PX[n]:PX[n] + 1]

            def self_wait(name):
                done(dve, name, i)

            last_pass(dve, "w_tanh", i)
            last_pass(dve, "a_tanh", i)
            V.tensor_copy(pt[:], parc[:, :, bass.ds(i, 1)].rearrange("p n o -> p (n o)"))
            V.tensor_copy(dcol[:], retcol[:, bass.ds(i, 1), :].rearrange("p o n -> p (o n)"))
            V.tensor_copy(ddec[:], retdec[:, bass.ds(i, 1), :].rearrange("p o n -> p (o n)")).then_inc(sem("pt_ready"), 1)
            self_wait("pt_ready")
            for n, (nm, dst) in enumerate((("r", r), ("k", kx), ("v", vx))):
                done(dve, f"mu_{nm}", i)
                V.scalar_tensor_tensor(out=dst[:, 0:TP], in0=pj[n % 2][:, 0:TP], scalar=par("om_" + nm), in1=mshift[n][:, 0:TP], op0=mult, op1=add)
                V.scalar_tensor_tensor(out=dst[:, TP:T], in0=pj[n % 2][:, TP:T], scalar=par("om_" + nm), in1=mshift[n][:, T + 1:TX + 1],
                                       op0=mult, op1=add).then_inc(sem(f"{nm}_mix"), 1)
            self_wait("k_mix")
            V.tensor_scalar(kk0[:], kx[:], par("k_k"), None, mult).then_inc(sem("kk0_ready"), 1)
            done(dve, "w_tanh", i)
            V.tensor_scalar(thw[:], thw[:], LOGW_C, LOGW_C, mult, add).then_inc(sem("lw_ready"), 1)
            self_wait("lw_ready")
            V.tensor_tensor_scan(lp[:], scanm[:], thw[:], 0.0, mult, add).then_inc(sem("lp_ready"), 1)
            self_wait("lp_ready")
            V.tensor_tensor(lpx[:], lp[:], thw[:], sub).then_inc(sem("lpx_ready"), 1)
            done(dve, "a_tanh", i)
            V.tensor_scalar(tha[:], tha[:], 0.5, 0.5, mult, add).then_inc(sem("a_ready"), 1)
            self_wait("a_ready")
            V.tensor_scalar(kmod[:], tha[:], par("k_a"), par("om_ka"), mult, add).then_inc(sem("km_part"), 1)
            self_wait("km_part")
            V.tensor_tensor(kmod[:], kmod[:], kx[:], mult).then_inc(sem("kmod_ready"), 1)
            self_wait("kmod_ready")
            V.scalar_tensor_tensor(out=rkk[:], in0=r[:], scalar=par("r_k"), in1=kmod[:], op0=mult, op1=mult).then_inc(sem("rkk_ready"), 1)
            done(dve, "kk_root", i)
            V.tensor_scalar(kkn[:], kkn[:], 1e-12, None, ALU.max).then_inc(sem("kk_max"), 1)
            self_wait("kk_max")
            V.reciprocal(kkn[:], kkn[:]).then_inc(sem("kk_inv"), 1)
            self_wait("kk_inv")
            V.tensor_tensor(kk[:], kk0[:], kkn[:], mult).then_inc(sem("kk_norm"), 1)
            self_wait("kk_norm")
            V.tensor_tensor(ba[:], kk[:], tha[:], mult).then_inc(sem("ba_ready"), 1)
            self_wait("ba_ready")
            done(dve, "exp_ready", i)
            c2 = "p (t c) -> p t c"
            V.scalar_tensor_tensor(out=ar[:, :, 0, :], in0=kk[:, 0:TP].rearrange(c2, t=TT), scalar=-1.0,
                                   in1=epx[:, 0:TP].rearrange(c2, t=TT), op0=mult, op1=mult)
            V.tensor_tensor(ar[:, :, 1, :], r[:, 0:TP].rearrange(c2, t=TT), ep[:, 0:TP].rearrange(c2, t=TT), mult)
            V.tensor_tensor(bt[:], ba[:, 0:TP], en[:, 0:TP], mult)
            V.tensor_tensor(kt[:], kmod[:, 0:TP], en[:, 0:TP], mult).then_inc(sem("abkr_ready"), 1)
            for n, src in enumerate((r, ep, kmod, vx, kk, ba)):
                V.tensor_copy(svec[:, bass.ds(i, 1), n, :].rearrange("p o b -> p (o b)"), src[:, TP:T])
            for nm, use, tabs, dst in (("q", 6, (0, 1), qr), ("k", 7, (2, 3), kr)):
                done(dve, f"proj{use}", i)
                bank = pj[use % 2]
                hf = P // 2
                if nm == "k":
                    self_wait("q_rope")
                V.tensor_tensor(ta[:], bank[:, 0:T], rope[:, tabs[0], :], mult)
                V.tensor_tensor(tb[0:hf, :], bank[hf:P, 0:T], rope[hf:P, tabs[1], :], mult)
                V.tensor_tensor(tb[hf:P, :], bank[0:hf, 0:T], rope[0:hf, tabs[1], :], mult).then_inc(sem(f"{nm}_part"), 1)
                self_wait(f"{nm}_part")
                V.tensor_tensor(dst[:], ta[:], tb[:], add).then_inc(sem(f"{nm}_rope"), 1)
            done(dve, "gs_tanh", i)
            V.scalar_tensor_tensor(out=sg[:], in0=thg[:], scalar=1.0, in1=pj[1][:, 0:T], op0=add, op1=mult).then_inc(sem("gs_silu"), 1)
            done(dve, "gb_tanh", i)
            V.tensor_scalar(ga[:], ga[:], 0.25, 0.25, mult, add)
            V.tensor_scalar(gb[:], gb[:], 0.5, 0.5, mult, add).then_inc(sem("gates_ready"), 1)
            self_wait("gates_ready")
            self_wait("gs_silu")
            V.scalar_tensor_tensor(out=sg[:], in0=sg[:], scalar=par("gn_w"), in1=ga[:], op0=mult, op1=mult).then_inc(sem("retgate_ready"), 1)
            V.tensor_tensor(gg[:], gg[:], gb[:], mult)
            done(dve, "rk_sum", i)
            V.tensor_tensor(bonus[:], M[1][:, 0:T], vx[:], mult).then_inc(sem("bonus_ready"), 1)
            self_wait("bonus_ready")
            V.tensor_copy(spost[:, 0, bass.ds(i, 1), :].rearrange("p o b -> p (o b)"), bonus[:, TP:T])
            V.tensor_copy(spost[:, 1, bass.ds(i, 1), :].rearrange("p o b -> p (o b)"), gg[:, TP:T])
            for u in range(4):
                done(dve, f"prod{u}", i)
                last = V.tensor_tensor(pr[:, u], v4(M[u]), mk[:], mult)
            last.then_inc(sem("masked"), 1)
            for h in range(2):
                done(dve, f"lmat{h}", i)
                src = M[4 + h][:, 0:TP].rearrange("p (t c) -> p t c", t=TT)
                for n in range(2):
                    last = V.tensor_tensor(la[:, h::2, n, :], src, mlo[:, n:n + 1, :].broadcast_to([P, TT, P]), mult)
            last.then_inc(sem("l_masked"), 1)
            self_wait("masked")
            V.tensor_tensor(at2w[:, :, 1, :], pr[:, :, 0, :], ident[:].unsqueeze(1).broadcast_to([P, 4, P]), add).then_inc(sem("w0_ready"), 1)
            done(dve, "at2_mm", i)
            V.tensor_copy(at2w[:, :, 0, :], v4(M[1])).then_inc(sem("at2_copy"), 1)
            self_wait("w0_ready")
            done(dve, "at4_copy", i)
            for half in range(2):
                us = slice(2 * half, 2 * half + 2)
                last = V.tensor_tensor(at4w[:, us, 1, :], M[2 + half][:].rearrange("p (u a c) -> p u a c", u=2, a=2)[:, :, 1, :], at2w[:, us, 1, :], add)
            last.then_inc(sem("w1_ready"), 1)
            done(dve, "w2_mm", i)
            self_wait("w1_ready")
            V.tensor_tensor(w2s[:], v4(M[1]), at4w[:, :, 1, :], add).then_inc(sem("w2_ready"), 1)
            done(dve, "w3_mm", i)
            self_wait("w2_ready")
            V.tensor_tensor(w3[:], v4(M[2]), w2s[:], add).then_inc(sem("w3_ready"), 1)
            done(dve, "x0_mm", i)
            V.tensor_copy(x0[:], v4(M[4])).then_inc(sem("x0_copy"), 1)
            self_wait("x0_copy")
            for nm, bank, dst in (("z1", M[5], z1), ("z2", M[0], z2), ("zf", M[1], zf)):
                done(dve, {"z1": "z1_mm", "z2": "z2_mm", "zf": "z3_mm"}[nm], i)
                V.tensor_tensor(dst[:], v4(bank), x0[:], add).then_inc(sem(nm + "_ready"), 1)
            done(dve, "q_mm", i)
            V.tensor_tensor(q[:].rearrange(c2, t=TT), M[2][:, 0:TP].rearrange(c2, t=TT), ar[:, :, 1, :], add).then_inc(sem("q_ready"), 1)
            for par_ in range(2):
                done(dve, f"fg_mm{par_}", i)
                last = V.tensor_tensor(fts[:, par_::2, :], M[4 + par_][:, 0:TP].rearrange("p (t a c) -> p t a c", t=TT, a=2)[:, :, 0, :],
                                       cst["c_id64"][:].unsqueeze(1).broadcast_to([P, TT, HD]), add)
            last.then_inc(sem("ft_ready"), 1)
            for c in range(NCH):
                if c:
                    done(dve, f"state_mm{c}", i)
                t, par_ = c // 2, c % 2
                V.tensor_scalar(zst[c][:], M[4 + par_][:, t * P + HD:(t + 1) * P], ep[:, (c + 1) * C - 1:(c + 1) * C], None, mult).then_inc(sem(f"state{c}"), 1)
            done(dve, "ymean_mm", i)
            V.tensor_tensor(yc[:, 0:TP], ys[:, 0:TP], M[1][:, 0:TP], sub).then_inc(sem("yc_ready"), 1)
            done(dve, "y_root", i)
            V.reciprocal(yrs[:, 0:TP], yrs[:, 0:TP]).then_inc(sem("y_inv"), 1)
            self_wait("y_inv")
            V.tensor_tensor(yc[:, 0:TP], yc[:, 0:TP], yrs[:, 0:TP], mult).then_inc(sem("yn"), 1)
            self_wait("yn")
            V.tensor_scalar(yc[:, 0:TP], yc[:, 0:TP], par("lnx_w"), par("lnx_b"), mult, add).then_inc(sem("yln"), 1)
            self_wait("yln")
            V.tensor_tensor(yc[:, 0:TP], yc[:, 0:TP], bonus[:, 0:TP], add).then_inc(sem("ybonus"), 1)
            self_wait("ybonus")
            V.tensor_tensor(yc[:, 0:TP], yc[:, 0:TP], gg[:, 0:TP], mult).then_inc(sem("rwkv_out"), 1)
            done(dve, "sc_mm", i)
            V.tensor_tensor(sc[:], M[4][:, 0:TP + P], ddec[:], mult).then_inc(sem("sc_ready"), 1)
            done(dve, "kvt_copy", i)
            V.tensor_scalar(vd[:, 0, :], kvt[:, 2, :], dcol[:, 0:1], None, mult)
            V.tensor_scalar(vd[:, 1, :], kvt[:, 3, :], dcol[:, 1:2], None, mult).then_inc(sem("vd_ready"), 1)
            done(dve, "ks8_ready", i)
            V.tensor_tensor(vdiag[:], ks8[:, 1:2, :].broadcast_to([B, B, P]), diag8[:], mult).then_inc(sem("vdiag_ready"), 1)
            dve.wait_ge(sem("sin_in"), 16 * (i + 1))
            last_pass(dve, "snew_sent", 16 * i if not isinstance(i, int) else i * 16)
            done(dve, "kv_mm", i)
            for half, bank in enumerate((M[0], M[3])):
                bs = slice(4 * half, 4 * half + 4)
                last = V.scalar_tensor_tensor(out=snew[:, bs, :], in0=sin_[:, bs, :], scalar=dcol[:, 2:3], in1=v4(bank), op0=mult, op1=add)
            last.then_inc(sem("snew_ready"), 1)
            done(dve, "omean_mm", i)
            V.tensor_tensor(oc[:], os_[:], M[0][:, 0:T], sub).then_inc(sem("oc_ready"), 1)
            done(dve, "o_root", i)
            V.reciprocal(ors[:], ors[:]).then_inc(sem("o_inv"), 1)
            self_wait("o_inv")
            V.tensor_tensor(oc[:], oc[:], ors[:], mult).then_inc(sem("on"), 1)
            self_wait("on")
            V.tensor_tensor(oc[:], oc[:], sg[:], mult).then_inc(sem("ret_out"), 1)
            self_wait("ret_out")
            self_wait("rwkv_out")
            V.tensor_tensor(merged[:, bass.ds(i, 1), 0:TP].rearrange("p o t -> p (o t)"), oc[:, 0:TP], yc[:, 0:TP], add)
            V.tensor_copy(spost[:, 2, bass.ds(i, 1), :].rearrange("p o b -> p (o b)"), oc[:, TP:T]).then_inc(sem("tile_done"), 1)

        def sp_pass(sp, i):
            for n, off in enumerate(SECTIONS):
                settle(sp)
                last_pass(sp, f"proj{n if n < 3 else n + 3}", i)
                sp.dma_start(wslot[n][:], w_in[:, :, bass.ds(i * P + off, P)]).then_inc(sem(f"w_in{n}"), 16)
            last_pass(sp, "snew_ready", i)
            sp.dma_start(sin_[:], a["state_ret"][0].rearrange("b h k v -> k h b v")[:, bass.ds(i, 1), :, :].rearrange("k o b v -> k (o b) v")).then_inc(sem("sin_in"), 16)

        def out_pass(eng, i):
            settle(eng)
            done(eng, "zt_copy", i)
            eng.dma_start(o["rwkv_p"][0, 0].rearrange("h v k -> v h k")[:, bass.ds(i * 2, 2), :], zout[:]).then_inc(sem("zout_sent"), 16)
            settle(eng)
            done(eng, "stp_ready", i)
            eng.dma_start(o["ret_p"][0, 0][bass.ds(i, 1)].rearrange("o k v -> (o k) v"), stp[:]).then_inc(sem("stp_sent"), 16)
            settle(eng)
            done(eng, "snew_ready", i)
            eng.dma_start(o["ret_s"][0].rearrange("b h k v -> k h b v")[:, bass.ds(i, 1), :, :].rearrange("k o b v -> k (o b) v"), snew[:]).then_inc(sem("snew_sent"), 16)

        with nc.Block() as block:

            @block.sync
            def _(sp):
                sp_pass(sp, 0)
                with sp.Fori(1, KT) as i:
                    sp_pass(sp, i)

            @block.gpsimd
            def _(pool):
                for m in mshift:
                    last = nc.gpsimd.memset(m[:, 0:1], 0.0)
                last.then_inc(sem("mshift_zero"), 1)
                out_pass(pool, 0)
                with pool.Fori(1, KT) as i:
                    out_pass(pool, i)
                for n in ("zout_sent", "stp_sent", "snew_sent"):
                    pool.wait_ge(sem(n), 16 * KT)

            @block.scalar
            def _(act):
                act_pass(act, 0)
                with act.Fori(1, KT) as i:
                    act_pass(act, i)

            @block.vector
            def _(dve):
                dve.wait_ge(sem("mshift_zero"), 1)
                dve_pass(dve, 0)
                with dve.Fori(1, KT) as i:
                    dve_pass(dve, i)

            @block.tensor
            def _(pe):
                pe_pass(pe, 0, wst)
                with pe.Fori(1, KT) as i:
                    last_pass(pe, "tile_done", i)
                    pe_pass(pe, i, wst)


def sample_phase(nc, a, o, k, alloc, sem, psum, cst, keep):
    mult, add, sub = ALU.mult, ALU.add, ALU.subtract
    with ExitStack() as ctx:
        sb = {}

        def buf(name, shape):
            return alloc(ctx, sb, name, shape)

        ident, mean64 = cst["c_ident"], cst["c_mean64"]
        merged, svec, spost, parc, eps = (keep[n] for n in ("merged", "svec", "spost", "parc", "eps"))
        NV = 6 * B
        st = buf("st", [P, HD, HD])
        vk = buf("vk", [P, HD, HD])
        prod = buf("prod", [P, HD, HD])
        stok = buf("stok", [NV, D])
        vec = buf("vec", [P, 6, HD])
        sa, y1 = buf("sa", [P, HD]), buf("y1", [P, HD])
        ytok = buf("ytok", [B, D])
        sy, syc, sysq, syr = (buf(n, [P, KT, B]) for n in ("sy", "syc", "sysq", "syr"))
        scr_vec = nc.dram_tensor("scr_vec", [NV, D], F32, kind="Internal").ap()
        scr_y = nc.dram_tensor("scr_y", [P, HD], F32, kind="Internal").ap()

        with nc.Block() as block:

            @block.sync
            def _(sp):
                sp.dma_start(st[:].rearrange("p v k -> p (v k)"), a["state_rwkv"][0].rearrange("b h v k -> (b h) (v k)")).then_inc(sem("st_in"), 16)
                sp.wait_ge(sem("stok_ready"), 2)
                sp.dma_start(scr_vec, stok[:]).then_inc(sem("scr_vec_in"), 16)
                sp.wait_ge(sem("scr_vec_in"), 16)
                sp.dma_start(vec[:], scr_vec.rearrange("(v b) (h c) -> (b h) v c", b=B, c=HD)).then_inc(sem("vec_in"), 16)
                sp.wait_ge(sem("state_new"), 1)
                sp.dma_start(o["rwkv_s"][0].rearrange("b h v k -> (b h) (v k)"), st[:].rearrange("p v k -> p (v k)")).then_inc(sem("rwkv_s_out"), 16)
                sp.wait_ge(sem("y1_ready"), 1)
                sp.dma_start(scr_y, y1[:]).then_inc(sem("scr_y_in"), 16)
                sp.wait_ge(sem("scr_y_in"), 16)
                sp.dma_start(ytok[:], scr_y.rearrange("(b h) c -> b (h c)", b=B)).then_inc(sem("ytok_in"), 16)
                sp.wait_ge(sem("rwkv_s_out"), 16)
                sp.wait_ge(sem("ytok_in"), 16)

            @block.tensor
            def _(pe):
                for kk in range(KT):
                    last = nc.tensor.transpose(psum[kk // 4][0:NV, (kk % 4) * P:(kk % 4 + 1) * P], svec[:, kk].rearrange("p v b -> p (v b)"), ident[:])
                    if kk % 4 == 3:
                        last.then_inc(sem("sv_mm"), 1)
                pe.wait_ge(sem("ytok_in"), 16)
                for kk in range(KT):
                    last = nc.tensor.transpose(psum[2][:, kk * B:(kk + 1) * B], ytok[:, kk * P:(kk + 1) * P], ident[0:B, 0:B])
                last.then_inc(sem("sy_mm"), 1)
                pe.wait_ge(sem("sy_ready"), 1)
                nc.tensor.matmul(psum[3][:, 0:KT * B], mean64[:], sy[:].rearrange("p k b -> p (k b)"), start=True, stop=True).then_inc(sem("symean"), 1)
                pe.wait_ge(sem("sysq_ready"), 1)
                nc.tensor.matmul(psum[4][:, 0:KT * B], mean64[:], sysq[:].rearrange("p k b -> p (k b)"), start=True, stop=True).then_inc(sem("syvar"), 1)

            @block.gpsimd
            def _(pool):
                pool.wait_ge(sem("vec_in"), 16)
                nc.gpsimd.tensor_tensor(vk[:], vec[:, 3, :].unsqueeze(2).broadcast_to([P, HD, HD]),
                                        vec[:, 2, :].unsqueeze(1).broadcast_to([P, HD, HD]), mult).then_inc(sem("vk_ready"), 1)

            @block.scalar
            def _(act):
                act.wait_ge(sem("sv_mm"), 1)
                nc.scalar.copy(stok[:, 0:512], psum[0][0:NV, :]).then_inc(sem("stok_ready"), 1)
                act.wait_ge(sem("sy_mm"), 1)
                nc.scalar.copy(sy[:].rearrange("p k b -> p (k b)"), psum[2][:, 0:KT * B]).then_inc(sem("sy_ready"), 1)
                act.wait_ge(sem("syc_ready"), 1)
                nc.scalar.activation(sysq[:], syc[:], ACT.Square).then_inc(sem("sysq_ready"), 1)
                act.wait_ge(sem("syvar"), 1)
                nc.scalar.activation(syr[:].rearrange("p k b -> p (k b)"), psum[4][:, 0:KT * B], ACT.Sqrt, bias=eps[:, 1:2]).then_inc(sem("syroot"), 1)

            @block.vector
            def _(dve):
                V = nc.vector

                def key(n):
                    return vec[:, n, :].unsqueeze(1).broadcast_to([P, HD, HD])

                step = [0]

                def then(ins):
                    step[0] += 1
                    ins.then_inc(sem("sample_step"), 1)
                    dve.wait_ge(sem("sample_step"), step[0])

                dve.wait_ge(sem("sv_mm"), 2)
                V.tensor_copy(stok[:, 512:1024], psum[1][0:NV, :]).then_inc(sem("stok_ready"), 1)
                dve.wait_ge(sem("st_in"), 16)
                dve.wait_ge(sem("vec_in"), 16)
                then(V.tensor_tensor(prod[:], st[:], key(4), mult))
                V.tensor_reduce(sa[:], prod[:], AX_X, add)
                then(V.tensor_tensor(st[:], st[:], key(1), mult))
                then(V.tensor_tensor(prod[:], sa[:].unsqueeze(2).broadcast_to([P, HD, HD]), key(5), mult))
                then(V.tensor_tensor(st[:], st[:], prod[:], sub))
                dve.wait_ge(sem("vk_ready"), 1)
                V.tensor_tensor(st[:], st[:], vk[:], add).then_inc(sem("state_new"), 1)
                dve.wait_ge(sem("state_new"), 1)
                then(V.tensor_tensor(prod[:], st[:], key(0), mult))
                V.tensor_reduce(y1[:], prod[:], AX_X, add).then_inc(sem("y1_ready"), 1)
                dve.wait_ge(sem("symean"), 1)
                V.tensor_tensor(syc[:].rearrange("p k b -> p (k b)"), sy[:].rearrange("p k b -> p (k b)"), psum[3][:, 0:KT * B], sub).then_inc(sem("syc_ready"), 1)
                dve.wait_ge(sem("syroot"), 1)
                then(V.reciprocal(syr[:], syr[:]))
                then(V.tensor_tensor(syc[:], syc[:], syr[:], mult))

                def chan(n):
                    return parc[:, PX[n], :].unsqueeze(2).broadcast_to([P, KT, B])

                then(V.tensor_tensor(syc[:], syc[:], chan("lnx_w"), mult))
                then(V.tensor_tensor(syc[:], syc[:], chan("lnx_b"), add))
                then(V.tensor_tensor(syc[:], syc[:], spost[:, 0], add))
                then(V.tensor_tensor(syc[:], syc[:], spost[:, 1], mult))
                V.tensor_tensor(merged[:, :, TP:T], syc[:], spost[:, 2], add).then_inc(sem("merged_all"), 1)


def moe_phase(nc, a, o, k, alloc, sem, psum, cst, keep):
    mult, add, sub = ALU.mult, ALU.add, ALU.subtract
    SIZE = [P, P, B]
    with ExitStack() as ctx:
        sb = {}

        def buf(name, shape, dt=F32):
            return alloc(ctx, sb, name, shape, dt)

        ident, tri, ones, slot = (cst["c_" + n] for n in ("ident", "tri", "ones", "slot"))
        merged, gbc, eps = keep["merged"], keep["gbc"], keep["eps"]
        RING = 4
        wg = [buf(f"wg{n}", [P, KT, DE]) for n in range(RING)]
        wu = [buf(f"wu{n}", [P, KT, DE]) for n in range(RING)]
        wd = [buf(f"wd{n}", [P, DE // P, D]) for n in range(RING)]
        wout = [wg[3], wu[3], wd[3], wg[2]]
        x = buf("x", [P, 3, D])
        xn = buf("xn", [P, 3, D])
        xnt = buf("xnt", [P, KT, T])
        stat = buf("mstat", [P, 3, 4])
        rw = buf("rw", [P, KT, NG + NE])
        rb = buf("rb", [P, NG + NE])
        lg = buf("lg", [P, 3, NG + NE])
        gpad = buf("gpad", [P, 3, 8])
        top, topi, topf = buf("topv", [P, 3, 8]), buf("topi", [P, 3, 8], mybir.dt.uint32), buf("topf", [P, 3, 8])
        gmask = buf("gmask", [P, 3, NG])
        gexp, gsum = buf("gexp", [P, 3, NG]), buf("gsum", [P, 3, 4])
        esel, eprod = buf("esel", [P, 3, 8]), buf("eprod", [P, 3, 8, NG])
        tw = buf("tw", [P, 3, 4])
        c8, c8b = buf("c8", [P, 3, 8]), buf("c8b", [P, 3, 8])
        comb = buf("comb", [P, 3, NG, EPG])
        pos = buf("pos", [P, 3, NG])
        cnt = buf("cnt", [P, 4])
        rounds_i = buf("rounds_i", [P, 1], I32)
        pcol, mcol, cg = buf("pcol", [P, 3]), buf("mcol", [P, 3]), buf("cg", [P, 3, EPG])
        G = buf("G", [P, 3, SLOTS])
        GT = buf("GT", [SLOTS, T])
        xg, cb = buf("xg", [P, KT, SLOTS]), buf("cb", [P, EPG, SLOTS])
        th = [buf(f"th{n}", [P, 2, SLOTS]) for n in range(2)]
        hs = [buf(f"hs{n}", [P, 2, SLOTS]) for n in range(2)]
        h = [buf(f"h{n}", [P, 2, SLOTS]) for n in range(2)]
        ysb, yt = buf("ysb", [P, KT, SLOTS]), buf("yt", [SLOTS, D])
        gfin = buf("gfin", [P, D])
        junk = buf("junk", [P, D])
        buf("zeros", [P, 4 * SLOTS])
        hold = buf("hold", [P, 1])
        MB = [psum[4], psum[5]]
        YB = [psum[6], psum[7]]

        def rows(tt):
            return slice(0, SIZE[tt])

        def cols(tt):
            return slice(tt * P, tt * P + SIZE[tt])

        with nc.Block() as block:

            def settle(eng):
                eng.wait_ge(sem("rounds_ready"), 1)

            def load_expert(sp, s, e, n):
                sp.wait_ge(sem(f"slot_free{s}"), n + 1)
                ew = [a[nm][0][bass.ds(e, 1)] for nm in ("expert_w_gate", "expert_w_up", "expert_w_down")]
                sp.dma_start(wg[s][:], ew[0].rearrange("o (k p) f -> p (o k) f", p=P)).then_inc(sem(f"expert_in{s}"), 16)
                sp.dma_start(wu[s][:], ew[1].rearrange("o (k p) f -> p (o k) f", p=P)).then_inc(sem(f"expert_in{s}"), 16)
                sp.dma_start(wd[s][:], ew[2].rearrange("o (k p) f -> p (o k) f", p=P)).then_inc(sem(f"expert_in{s}"), 16)

            @block.sync
            def _(sp):
                sp.dma_start(x[:, 0:2, :], a["x_prompt"][0].rearrange("(t p) d -> p t d", p=P)).then_inc(sem("x2_in"), 16)
                sp.dma_start(x[0:B, 2, :], a["x_sample"].rearrange("b t d -> (b t) d")).then_inc(sem("x2_in"), 16)
                wo = a["w_out"][0].rearrange("(k p) c -> p k c", p=P)
                for n in range(4):
                    sp.dma_start(wout[n][:].rearrange("p a b -> p (a b)").rearrange("p (k c) -> p k c", k=2), wo[:, 2 * n:2 * n + 2, :]).then_inc(sem("wout_in"), 16)
                sp.dma_start(gbc[:], a["norm_ffn"].partition_broadcast(P)).then_inc(sem("gffn_in"), 16)
                sp.dma_start(gfin[:], a["norm_final"].rearrange("(o d) -> o d", o=1).partition_broadcast(P)).then_inc(sem("gfin_in"), 16)
                sp.dma_start(rw[:, :, 0:NG], a["router_group_w"][0].rearrange("(k p) c -> p k c", p=P)).then_inc(sem("rw_in"), 16)
                sp.dma_start(rw[:, :, NG:NG + NE], a["router_expert_w"][0].rearrange("(k p) c -> p k c", p=P)).then_inc(sem("rw_in"), 16)
                sp.dma_start(rb[:, 0:NG], a["router_group_b"].partition_broadcast(P)).then_inc(sem("rw_in"), 16)
                sp.dma_start(rb[:, NG:NG + NE], a["router_expert_b"].partition_broadcast(P)).then_inc(sem("rw_in"), 16)
                with sp.Fori(0, NE // RING) as quad:
                    for s in range(RING):
                        load_expert(sp, s, quad * RING + s, quad)
                sp.wait_ge(sem("rounds_ready"), 1)
                n_rounds = sp.value_load(rounds_i[0:1, 0:1], min_val=1, max_val=3)
                with sp.If(n_rounds > 1):
                    with sp.Fori(1, n_rounds) as rnd:
                        with sp.Fori(0, NE // RING) as quad:
                            for s in range(RING):
                                load_expert(sp, s, quad * RING + s, rnd * (NE // RING) + quad)
                sp.wait_ge(sem("y_final"), 1)
                sp.dma_start(o["y_p"][0].rearrange("(t p) d -> p t d", p=P), xn[:, 0:2, :]).then_inc(sem("y_sent"), 16)
                sp.dma_start(o["y_s"].rearrange("b t d -> (b t) d"), xn[0:B, 2, :]).then_inc(sem("y_sent"), 16)
                sp.wait_ge(sem("y_sent"), 32)

            def loop(eng, group_pre, expert, group_post, round_end=None):
                eng.wait_ge(sem("rounds_ready"), 1)
                n_rounds = eng.value_load(rounds_i[0:1, 0:1], min_val=1, max_val=3)
                with eng.Fori(0, n_rounds) as rnd:
                    with eng.Fori(0, NG) as g:
                        n = rnd * NG + g
                        group_pre(g, n)
                        with eng.Fori(0, EPG // RING) as half:
                            q = n * (EPG // RING) + half
                            expert(half, q)
                        group_post(g, n)
                    if round_end:
                        round_end(rnd)

            @block.tensor
            def _(pe):
                mm = nc.tensor.matmul

                def loose(out, lhsT, rhs, start, stop):
                    return nc.tensor.matmul(out, lhsT, rhs, start=start, stop=stop, skip_group_check=True)

                pe.wait_ge(sem("wout_in"), 64)
                for tt in range(3):
                    for hf in range(2):
                        for kk in range(KT):
                            w = wout[kk // 2][:].rearrange("p a b -> p (a b)")[:, (kk % 2) * D + hf * 512:(kk % 2) * D + hf * 512 + 512]
                            last = mm(psum[2 * tt + hf][rows(tt), :], merged[:, kk, cols(tt)], w, start=(kk == 0), stop=(kk == KT - 1))
                    last.then_inc(sem("wo_mm"), 1)
                for tt in range(3):
                    pe.wait_ge(sem("xn2_ready"), tt + 1)
                for kk in range(KT):
                    if kk >= 2:
                        pe.wait_ge(sem("xnt_copy"), kk - 1)
                    for tt in range(3):
                        last = nc.tensor.transpose(psum[6 + kk % 2][:, cols(tt)], xn[rows(tt), tt, kk * P:(kk + 1) * P], ident[rows(tt), rows(tt)])
                    last.then_inc(sem("xnt_mm"), 1)
                pe.wait_ge(sem("xnt_copy"), KT)
                pe.wait_ge(sem("rw_in"), 64)
                for tt in range(3):
                    for kk in range(KT):
                        last = mm(psum[0][rows(tt), tt * 64:tt * 64 + NG + NE], xnt[:, kk, cols(tt)], rw[:, kk, :], start=(kk == 0), stop=(kk == KT - 1))
                last.then_inc(sem("logit_mm"), 1)
                pe.wait_ge(sem("gmask_ready"), 1)
                for tt in range(3):
                    m = SIZE[tt]
                    for u in range(tt):
                        mm(psum[1][0:m, tt * NG:(tt + 1) * NG], ones[:, 0:m], gmask[:, u, :], start=(u == 0), stop=False)
                    mm(psum[1][0:m, tt * NG:(tt + 1) * NG], tri[0:m, 0:m], gmask[0:m, tt, :], start=(tt == 0), stop=True)
                for tt in range(3):
                    last = mm(psum[1][:, 16:16 + NG], ones[rows(tt), :], gmask[rows(tt), tt, :], start=(tt == 0), stop=(tt == 2))
                last.then_inc(sem("pos_mm"), 1)

                def group_pre(g, n):
                    pe.wait_ge(sem("G_ready"), n + 1)
                    pe.wait_ge(sem("bank_free"), n + 1)
                    for kk in range(KT):
                        for tt in range(3):
                            last = mm(psum[kk // 4][:, (kk % 4) * SLOTS:(kk % 4 + 1) * SLOTS], xn[rows(tt), tt, kk * P:(kk + 1) * P],
                                      G[rows(tt), tt, :], start=(tt == 0), stop=(tt == 2))
                    last.then_inc(sem("xg_mm"), 1)
                    for e in range(EPG):
                        for tt in range(3):
                            last = mm(psum[2 + e // 4][:, (e % 4) * SLOTS:(e % 4 + 1) * SLOTS], cg[rows(tt), tt, e:e + 1].broadcast_to([SIZE[tt], P]),
                                      G[rows(tt), tt, :], start=(tt == 0), stop=(tt == 2))
                    last.then_inc(sem("cb_mm"), 1)
                    pe.wait_ge(sem("xg_copy"), 2 * n + 2)
                    for tt in range(3):
                        last = nc.tensor.transpose(psum[0][0:SLOTS, cols(tt)], G[rows(tt), tt, :], ident[rows(tt), rows(tt)])
                    last.then_inc(sem("gt_mm"), 1)

                def gate_up(s, q):
                    b = MB[s % 2]
                    pe.wait_ge(sem(f"expert_in{s}"), 48 * (q + 1))
                    pe.wait_ge(sem(f"h_bank{s % 2}"), q * 2 + s // 2 + 1)
                    for f in range(4):
                        w = wg[s] if f < 2 else wu[s]
                        for kk in range(KT):
                            last = mm(b[:, f * SLOTS:(f + 1) * SLOTS], w[:, kk, (f % 2) * P:(f % 2 + 1) * P], xg[:, kk, :], start=(kk == 0), stop=(kk == KT - 1))
                    last.then_inc(sem(f"gu_mm{s % 2}"), 1)

                def down(s, q, half):
                    pe.wait_ge(sem(f"h_ready{s % 2}"), q * 2 + s // 2 + 1)
                    for kk in range(KT):
                        for f in range(2):
                            last = loose(YB[kk // 4][:, (kk % 4) * SLOTS:(kk % 4 + 1) * SLOTS], wd[s][:, f, kk * P:(kk + 1) * P], h[s % 2][:, f, :], False, True)
                    last.then_inc(sem(f"slot_free{s}"), 1)
                    return last

                def expert(half, q):
                    gate_up(0, q)
                    gate_up(1, q)
                    down(0, q, half)
                    gate_up(2, q)
                    down(1, q, half)
                    gate_up(3, q)
                    down(2, q, half)
                    down(3, q, half)

                def group_clear(g, n):
                    group_pre(g, n)
                    for b in range(2):
                        loose(YB[b][:, 0:4 * SLOTS], zeros[:, 0:P], zeros[:, 0:4 * SLOTS], True, False)

                def group_post(g, n):
                    loose(YB[1][:, 0:4 * SLOTS], zeros[:, 0:P], zeros[:, 0:4 * SLOTS], False, True).then_inc(sem("ysum_mm"), 1)
                    pe.wait_ge(sem("ysb_copy"), 2 * n + 2)
                    for kk in range(KT):
                        last = nc.tensor.transpose(psum[2 + kk // 4][0:SLOTS, (kk % 4) * P:(kk % 4 + 1) * P], ysb[:, kk, :], ident[:])
                    last.then_inc(sem("yt_mm"), 1)
                    pe.wait_ge(sem("yt_copy"), 2 * n + 2)
                    for tt in range(3):
                        for hf in range(2):
                            bank = psum[(2 * tt + hf) % 4]
                            if tt == 2:
                                pe.wait_ge(sem("scat_add"), n * 6 + hf + 1)
                            mm(bank[rows(tt), :], GT[:, cols(tt)], yt[:, hf * 512:(hf + 1) * 512], start=True, stop=True).then_inc(sem("scat_mm"), 1)

                zeros = sb["zeros"]
                loop(pe, group_clear, expert, group_post)

            @block.scalar
            def _(act):
                A = nc.scalar
                for tt in range(3):
                    act.wait_ge(sem("x1_ready"), tt + 1)
                    if tt:
                        act.wait_ge(sem("x1_sq"), tt)
                    A.activation(junk[rows(tt), :], x[rows(tt), tt, :], ACT.Square, accum_out=stat[rows(tt), tt, 0:1]).then_inc(sem("x1_sq"), 1)
                act.wait_ge(sem("x1_sq"), 3)
                A.activation(stat[:, :, 1:2], stat[:, :, 0:1], ACT.Sqrt, scale=1.0 / D, bias=eps[:, 2:3]).then_inc(sem("x1_root"), 1)
                for kk in range(0, KT, 2):
                    act.wait_ge(sem("xnt_mm"), kk + 1)
                    if kk:
                        act.wait_ge(sem("xnt_copy"), kk)
                    A.copy(xnt[:, kk, :], psum[6 + kk % 2][:, 0:T]).then_inc(sem("xnt_copy"), 1)
                act.wait_ge(sem("gdiff_ready"), 1)
                A.activation(gexp[:], gexp[:], ACT.Exp).then_inc(sem("gexp_ready"), 1)
                act.wait_ge(sem("ediff_ready"), 1)
                A.activation(tw[:, :, 1:2], tw[:, :, 0:1], ACT.Exp).then_inc(sem("eexp_ready"), 1)

                def group_pre(g, n):
                    act.wait_ge(sem("xg_mm"), n + 1)
                    A.copy(xg[:, 0:4, :], psum[0][:, 0:4 * SLOTS].rearrange("p (k s) -> p k s", k=4)).then_inc(sem("xg_copy"), 1)
                    act.wait_ge(sem("cb_mm"), n + 1)
                    A.copy(cb[:, 0:4, :], psum[2][:, 0:4 * SLOTS].rearrange("p (k s) -> p k s", k=4)).then_inc(sem("cb_copy"), 1)
                    act.wait_ge(sem("gt_mm"), n + 1)
                    A.copy(GT[:], psum[0][0:SLOTS, 0:T]).then_inc(sem("gt_copy"), 1)

                def expert(half, q):
                    for s in range(RING):
                        p = s % 2
                        act.wait_ge(sem(f"gu_mm{p}"), q * 2 + s // 2 + 1)
                        act.wait_ge(sem(f"h_bank{p}"), q * 2 + s // 2 + 1)
                        A.activation(th[p][:], MB[p][:, 0:2 * SLOTS].rearrange("p (f s) -> p f s", f=2), ACT.Tanh, scale=0.5).then_inc(sem(f"th_ready{p}"), 1)

                def group_post(g, n):
                    act.wait_ge(sem("ysum_mm"), n + 1)
                    A.copy(ysb[:, 0:4, :], YB[0][:, 0:4 * SLOTS].rearrange("p (k s) -> p k s", k=4)).then_inc(sem("ysb_copy"), 1)
                    act.wait_ge(sem("yt_mm"), n + 1)
                    A.copy(yt[:, 0:512], psum[2][0:SLOTS, :]).then_inc(sem("yt_copy"), 1)

                loop(act, group_pre, expert, group_post)
                act.wait_ge(sem("moe_done"), 1)
                for tt in range(3):
                    if tt:
                        act.wait_ge(sem("x2_sq"), tt)
                    A.activation(junk[rows(tt), :], x[rows(tt), tt, :], ACT.Square, accum_out=stat[rows(tt), tt, 0:1]).then_inc(sem("x2_sq"), 1)
                act.wait_ge(sem("x2_sq"), 3)
                A.activation(stat[:, :, 1:2], stat[:, :, 0:1], ACT.Sqrt, scale=1.0 / D, bias=eps[:, 2:3]).then_inc(sem("x2_root"), 1)

            @block.vector
            def _(dve):
                V = nc.vector
                step = [0]

                def then(ins):
                    step[0] += 1
                    ins.then_inc(sem("router_step"), 1)
                    dve.wait_ge(sem("router_step"), step[0])

                V.memset(sb["zeros"][:], 0.0)
                V.memset(stat[:], 1.0)
                V.memset(gmask[:], 0.0)
                V.memset(cg[:], 0.0)
                V.memset(lg[:], 0.0)
                V.memset(gpad[:], -3.0e38)
                for s in range(2):
                    dve.sem_inc(sem(f"slot_free{s}"), 1)
                    dve.sem_inc(sem(f"h_bank{s}"), 1)
                dve.wait_ge(sem("x2_in"), 32)
                for tt in range(3):
                    dve.wait_ge(sem("wo_mm"), tt + 1)
                    for hf in range(2):
                        hc = slice(hf * 512, (hf + 1) * 512)
                        last = V.tensor_tensor(x[rows(tt), tt, hc], x[rows(tt), tt, hc], psum[2 * tt + hf][rows(tt), :], add)
                    last.then_inc(sem("x1_ready"), 1)
                for s in (2, 3):
                    dve.sem_inc(sem(f"slot_free{s}"), 1)
                dve.wait_ge(sem("x1_root"), 1)
                then(V.reciprocal(stat[:, :, 2:3], stat[:, :, 1:2]))
                dve.wait_ge(sem("gffn_in"), 16)
                for tt in range(3):
                    V.scalar_tensor_tensor(out=xn[rows(tt), tt, :], in0=x[rows(tt), tt, :], scalar=stat[rows(tt), tt, 2:3],
                                           in1=gbc[rows(tt), :], op0=mult, op1=mult).then_inc(sem("xn2_ready"), 1)
                for kk in range(1, KT, 2):
                    dve.wait_ge(sem("xnt_mm"), kk + 1)
                    dve.wait_ge(sem("xnt_copy"), kk)
                    V.tensor_copy(xnt[:, kk, :], psum[6 + kk % 2][:, 0:T]).then_inc(sem("xnt_copy"), 1)
                dve.wait_ge(sem("logit_mm"), 1)
                for tt in range(3):
                    last = V.tensor_tensor(lg[rows(tt), tt, :], psum[0][rows(tt), tt * 64:tt * 64 + NG + NE], rb[rows(tt), :], add)
                then(last)
                then(V.tensor_copy(gpad[:, :, 0:NG], lg[:, :, 0:NG]))
                for tt in range(3):
                    last = V.max(top[:, tt, :], gpad[:, tt, :])
                then(last)
                for tt in range(3):
                    last = V.max_index(topi[:, tt, :], top[:, tt, :], gpad[:, tt, :])
                then(last)
                then(V.tensor_copy(topf[:], topi[:]))
                for tt, m in enumerate(SIZE):
                    last = V.tensor_scalar(gmask[0:m, tt, :], slot[0:m, 0:NG], topf[0:m, tt, 0:1], None, ALU.is_equal)
                last.then_inc(sem("gmask_ready"), 1)
                V.tensor_tensor(gexp[:], lg[:, :, 0:NG], top[:, :, 0:1].broadcast_to([P, 3, NG]), sub).then_inc(sem("gdiff_ready"), 1)
                dve.wait_ge(sem("gmask_ready"), 1)
                then(V.tensor_tensor(eprod[:], lg[:, :, NG:NG + NE].rearrange("p t (g e) -> p t e g", g=NG),
                                     gmask[:].unsqueeze(2).broadcast_to([P, 3, EPG, NG]), mult))
                then(V.tensor_reduce(esel[:], eprod[:], AX_X, add))
                dve.wait_ge(sem("gexp_ready"), 1)
                V.tensor_reduce(gsum[:, :, 0:1], gexp[:], AX_X, add)
                for tt in range(3):
                    last = V.max(top[:, tt, :], esel[:, tt, :])
                then(last)
                for tt in range(3):
                    last = V.max_index(topi[:, tt, :], top[:, tt, :], esel[:, tt, :])
                then(last)
                V.reciprocal(gsum[:, :, 1:2], gsum[:, :, 0:1])
                V.tensor_copy(topf[:], topi[:])
                V.tensor_tensor(tw[:, :, 0:1], top[:, :, 1:2], top[:, :, 0:1], sub).then_inc(sem("ediff_ready"), 1)
                dve.wait_ge(sem("eexp_ready"), 1)
                then(V.tensor_scalar(tw[:, :, 2:3], tw[:, :, 1:2], 1.0, None, add))
                then(V.reciprocal(tw[:, :, 3:4], tw[:, :, 2:3]))
                then(V.tensor_tensor(tw[:, :, 2:3], tw[:, :, 3:4], gsum[:, :, 1:2], mult))
                then(V.tensor_tensor(tw[:, :, 3:4], tw[:, :, 2:3], tw[:, :, 1:2], mult))
                for tt in range(3):
                    V.tensor_scalar(c8[:, tt, :], slot[:, 0:8], topf[:, tt, 0:1], tw[:, tt, 2:3], ALU.is_equal, mult)
                    last = V.tensor_scalar(c8b[:, tt, :], slot[:, 0:8], topf[:, tt, 1:2], tw[:, tt, 3:4], ALU.is_equal, mult)
                then(last)
                then(V.tensor_tensor(c8[:], c8[:], c8b[:], add))
                for tt in range(3):
                    V.tensor_tensor(comb[:, tt], gmask[:, tt, :].unsqueeze(2).broadcast_to([P, NG, EPG]),
                                    c8[:, tt, :].unsqueeze(1).broadcast_to([P, NG, EPG]), mult)
                dve.wait_ge(sem("pos_mm"), 1)
                for tt in range(3):
                    V.tensor_copy(pos[rows(tt), tt, :], psum[1][rows(tt), tt * NG:(tt + 1) * NG])
                then(V.tensor_reduce(cnt[:, 0:1], psum[1][:, 16:16 + NG], AX_X, ALU.max))
                then(V.tensor_scalar(cnt[:, 1:2], cnt[:, 0:1], float(SLOTS), 1.0, ALU.is_gt, add))
                V.tensor_scalar(cnt[:, 2:3], cnt[:, 0:1], float(2 * SLOTS), None, ALU.is_gt).then_inc(sem("cnt_step"), 1)
                dve.wait_ge(sem("cnt_step"), 1)
                V.tensor_tensor(rounds_i[:], cnt[:, 1:2], cnt[:, 2:3], add).then_inc(sem("rounds_ready"), 1)
                dve.sem_inc(sem("bank_free"), 1)

                def group_pre(g, n):
                    V.tensor_copy(pcol[:, 0:2], pos[:, 0:2, bass.ds(g, 1)].rearrange("p t o -> p (t o)"))
                    V.tensor_copy(pcol[0:B, 2:3], pos[0:B, 2, bass.ds(g, 1)])
                    V.tensor_copy(mcol[:], gmask[:, :, bass.ds(g, 1)].rearrange("p t o -> p (t o)"))
                    V.tensor_copy(cg[:], comb[:, :, bass.ds(g, 1), :].rearrange("p t o e -> p t (o e)")).then_inc(sem("cols_ready"), 1)
                    dve.wait_ge(sem("cols_ready"), n + 1)
                    for tt in range(3):
                        last = V.tensor_scalar(G[rows(tt), tt, :], slot[rows(tt), :], pcol[rows(tt), tt:tt + 1], mcol[rows(tt), tt:tt + 1], ALU.is_equal, mult)
                    last.then_inc(sem("G_ready"), 1)
                    dve.wait_ge(sem("xg_mm"), n + 1)
                    V.tensor_copy(xg[:, 4:8, :], psum[1][:, 0:4 * SLOTS].rearrange("p (k s) -> p k s", k=4)).then_inc(sem("xg_copy"), 1)
                    dve.wait_ge(sem("cb_mm"), n + 1)
                    V.tensor_copy(cb[:, 4:8, :], psum[3][:, 0:4 * SLOTS].rearrange("p (k s) -> p k s", k=4)).then_inc(sem("cb_copy"), 1)
                    dve.wait_ge(sem("cb_copy"), 2 * n + 2)
                    V.memset(hold[:], 0.0)

                def expert(half, q):
                    for s in range(RING):
                        p = s % 2
                        turn = q * 2 + s // 2
                        gate = MB[p][:, 0:2 * SLOTS].rearrange("p (f s) -> p f s", f=2)
                        up = MB[p][:, 2 * SLOTS:4 * SLOTS].rearrange("p (f s) -> p f s", f=2)
                        dve.wait_ge(sem(f"th_ready{p}"), turn + 1)
                        V.scalar_tensor_tensor(out=hs[p][:], in0=th[p][:], scalar=1.0, in1=gate, op0=add, op1=mult).then_inc(sem(f"silu{p}"), 1)
                        dve.wait_ge(sem(f"silu{p}"), turn + 1)
                        V.tensor_tensor(th[p][:], hs[p][:], up, mult).then_inc(sem(f"h_bank{p}"), 1)
                        dve.wait_ge(sem(f"h_bank{p}"), turn + 2)
                        V.scalar_tensor_tensor(out=h[p][:], in0=th[p][:], scalar=0.5,
                                               in1=cb[:, bass.ds(half * RING + s, 1), :].broadcast_to([P, 2, SLOTS]),
                                               op0=mult, op1=mult).then_inc(sem(f"h_ready{p}"), 1)

                def group_post(g, n):
                    dve.wait_ge(sem("ysum_mm"), n + 1)
                    V.tensor_copy(ysb[:, 4:8, :], YB[1][:, 0:4 * SLOTS].rearrange("p (k s) -> p k s", k=4)).then_inc(sem("ysb_copy"), 1)
                    dve.wait_ge(sem("yt_mm"), n + 1)
                    V.tensor_copy(yt[:, 512:1024], psum[3][0:SLOTS, :]).then_inc(sem("yt_copy"), 1)
                    for tt in range(3):
                        for hf in range(2):
                            hc = slice(hf * 512, (hf + 1) * 512)
                            dve.wait_ge(sem("scat_mm"), n * 6 + 2 * tt + hf + 1)
                            last = V.tensor_tensor(x[rows(tt), tt, hc], x[rows(tt), tt, hc], psum[(2 * tt + hf) % 4][rows(tt), :], add)
                            last.then_inc(sem("scat_add"), 1)
                    settle(dve)
                    dve.wait_ge(sem("scat_add"), n * 6 + 6)
                    dve.sem_inc(sem("bank_free"), 1)

                def round_end(rnd):
                    for tt in range(3):
                        last = V.tensor_scalar(pos[rows(tt), tt, :], pos[rows(tt), tt, :], -float(SLOTS), None, add)
                    last.then_inc(sem("pos_shifted"), 1)
                    settle(dve)
                    dve.wait_ge(sem("pos_shifted"), rnd + 1)

                loop(dve, group_pre, expert, group_post, round_end)
                dve.sem_inc(sem("moe_done"), 1)
                dve.wait_ge(sem("x2_root"), 1)
                V.reciprocal(stat[:, :, 2:3], stat[:, :, 1:2]).then_inc(sem("x2_inv"), 1)
                dve.wait_ge(sem("x2_inv"), 1)
                dve.wait_ge(sem("gfin_in"), 16)
                for tt in range(3):
                    last = V.scalar_tensor_tensor(out=xn[rows(tt), tt, :], in0=x[rows(tt), tt, :], scalar=stat[rows(tt), tt, 2:3],
                                                  in1=gfin[rows(tt), :], op0=mult, op1=mult)
                last.then_inc(sem("y_final"), 1)


_INS = ['x_prompt', 'x_sample', 'state_ret', 'state_rwkv', 'state_shift', 'norm_mix', 'w_in', 'mu_shift', 'ret_gn_w',
        'rwkv_w0', 'rwkv_w2', 'rwkv_a0', 'rwkv_a2', 'rwkv_g2', 'rwkv_k_k', 'rwkv_k_a', 'rwkv_r_k', 'rwkv_lnx_w',
        'rwkv_lnx_b', 'w_out', 'norm_ffn', 'router_group_w', 'router_group_b', 'router_expert_w', 'router_expert_b',
        'expert_w_gate', 'expert_w_up', 'expert_w_down', 'norm_final']
_OUTS = [("y_p", (1, TP, D)), ("y_s", (B, 1, D)), ("ret_p", (1, 1, HEADS, P, P)), ("rwkv_p", (1, 1, RH, HD, HD)),
         ("shift_p", (1, 1, D)), ("ret_s", (1, B, HEADS, P, P)), ("rwkv_s", (1, B, RH, HD, HD)), ("shift_s", (1, B, D))]


def kernel(**inputs):
    import numpy as _np
    import concourse.bacc as _bacc
    from concourse import mybir as _mybir
    from concourse.bass_utils import run_bass_kernel_spmd as _run

    nc = _bacc.Bacc("TRN2", target_bir_lowering=False, num_devices=1)
    arrays, args, consts, outs = {}, {}, {}, {}
    for name in _INS:
        arr = _np.ascontiguousarray(inputs[name])
        arrays[f"in_{name}_dram"] = arr
        args[name] = nc.dram_tensor(f"in_{name}_dram", arr.shape, _mybir.dt.from_np(arr.dtype), kind="ExternalInput").ap()
    for name, arr in constants().items():
        arrays[f"const_{name}_dram"] = arr
        consts[name] = nc.dram_tensor(f"const_{name}_dram", arr.shape, _mybir.dt.from_np(arr.dtype), kind="ExternalInput").ap()
    for name, shape in _OUTS:
        outs[name] = nc.dram_tensor(f"out_{name}_dram", shape, _mybir.dt.float32, kind="ExternalOutput").ap()
    hybrid_moe_step(nc, args, outs, consts)
    res = _run(nc, [arrays], core_ids=[0]).results[0]
    return tuple(res[f"out_{name}_dram"] for name, _ in _OUTS)
```

```python
from contextlib import ExitStack

import numpy as np

import concourse.bass as bass
from concourse import mybir

ALU = mybir.AluOpType
ACT = mybir.ActivationFunctionType
F32 = mybir.dt.float32
I32 = mybir.dt.int32
AX_X = mybir.AxisListType.X

P = 128
D = 1024
KT = D // P
TP = 256
TT = TP // P
B = 8
T = TP + B
TX = T + B
HEADS = 8
RH = 16
HD = 64
C = 64
NCH = TP // C
PAST = 2048
NG, EPG = 4, 8
NE = NG * EPG
DE = 256
SLOTS = 96
LORA = 64
LORA_G = 160
RMS_EPS, RET_EPS, RWKV_EPS = 1e-6, 1e-5, 64e-5

O_Q, O_K, O_V, O_GS = 0, D, 2 * D, 3 * D
O_SH = 4 * D
O_R, O_RK, O_RV = O_SH, O_SH + D, O_SH + 2 * D
O_LORA = O_SH + 3 * D
N_LORA = 2 * LORA + LORA_G
O_GA = O_LORA + N_LORA
O_GB = O_GA + D
N_IN = O_GB + D
SECTIONS = [O_R, O_RK, O_RV, O_Q, O_K, O_V, O_GS, O_GA, O_GB]

PAR = ["mu_r", "mu_k", "mu_v", "w0", "a0", "k_k", "k_a", "r_k", "lnx_w", "lnx_b", "gn_w"]
NPAR = len(PAR)
DERIVED = ["om_r", "om_k", "om_v", "w0h", "a0h", "om_ka"]
PX = {n: i for i, n in enumerate(PAR + DERIVED)}
NPX = len(PX)
LOGW_C = -0.5 * float(np.exp(-0.5))


def constants():
    out = {}
    half = P // 2
    inv = (10000.0 ** (-np.arange(half, dtype=np.float32) / np.float32(half))).astype(np.float32)
    pos = np.concatenate([np.arange(TP), np.full(B, PAST)]).astype(np.float32)
    ang = (inv[:, None] * pos[None, :]).astype(np.float32).astype(np.float64)
    cos, sin = np.cos(ang), np.sin(ang)
    cs = np.concatenate([cos, cos], 0)
    sn = np.concatenate([sin, -sin], 0)
    scale = P ** -0.5
    out["rope"] = np.stack([cs, sn, cs * scale, sn * scale], 1)
    lg = np.log1p(-np.exp2(-5.0 - np.arange(HEADS)))
    j = np.arange(P)[:, None]
    i0 = np.arange(TP)[None, :]
    dec = np.zeros((P, HEADS, TP + P))
    kd = np.zeros((P, HEADS, 3))
    for h in range(HEADS):
        dec[:, h, :TP] = np.where(i0 >= j, np.exp(np.maximum(i0 - j, 0) * lg[h]), 0)
        i1 = np.arange(P)[None, :]
        dec[:, h, TP:] = np.where(i1 >= j, np.exp(np.maximum(i1 - j, 0) * lg[h]), 0)
        for tt in range(TT):
            kd[:, h, tt] = np.exp((TP - 1 - tt * P - np.arange(P)) * lg[h])
        kd[:, h, 2] = np.exp(lg[h])
    out["retdec"] = dec
    out["retcol"] = kd
    s, t = np.meshgrid(np.arange(P), np.arange(P), indexing="ij")
    same64 = s // C == t // C
    same16 = s // 16 == t // 16
    m = np.zeros((P, 4, P))
    m[:, 0] = same16 & (s < t)
    m[:, 1] = same64 & (s <= t)
    m[:, 2] = same64 & (s < t)
    m[:, 3] = same64 & (s <= t)
    out["mk"] = m
    lo = np.zeros((P, 2, P))
    lo[:, 0] = same16 & (t < s)
    lo[:, 1] = same64 & ~same16 & (t < s)
    out["mlo"] = lo
    out["ident"] = np.eye(P)
    out["one64"] = (s // HD == t // HD).astype(np.float64)
    out["mean64"] = out["one64"] / HD
    out["mean128"] = np.ones((P, P)) / P
    sm = np.ones((P, T))
    sm[:, 0:TP:C] = 0
    sm[:, TP:] = 0
    out["scanm"] = sm
    out["tri"] = (s < t).astype(np.float64)
    out["ones"] = np.ones((P, P))
    out["id64"] = np.concatenate([np.eye(HD), np.eye(HD)], 0)
    out["slot"] = np.tile(np.arange(SLOTS)[None, :], (P, 1)).astype(np.float64)
    d8 = np.zeros((B, B, P))
    for b in range(B):
        d8[b, b] = 1
    out["diag8"] = d8
    return {k: np.ascontiguousarray(v.astype(np.float32)) for k, v in out.items()}


class Semaphores:

    def __init__(self, nc):
        self.nc = nc
        self.named = {}
        self.stack = ExitStack()

    def __call__(self, name):
        if name not in self.named:
            self.named[name] = self.stack.enter_context(self.nc.semaphore(name))
        return self.named[name]

    def next_phase(self):
        with self.nc.Block() as block:

            @block.gpsimd
            def _(pool):
                for handle in self.named.values():
                    pool.sem_clear(handle)

        self.named = {}
        self.stack.close()


def hybrid_moe_step(nc, a, o, k):
    w_in = a["w_in"][0].rearrange("(k p) c -> p k c", p=P)

    with ExitStack() as top:
        keep = {}

        def alloc(ctx, table, name, shape, dt=F32):
            table[name] = ctx.enter_context(nc.sbuf_tensor(name, shape, dt))
            return table[name]

        sem = Semaphores(nc)

        psum = [top.enter_context(nc.psum_tensor(f"bank{n}", [P, 512], F32)) for n in range(8)]
        cst = {}
        for n in ("ident", "one64", "mean64", "mean128", "tri", "ones", "slot", "id64"):
            alloc(top, cst, "c_" + n, list(k[n].shape))
        merged = alloc(top, keep, "merged", [P, KT, T])
        svec = alloc(top, keep, "svec", [P, KT, 6, B])
        spost = alloc(top, keep, "spost", [P, 3, KT, B])
        parc = alloc(top, keep, "parc", [P, NPX, KT])
        gbc = alloc(top, keep, "gbc", [P, D])
        eps = alloc(top, keep, "eps", [P, 4])

        mixer_phase(nc, a, o, k, w_in, alloc, sem, psum, cst, keep)
        sem.next_phase()
        sample_phase(nc, a, o, k, alloc, sem, psum, cst, keep)
        sem.next_phase()
        moe_phase(nc, a, o, k, alloc, sem, psum, cst, keep)
        sem.next_phase()


def mixer_phase(nc, a, o, k, w_in, alloc, sem, psum, cst, keep):
    with ExitStack() as ctx:
        sb = {}

        def buf(name, shape):
            return alloc(ctx, sb, name, shape)

        ident, one64, mean64, mean128 = (cst["c_" + n] for n in ("ident", "one64", "mean64", "mean128"))
        merged, svec, spost, parc, gbc, eps = (keep[n] for n in ("merged", "svec", "spost", "parc", "gbc", "eps"))
        rope = buf("rope", [P, 4, T])
        retdec = buf("retdec", [P, HEADS, TP + P])
        retcol = buf("retcol", [P, HEADS, 3])
        mk = buf("mk", [P, 4, P])
        mlo = buf("mlo", [P, 2, P])
        scanm = buf("scanm", [P, T])
        diag8 = buf("diag8", [B, B, P])

        xt = buf("xt", [P, KT, TX])
        wslot = [buf(f"wslot{n}", [P, KT, P]) for n in range(9)]
        lowa = buf("lowa", [P, D])
        g2a = buf("g2a", [P, D])
        g2b = buf("g2b", [LORA_G - P, D])
        lwa = buf("lwa", [P, T])
        lga = buf("lga", [P, T])
        lgb = buf("lgb", [LORA_G - P, T])
        mulora = buf("mulora", [P, 6])

        def tok(name):
            return buf(name, [P, T])

        pro = ExitStack()
        x_tok = alloc(pro, sb, "x_tok", [P, TT, D])
        xs_tok = alloc(pro, sb, "xs_tok", [2 * B, D])
        sq_junk = alloc(pro, sb, "sq_junk", [P, D])
        stat = alloc(pro, sb, "stat", [P, 3, 4])
        prow = alloc(pro, sb, "prow", [P, P])
        wlora = alloc(pro, sb, "wlora", [P, KT, N_LORA])
        mpro = alloc(pro, sb, "mpro", [P, 3, TX + 1])

        mult, add, sub = ALU.mult, ALU.add, ALU.subtract

        def mm(pe, out, lhsT, rhs, start, stop, loose=False):
            return nc.tensor.matmul(out, lhsT, rhs, start=start, stop=stop, skip_group_check=loose)

        with nc.Block() as block:

            @block.sync
            def _(sp):
                sp.dma_start(sb["x_tok"][:], a["x_prompt"][0].rearrange("(t p) d -> p t d", p=P)).then_inc(sem("x_in"), 16)
                sp.dma_start(sb["xs_tok"][0:B, :], a["x_sample"].rearrange("b t d -> (b t) d")).then_inc(sem("x_in"), 16)
                sp.dma_start(sb["xs_tok"][B:2 * B, :], a["state_shift"][0]).then_inc(sem("x_in"), 16)
                sp.dma_start(gbc[:], a["norm_mix"].partition_broadcast(P)).then_inc(sem("x_in"), 16)
                sp.dma_start(wlora[:], w_in[:, :, O_LORA:O_LORA + N_LORA]).then_inc(sem("wlora_in"), 16)
                sp.dma_start(lowa[0:LORA, :], a["rwkv_w2"][0]).then_inc(sem("lora_in"), 16)
                sp.dma_start(lowa[LORA:2 * LORA, :], a["rwkv_a2"][0]).then_inc(sem("lora_in"), 16)
                sp.dma_start(g2a[:], a["rwkv_g2"][0][0:P, :]).then_inc(sem("lora_in"), 16)
                sp.dma_start(g2b[:], a["rwkv_g2"][0][P:LORA_G, :]).then_inc(sem("lora_in"), 16)
                sp.wait_ge(sem("xn_ready"), 1)
                sp.dma_start(o["shift_p"][0, 0:1, :], sb["x_tok"][P - 1:P, TT - 1, :]).then_inc(sem("out_done"), 16)
                sp.dma_start(o["shift_s"][0], sb["xs_tok"][0:B, :]).then_inc(sem("out_done"), 16)
                sp.wait_ge(sem("out_done"), 32)
                sp.wait_ge(sem("lora_in"), 64)

            @block.scalar
            def _(act):
                act.wait_ge(sem("prow_zero"), 1)
                rows = [a["mu_shift"][0, n * D:(n + 1) * D] for n in range(3)]
                rows += [a[n][0] for n in ("rwkv_w0", "rwkv_a0", "rwkv_k_k", "rwkv_k_a")]
                rows += [a["rwkv_r_k"][0].rearrange("h c -> (h c)")]
                rows += [a[n][0] for n in ("rwkv_lnx_w", "rwkv_lnx_b", "ret_gn_w")]
                for n, row in enumerate(rows):
                    act.dma_start(prow[n * KT:(n + 1) * KT, :], row.rearrange("(k c) -> k c", c=P)).then_inc(sem("prow_in"), 16)
                lo = NPAR * KT
                mu = a["mu_shift"][0:1, :]
                act.dma_start(prow[lo:lo + 1, :], mu[:, 3 * D:3 * D + P]).then_inc(sem("prow_in"), 16)
                act.dma_start(prow[lo + 1:lo + 2, :], mu[:, 3 * D + P:3 * D + 2 * P]).then_inc(sem("prow_in"), 16)
                act.dma_start(prow[lo + 2:lo + 3, 0:LORA_G - P], mu[:, 3 * D + 2 * P:3 * D + N_LORA]).then_inc(sem("prow_in"), 16)
                for n in ("ident", "one64", "mean64", "mean128", "tri", "ones", "slot", "id64"):
                    act.dma_start(cst["c_" + n][:], k[n]).then_inc(sem("const_in"), 16)
                for n, t in (("rope", rope), ("retdec", retdec), ("retcol", retcol), ("mk", mk), ("mlo", mlo),
                             ("scanm", scanm), ("diag8", diag8)):
                    act.dma_start(t[:], k[n]).then_inc(sem("const_in"), 16)
                act.wait_ge(sem("x_in"), 64)
                act.wait_ge(sem("stat_zero"), 1)
                for t in range(TT):
                    act.activation(sq_junk[:], sb["x_tok"][:, t, :], ACT.Square, accum_out=stat[:, t, 0:1]).then_inc(sem("sq_done"), 1)
                    act.wait_ge(sem("sq_done"), t + 1)
                act.activation(sq_junk[0:B, :], sb["xs_tok"][0:B, :], ACT.Square, accum_out=stat[0:B, 2, 0:1]).then_inc(sem("sq_done"), 1)
                act.wait_ge(sem("ms_ready"), 1)
                act.activation(stat[:, :, 2:3], stat[:, :, 1:2], ACT.Sqrt).then_inc(sem("rms_ready"), 1)
                for kk in range(0, KT, 2):
                    act.wait_ge(sem("xt_mm"), kk + 1)
                    act.copy(xt[:, kk, :], psum[kk][:, 0:TX]).then_inc(sem("xt_act"), 1)
                for n, m in enumerate((P, P, LORA_G - P)):
                    act.wait_ge(sem("lora_mm"), n + 1)
                    act.wait_ge(sem("mulora_ready"), 2)
                    act.activation(mpro[0:m, n, 1:TX + 1], psum[n][0:m, 0:TX], ACT.Copy, scale=mulora[0:m, n:n + 1]).then_inc(sem("lora_mu"), 1)
                act.wait_ge(sem("lora_mix"), 1)
                act.activation(lwa[0:LORA, :], lwa[0:LORA, :], ACT.Tanh)
                act.wait_ge(sem("lora_mix"), 3)
                act.activation(lga[:], lga[:], ACT.Tanh, scale=0.5)
                act.activation(lgb[:], lgb[:], ACT.Tanh, scale=0.5).then_inc(sem("lora_tanh"), 1)

            @block.vector
            def _(dve):
                nc.vector.memset(prow[:], 0.0).then_inc(sem("prow_zero"), 1)
                nc.vector.memset(stat[:], 1.0).then_inc(sem("stat_zero"), 1)
                nc.vector.memset(mpro[:], 0.0).then_inc(sem("mpro_zero"), 1)
                nc.vector.memset(eps[:, 0:1], RET_EPS)
                nc.vector.memset(eps[:, 1:2], RWKV_EPS)
                nc.vector.memset(eps[:, 2:3], RMS_EPS)
                nc.vector.memset(eps[:, 3:4], 0.0).then_inc(sem("eps_ready"), 1)
                dve.wait_ge(sem("sq_done"), 3)
                nc.vector.tensor_scalar(stat[:, :, 1:2], stat[:, :, 0:1], 1.0 / D, RMS_EPS, mult, add).then_inc(sem("ms_ready"), 1)
                dve.wait_ge(sem("rms_ready"), 1)
                nc.vector.reciprocal(stat[:, :, 3:4], stat[:, :, 2:3]).then_inc(sem("rstd_ready"), 1)
                dve.wait_ge(sem("rstd_ready"), 1)
                for t in range(TT):
                    nc.vector.scalar_tensor_tensor(out=sb["x_tok"][:, t, :], in0=sb["x_tok"][:, t, :], scalar=stat[:, t, 3:4],
                                                   in1=gbc[:], op0=mult, op1=mult)
                nc.vector.scalar_tensor_tensor(out=sb["xs_tok"][0:B, :], in0=sb["xs_tok"][0:B, :], scalar=stat[0:B, 2, 3:4],
                                               in1=gbc[0:B, :], op0=mult, op1=mult).then_inc(sem("xn_ready"), 1)
                for kk in range(1, KT, 2):
                    dve.wait_ge(sem("xt_mm"), kk + 1)
                    nc.vector.tensor_copy(xt[:, kk, :], psum[kk][:, 0:TX]).then_inc(sem("xt_dve"), 1)
                dve.wait_ge(sem("par_mm"), 1)
                nc.vector.tensor_copy(parc[:, 0:NPAR, :], psum[7][:, 0:NPAR * KT].rearrange("p (n k) -> p n k", k=KT)).then_inc(sem("par_c"), 1)
                nc.vector.tensor_copy(mulora[:, 0:3], psum[7][:, NPAR * KT:NPAR * KT + 3]).then_inc(sem("mulora_ready"), 1)
                dve.wait_ge(sem("par_c"), 1)
                dve.wait_ge(sem("mulora_ready"), 1)
                nc.vector.tensor_scalar(mulora[:, 3:6], mulora[:, 0:3], -1.0, 1.0, mult, add).then_inc(sem("mulora_ready"), 1)
                nc.vector.tensor_scalar(parc[:, PX["om_r"]:PX["om_v"] + 1, :], parc[:, PX["mu_r"]:PX["mu_v"] + 1, :], -1.0, 1.0, mult, add)
                nc.vector.tensor_scalar(parc[:, PX["w0h"]:PX["a0h"] + 1, :], parc[:, PX["w0"]:PX["a0"] + 1, :], 0.5, None, mult)
                nc.vector.tensor_scalar(parc[:, PX["om_ka"], :], parc[:, PX["k_a"], :], -1.0, 1.0, mult, add).then_inc(sem("parc_ready"), 1)
                dve.wait_ge(sem("mulora_ready"), 2)
                for n, (m, dst) in enumerate(((P, lwa), (P, lga), (LORA_G - P, lgb))):
                    dve.wait_ge(sem("lora_mu"), n + 1)
                    om = mulora[0:m, 3 + n:4 + n]
                    nc.vector.scalar_tensor_tensor(out=dst[0:m, 0:TP], in0=psum[n][0:m, 0:TP], scalar=om, in1=mpro[0:m, n, 0:TP], op0=mult, op1=add)
                    nc.vector.scalar_tensor_tensor(out=dst[0:m, TP:T], in0=psum[n][0:m, TP:T], scalar=om, in1=mpro[0:m, n, T + 1:TX + 1],
                                                   op0=mult, op1=add).then_inc(sem("lora_mix"), 1)
                dve.wait_ge(sem("lora_tanh"), 1)
                nc.vector.tensor_scalar(lga[:], lga[:], 0.5, 0.5, mult, add)
                nc.vector.tensor_scalar(lgb[:], lgb[:], 0.5, 0.5, mult, add).then_inc(sem("lora_ready"), 1)

            @block.tensor
            def _(pe):
                pe.wait_ge(sem("const_in"), 16 * 15)
                pe.wait_ge(sem("prow_in"), 16 * 14)
                pe.wait_ge(sem("xn_ready"), 1)
                for kk in range(KT):
                    for t in range(TT):
                        nc.tensor.transpose(psum[kk][:, t * P:(t + 1) * P], sb["x_tok"][:, t, kk * P:(kk + 1) * P], ident[:])
                    nc.tensor.transpose(psum[kk][:, TP:TX], sb["xs_tok"][:, kk * P:(kk + 1) * P], ident[0:2 * B, 0:2 * B]).then_inc(sem("xt_mm"), 1)
                pe.wait_ge(sem("xt_dve"), 4)
                nrow = NPAR * KT + 3
                nc.tensor.transpose(psum[7][:, 0:nrow], prow[0:nrow, :], ident[0:nrow, 0:nrow]).then_inc(sem("par_mm"), 1)
                pe.wait_ge(sem("xt_act"), 4)
                pe.wait_ge(sem("wlora_in"), 16)
                for n, m in enumerate((P, P, LORA_G - P)):
                    for kk in range(KT):
                        last = mm(pe, psum[n][0:m, 0:TX], wlora[:, kk, n * P:n * P + m], xt[:, kk, :], kk == 0, kk == KT - 1)
                    last.then_inc(sem("lora_mm"), 1)
        pro.close()
        sem.next_phase()

        pt = buf("pt", [P, NPX])
        dcol = buf("dcol", [P, 3])
        epc = buf("epc", [P, NCH])
        ygate, ybias = buf("ygate", [P, TP]), buf("ybias", [P, TP])
        mshift = [buf(f"mshift{n}", [P, TX + 1]) for n in range(3)]
        r, kx, vx = tok("r"), tok("kx"), tok("vx")
        thw, tha, gg = tok("thw"), tok("tha"), tok("gg")
        kk0, kks, kkn = tok("kk0"), tok("kks"), tok("kkn")
        kk, ba, kmod, lp, lpx = tok("kk"), tok("ba"), tok("kmod"), tok("lp"), tok("lpx")
        ep, en, epx = tok("ep"), tok("en"), tok("epx")
        ar = buf("ar", [P, TT, 2, P])
        bt, kt = buf("bt", [P, TP]), buf("kt", [P, TP])
        rkk, bonus = tok("rkk"), tok("bonus")
        qr, kr, vr = tok("qr"), tok("kr"), tok("vr")
        ta, tb = tok("ta"), tok("tb")
        sg, thg = tok("sg"), kks
        ga, gb = tok("ga"), tok("gb")
        pr = buf("pr", [P, 4, 4, P])
        la = buf("la", [P, 4, 2, P])
        a2 = buf("a2", [P, 4, P])
        at2w = buf("at2w", [P, 4, 2, P])
        a4 = buf("a4", [P, 4, P])
        at4w = buf("at4w", [P, 4, 2, P])
        a8, w2s, w3 = buf("a8", [P, 4, P]), buf("w2s", [P, 4, P]), buf("w3", [P, 4, P])
        rhs = buf("rhs", [P, 4, 2, HD])
        nt, x0 = buf("nt", [P, 4, P]), buf("x0", [P, 4, P])
        z1, z2, zf = a2, a4, a8
        tmk = buf("tmk", [P, TT, 3, P])
        fts = buf("fts", [P, NCH, HD])
        q = buf("q", [P, TP])
        zst = [buf(f"zst{n}", [P, HD]) for n in range(NCH)]
        zout = buf("zout", [HD, 2, HD])
        ys, yc, ysq, yrs = tok("ys"), tok("yc"), tok("ysq"), tok("yrs")
        kvt = buf("kvt", [P, 4, P])
        vd = buf("vd", [P, TT, P])
        sc = buf("sc", [P, TP + P])
        ks8 = buf("ks8", [B, 2, P])
        vdiag = buf("vdiag", [B, B, P])
        sin_, snew = buf("sin_", [P, B, P]), buf("snew", [P, B, P])
        stp = buf("stp", [P, P])
        os_, osq, ors = ys, ysq, yrs
        oc = tok("oc")

        pj = [psum[0], psum[1]]
        M = psum[2:8]

        def v4(x):
            return x[:].rearrange("p (u c) -> p u c", u=4)


        def done(eng, name, i):
            eng.wait_ge(sem(name), i + 1)

        def past(eng, name, n):
            eng.wait_ge(sem(name), n)

        def settle(eng):
            eng.wait_ge(sem("mshift_zero"), 1)

        def last_pass(eng, name, i):
            if not (isinstance(i, int) and i == 0):
                eng.wait_ge(sem(name), i)

        emptied = ["k_mix", "w_tanh", "a_tanh", "r_mix", "v_mix", "kk_root", "q_rope", "k_rope", "g_copy", "bonus_sum",
                   "v_copy", "gs_silu", "ga_tanh", "gb_tanh"]
        U_RK, U_W, U_A, U_R, U_RV, U_KK, U_Q, U_K, U_G, U_BON, U_V, U_GS, U_GA, U_GB = range(14)
        slot_of = {use: s for s, use in enumerate((U_RK, U_R, U_RV, U_Q, U_K, U_V, U_GS, U_GA, U_GB))}

        def bank_free(pe, i, use):
            if use >= 2:
                done(pe, emptied[use - 2], i)
            else:
                last_pass(pe, emptied[12 + use], i)

        def project(pe, i, use, half):
            n = slot_of[use]
            if half == 0:
                bank_free(pe, i, use)
                pe.wait_ge(sem(f"w_in{n}"), 16 * (i + 1))
            width = TX if use in (U_RK, U_R, U_RV) else T
            for kk_ in range(half * KT // 2, (half + 1) * KT // 2):
                last = mm(pe, pj[use % 2][:, 0:width], wslot[n][:, kk_, :], xt[:, kk_, 0:width], kk_ == 0, kk_ == KT - 1)
            if half:
                last.then_inc(sem(f"proj{use}"), 1)

        def pe_pass(pe, i, n, wst):
            front, back = i is not None, n is not None
            if front:
                project(pe, i, U_RK, 0)
                project(pe, i, U_RK, 1)
            if back:
                past(pe, "abkr_ready", n)
                past(pe, "o_root", n)
                for t in range(TT):
                    for m, src in enumerate((ar[:, t, 0, :], bt[:, t * P:(t + 1) * P], kt[:, t * P:(t + 1) * P], vx[:, t * P:(t + 1) * P])):
                        last = nc.tensor.transpose(M[4 + t][:, m * P:(m + 1) * P], src, ident[:])
                    last.then_inc(sem(f"tok_mm{t}"), 1)
                for t in range(TT):
                    for h in range(2):
                        u = 2 * t + h
                        hs = slice(HD * h, HD * h + HD)
                        cols = slice(t * P, (t + 1) * P)
                        mm(pe, M[u][:, 0:2 * P], bt[hs, cols], ar[hs, t].rearrange("p a b -> p (a b)"), True, True)
                        mm(pe, M[u][:, 2 * P:4 * P], kt[hs, cols], ar[hs, t].rearrange("p a b -> p (a b)"), True, True).then_inc(sem(f"prod{u}"), 1)
                for h in range(2):
                    past(pe, f"tok_copy{h}", n)
                    for t in range(TT):
                        hs = slice(HD * h, HD * h + HD)
                        last = mm(pe, M[4 + h][:, t * P:(t + 1) * P], ar[hs, t, 0, :], bt[hs, t * P:(t + 1) * P], True, True)
                    last.then_inc(sem(f"lmat{h}"), 1)
            if front:
                done(pe, "stage_lora", i)
                bank_free(pe, i, U_W)
                mm(pe, pj[1][:, 0:T], wst["w"][0:LORA, :], lwa[0:LORA, :], True, True).then_inc(sem(f"proj{U_W}"), 1)
                bank_free(pe, i, U_A)
                mm(pe, pj[0][:, 0:T], wst["w"][LORA:P, :], lwa[LORA:P, :], True, True).then_inc(sem(f"proj{U_A}"), 1)
                project(pe, i, U_R, 0)
                project(pe, i, U_R, 1)
            if back:
                past(pe, "masked", n)
                past(pe, "l_masked", n)
                for u in range(4):
                    last = mm(pe, v4(M[0])[:, u, :], pr[:, u, 0, :], la[:, u, 0, :], True, True)
                last.then_inc(sem("a2_mm"), 1)
                for u in range(4):
                    last = mm(pe, v4(M[1])[:, u, :], la[:, u, 0, :], pr[:, u, 0, :], True, True)
                last.then_inc(sem("at2_mm"), 1)
                for u in range(4):
                    h = u % 2
                    last = mm(pe, M[4][:, u * HD:(u + 1) * HD], pr[:, u, 2, :], tmk[:, u // 2, 2, HD * h:HD * h + HD], True, True)
                last.then_inc(sem("lakv_mm"), 1)
            if front:
                project(pe, i, U_RV, 0)
            if back:
                past(pe, "a2_copy", n)
                past(pe, "w0_ready", n)
                past(pe, "at2_copy", n)
                for u in range(4):
                    last = mm(pe, M[2 + u // 2][:, (u % 2) * 2 * P:(u % 2 + 1) * 2 * P], a2[:, u, :], at2w[:, u].rearrange("p a b -> p (a b)"), True, True)
                last.then_inc(sem("at4w1_mm"), 1)
                for u in range(4):
                    last = mm(pe, v4(M[0])[:, u, :], at2w[:, u, 0, :], a2[:, u, :], True, True)
                last.then_inc(sem("a4_mm"), 1)
            if front:
                project(pe, i, U_RV, 1)
            if back:
                past(pe, "at4_copy", n)
                past(pe, "w1_ready", n)
                past(pe, "a4_copy", n)
                for u in range(4):
                    last = mm(pe, v4(M[5])[:, u, :], at4w[:, u, 0, :], a4[:, u, :], True, True)
                last.then_inc(sem("a8_mm"), 1)
                for u in range(4):
                    last = mm(pe, v4(M[1])[:, u, :], a4[:, u, :], at4w[:, u, 1, :], True, True)
                last.then_inc(sem("w2_mm"), 1)
            if front:
                bank_free(pe, i, U_KK)
                done(pe, "kk_sq", i)
                mm(pe, pj[1][:, 0:T], one64[:], kks[:], True, True).then_inc(sem(f"proj{U_KK}"), 1)
                project(pe, i, U_Q, 0)
            if back:
                past(pe, "a8_copy", n)
                past(pe, "w2_ready", n)
                for u in range(4):
                    last = mm(pe, v4(M[2])[:, u, :], a8[:, u, :], w2s[:, u, :], True, True)
                last.then_inc(sem("w3_mm"), 1)
            if front:
                project(pe, i, U_Q, 1)
            if back:
                past(pe, "w3_ready", n)
                past(pe, "rhs_ready", n)
                for u in range(4):
                    last = mm(pe, v4(M[3])[:, u, :], la[:, u, 1, :], w3[:, u, :], True, True)
                last.then_inc(sem("nt_mm"), 1)
                for u in range(4):
                    last = mm(pe, v4(M[4])[:, u, :], w3[:, u, :], rhs[:, u].rearrange("p a b -> p (a b)"), True, True)
                last.then_inc(sem("x0_mm"), 1)

            def horner(src, bank, ready, name):
                past(pe, ready, n)
                for u in range(4):
                    last = mm(pe, v4(bank)[:, u, :], nt[:, u, :], src[:, u, :], True, True)
                last.then_inc(sem(name), 1)

            if front:
                project(pe, i, U_K, 0)
            if back:
                past(pe, "nt_copy", n)
                horner(x0, M[5], "x0_copy", "z1_mm")
            if front:
                project(pe, i, U_K, 1)
            if back:
                horner(z1, M[0], "z1_ready", "z2_mm")
            if front:
                bank_free(pe, i, U_G)
                mm(pe, pj[0][:, 0:T], wst["ga"][:], lga[:], True, False)
                mm(pe, pj[0][:, 0:T], wst["gb"][:], lgb[:], False, True).then_inc(sem(f"proj{U_G}"), 1)
                bank_free(pe, i, U_BON)
                done(pe, "rkk_ready", i)
                mm(pe, pj[1][:, 0:T], one64[:], rkk[:], True, True).then_inc(sem(f"proj{U_BON}"), 1)
            if back:
                horner(z2, M[1], "z2_ready", "z3_mm")
            if front:
                project(pe, i, U_V, 0)
            if back:
                past(pe, "zf_ready", n)
                for u in range(4):
                    h, t = u % 2, u // 2
                    hs = slice(HD * h, HD * h + HD)
                    last = mm(pe, M[2][hs, t * P:(t + 1) * P], zf[:, u, 0:HD], pr[:, u, 1, :], True, True, True)
                last.then_inc(sem("q_mm"), 1)
                for par in range(2):
                    ps = slice(C * par, C * par + C)
                    for u in range(4):
                        h, t = u % 2, u // 2
                        hs = slice(HD * h, HD * h + HD)
                        hc = slice(HD * h, HD * h + HD)
                        mm(pe, M[4 + par][hs, t * P:t * P + HD], zf[ps, u, 0:HD], tmk[ps, t, 0, hc], t == 0, False, True)
                        mm(pe, M[4 + par][hs, t * P + HD:(t + 1) * P], tmk[ps, t, 0, hc], zf[ps, u, HD:P], False, False, True)
                        last = mm(pe, M[4 + par][hs, t * P + HD:(t + 1) * P], tmk[ps, t, 1, hc], tmk[ps, t, 2, hc], False, False, True)
                    last.then_inc(sem(f"fg_mm{par}"), 1)
                for u in range(4):
                    h, t = u % 2, u // 2
                    hs = slice(HD * h, HD * h + HD)
                    mm(pe, M[3][hs, t * P:(t + 1) * P], zf[:, u, HD:P], pr[:, u, 1, :], t == 0, False, True)
                    mm(pe, M[3][hs, t * P:(t + 1) * P], tmk[:, t, 2, HD * h:HD * h + HD], pr[:, u, 3, :], False, False, True)
            if front:
                project(pe, i, U_V, 1)
            for c in range(1, NCH):
                if back:
                    settle(pe)
                    past(pe, f"state{c - 1}", n)
                    if c == 1:
                        past(pe, "q_ready", n)
                        past(pe, "ft_ready", n)
                    t, par = c // 2, c % 2
                    for h in range(2):
                        hs = slice(HD * h, HD * h + HD)
                        last = mm(pe, M[4 + par][hs, t * P + HD:(t + 1) * P], fts[hs, c, :], zst[c - 1][hs, :], False, True, True)
                    last.then_inc(sem(f"state_mm{c}"), 1)
                    for h in range(2):
                        hs = slice(HD * h, HD * h + HD)
                        last = mm(pe, M[3][hs, c * C:(c + 1) * C], zst[c - 1][hs, :], q[hs, c * C:(c + 1) * C], False, True, True)
                    if c == NCH - 1:
                        last.then_inc(sem("y_mm"), 1)
                if front:
                    project(pe, i, U_GS if c < 3 else U_GA, (c - 1) % 2)
            if back:
                settle(pe)
                past(pe, f"state{NCH - 1}", n)
                nc.tensor.transpose(M[0][0:HD, 0:P], zst[NCH - 1][:], ident[:]).then_inc(sem("zt_mm"), 1)
                past(pe, "y_copy", n)
                mm(pe, M[1][:, 0:TP], mean64[:], ys[:, 0:TP], True, True).then_inc(sem("ymean_mm"), 1)
                past(pe, "zt_copy", n)
            if front:
                done(pe, "q_rope", i)
                done(pe, "k_rope", i)
                mm(pe, M[4][:, 0:TP], kr[:, 0:P], qr[:, 0:TP], True, True)
                mm(pe, M[4][:, TP:TP + P], kr[:, P:TP], qr[:, P:TP], True, True).then_inc(sem("sc_mm"), 1)
                done(pe, "v_copy", i)
                for m, src in enumerate((kr[:, 0:P], kr[:, P:TP], vr[:, 0:P], vr[:, P:TP])):
                    last = nc.tensor.transpose(v4(M[3])[:, m, :], src, ident[:])
                last.then_inc(sem("kvt_mm"), 1)
                nc.tensor.transpose(M[0][0:B, 0:P], kr[:, TP:T], ident[:])
                nc.tensor.transpose(M[0][0:B, P:2 * P], vr[:, TP:T], ident[:]).then_inc(sem("kv8_mm"), 1)
                project(pe, i, U_GA, 1)
            if back:
                past(pe, "y_sq", n)
                mm(pe, M[2][:, 0:TP], mean64[:], ysq[:, 0:TP], True, True).then_inc(sem("yvar_mm"), 1)
            if front:
                done(pe, "sc_ready", i)
                done(pe, "kvt_copy", i)
                mm(pe, M[5][:, 0:TP], kvt[:, 2, :], sc[:, 0:TP], True, False, True)
                mm(pe, M[5][:, P:TP], kvt[:, 3, :], sc[:, TP:TP + P], False, True, True)
                done(pe, "vd_ready", i)
                mm(pe, M[4][:, 0:P], kvt[:, 0, :], vd[:, 0, :], True, False)
                mm(pe, M[4][:, 0:P], kvt[:, 1, :], vd[:, 1, :], False, True).then_inc(sem("stp_mm"), 1)
                done(pe, "vdiag_ready", i)
                vflat = vdiag[:].rearrange("b c d -> b (c d)")
                mm(pe, M[0][:, :], ks8[:, 0, :], vflat[:, 0:512], True, True)
                mm(pe, M[3][:, :], ks8[:, 0, :], vflat[:, 512:1024], True, True).then_inc(sem("kv_mm"), 1)
                project(pe, i, U_GB, 0)
                done(pe, "snew_ready", i)
                for b in range(B):
                    last = mm(pe, M[5][:, TP + b:TP + b + 1], snew[:, b, :], qr[:, TP + b:TP + b + 1], False, True, True)
                last.then_inc(sem("o_mm"), 1)
                project(pe, i, U_GB, 1)
                done(pe, "o_copy", i)
                mm(pe, M[0][:, 0:T], mean128[:], os_[:], True, True).then_inc(sem("omean_mm"), 1)
                done(pe, "o_sq", i)
                mm(pe, M[3][:, 0:T], mean128[:], osq[:], True, True).then_inc(sem("ovar_mm"), 1)

        wst = {"w": buf("wst_w", [P, P]), "ga": buf("wst_ga", [P, P]), "gb": buf("wst_gb", [LORA_G - P, P])}

        def act_pass(act, i, n):
            A = nc.scalar
            front, back = i is not None, n is not None

            def shifted(m, nm, use):
                done(act, f"proj{use}", i)
                A.activation(mshift[m][:, 1:TX + 1], pj[use % 2][:, 0:TX], ACT.Copy, scale=pt[:, PX["mu_" + nm]:PX["mu_" + nm] + 1]).then_inc(sem(f"mu_{nm}"), 1)

            if front:
                ci = bass.ts(i, P)
                last_pass(act, "g_copy", i)
                A.copy(wst["w"][:], lowa[:, ci])
                A.copy(wst["ga"][:], g2a[:, ci])
                A.copy(wst["gb"][:], g2b[:, ci]).then_inc(sem("stage_lora"), 1)
                done(act, "pt_ready", i)
                shifted(1, "k", U_RK)
            if back:
                for t in range(TT):
                    past(act, f"tok_mm{t}", n)
                    A.copy(rhs[:, 2 * t:2 * t + 2, 0, :], M[4 + t][:, 0:P].rearrange("p (h c) -> p h c", h=2))
                    A.copy(tmk[:, t], M[4 + t][:, P:4 * P].rearrange("p (n c) -> p n c", n=3)).then_inc(sem(f"tok_copy{t}"), 1)
            if front:
                done(act, "kk0_ready", i)
                A.activation(kks[:], kk0[:], ACT.Square).then_inc(sem("kk_sq"), 1)
                done(act, f"proj{U_W}", i)
                A.activation(thw[:], pj[1][:, 0:T], ACT.Tanh, scale=0.5, bias=pt[:, PX["w0h"]:PX["w0h"] + 1]).then_inc(sem("w_tanh"), 1)
                done(act, f"proj{U_A}", i)
                A.activation(tha[:], pj[0][:, 0:T], ACT.Tanh, scale=0.5, bias=pt[:, PX["a0h"]:PX["a0h"] + 1]).then_inc(sem("a_tanh"), 1)
                shifted(0, "r", U_R)
            if back:
                past(act, "a2_mm", n)
                A.copy(a2[:], v4(M[0])).then_inc(sem("a2_copy"), 1)
                past(act, "lakv_mm", n)
                A.copy(rhs[:, :, 1, :], M[4][:, 0:4 * HD].rearrange("p (u c) -> p u c", u=4)).then_inc(sem("rhs_ready"), 1)
                past(act, "at4w1_mm", n)
                for half in range(2):
                    last = A.copy(at4w[:, 2 * half:2 * half + 2, 0, :], M[2 + half][:].rearrange("p (u a c) -> p u a c", u=2, a=2)[:, :, 0, :])
                last.then_inc(sem("at4_copy"), 1)
                past(act, "a4_mm", n)
                A.copy(a4[:], v4(M[0])).then_inc(sem("a4_copy"), 1)
            if front:
                shifted(2, "v", U_RV)
            if back:
                past(act, "a8_mm", n)
                A.copy(a8[:], v4(M[5])).then_inc(sem("a8_copy"), 1)
            if front:
                done(act, f"proj{U_KK}", i)
                A.activation(kkn[:], pj[1][:, 0:T], ACT.Sqrt).then_inc(sem("kk_root"), 1)
                done(act, "lp_ready", i)
                A.activation(ep[:], lp[:], ACT.Exp)
                A.activation(en[:], lp[:], ACT.Exp, scale=-1.0)
                done(act, "lpx_ready", i)
                A.activation(epx[:], lpx[:], ACT.Exp).then_inc(sem("exp_ready"), 1)
            if back:
                past(act, "nt_mm", n)
                A.copy(nt[:], v4(M[3])).then_inc(sem("nt_copy"), 1)
            if front:
                done(act, f"proj{U_G}", i)
                A.copy(gg[:], pj[0][:, 0:T]).then_inc(sem("g_copy"), 1)
                done(act, f"proj{U_V}", i)
                A.copy(vr[:], pj[0][:, 0:T]).then_inc(sem("v_copy"), 1)
                done(act, f"proj{U_GS}", i)
                A.activation(thg[:], pj[1][:, 0:T], ACT.Tanh, scale=0.5).then_inc(sem("gs_tanh"), 1)
            if back:
                past(act, "y_mm", n)
                A.copy(ys[:, 0:TP], M[3][:, 0:TP]).then_inc(sem("y_copy"), 1)
                past(act, "zt_mm", n)
                act.wait_ge(sem("zout_free"), n)
                A.copy(zout[:], M[0][0:HD, 0:P].rearrange("p (h c) -> p h c", h=2)).then_inc(sem("zt_copy"), 1)
            if front:
                done(act, "kvt_mm", i)
                A.copy(kvt[:], v4(M[3])).then_inc(sem("kvt_copy"), 1)
                done(act, "kv8_mm", i)
                A.copy(ks8[:], M[0][0:B, 0:2 * P].rearrange("p (n c) -> p n c", n=2)).then_inc(sem("ks8_ready"), 1)
            if back:
                past(act, "yc_ready", n)
                A.activation(ysq[:, 0:TP], yc[:, 0:TP], ACT.Square).then_inc(sem("y_sq"), 1)
            if front:
                done(act, f"proj{U_GA}", i)
                A.activation(ga[:], pj[0][:, 0:T], ACT.Tanh, scale=0.5).then_inc(sem("ga_tanh"), 1)
            if back:
                past(act, "yvar_mm", n)
                A.activation(yrs[:, 0:TP], M[2][:, 0:TP], ACT.Sqrt, bias=eps[:, 1:2]).then_inc(sem("y_root"), 1)
            if front:
                done(act, "stp_mm", i)
                last_pass(act, "stp_sent", i * 16)
                A.copy(stp[:], M[4][:, 0:P]).then_inc(sem("stp_ready"), 1)
                done(act, "o_mm", i)
                A.copy(os_[:], M[5][:, 0:T]).then_inc(sem("o_copy"), 1)
                done(act, f"proj{U_GB}", i)
                A.activation(gb[:], pj[1][:, 0:T], ACT.Tanh, scale=0.5).then_inc(sem("gb_tanh"), 1)
                done(act, "oc_ready", i)
                A.activation(osq[:], oc[:], ACT.Square).then_inc(sem("o_sq"), 1)
                done(act, "ovar_mm", i)
                A.activation(ors[:], M[3][:, 0:T], ACT.Sqrt, bias=eps[:, 0:1]).then_inc(sem("o_root"), 1)

        def dve_pass(dve, i, n):
            V = nc.vector
            front, back = i is not None, n is not None
            c2 = "p (t c) -> p t c"

            def par(nm):
                return pt[:, PX[nm]:PX[nm] + 1]

            def self_wait(name):
                done(dve, name, i)

            def mix(m, nm, dst, use):
                done(dve, f"mu_{nm}", i)
                bank = pj[use % 2]
                V.scalar_tensor_tensor(out=dst[:, 0:TP], in0=bank[:, 0:TP], scalar=par("om_" + nm), in1=mshift[m][:, 0:TP], op0=mult, op1=add)
                V.scalar_tensor_tensor(out=dst[:, TP:T], in0=bank[:, TP:T], scalar=par("om_" + nm), in1=mshift[m][:, T + 1:TX + 1],
                                       op0=mult, op1=add).then_inc(sem(f"{nm}_mix"), 1)

            def rotary(nm, use, tabs, dst):
                done(dve, f"proj{use}", i)
                bank = pj[use % 2]
                hf = P // 2
                V.tensor_tensor(ta[:], bank[:, 0:T], rope[:, tabs[0], :], mult)
                V.tensor_tensor(tb[0:hf, :], bank[hf:P, 0:T], rope[hf:P, tabs[1], :], mult)
                V.tensor_tensor(tb[hf:P, :], bank[0:hf, 0:T], rope[0:hf, tabs[1], :], mult).then_inc(sem(f"{nm}_part"), 1)
                self_wait(f"{nm}_part")
                V.tensor_tensor(dst[:], ta[:], tb[:], add).then_inc(sem(f"{nm}_rope"), 1)

            if front:
                V.tensor_copy(pt[:], parc[:, :, bass.ds(i, 1)].rearrange("p n o -> p (n o)"))
                V.tensor_copy(dcol[:], retcol[:, bass.ds(i, 1), :].rearrange("p o n -> p (o n)")).then_inc(sem("pt_ready"), 1)
                self_wait("pt_ready")
                mix(1, "k", kx, U_RK)
                self_wait("k_mix")
                V.tensor_scalar(kk0[:], kx[:], par("k_k"), None, mult).then_inc(sem("kk0_ready"), 1)
            if back:
                for u in range(4):
                    past(dve, f"prod{u}", n)
                    last = V.tensor_tensor(pr[:, u], v4(M[u]), mk[:], mult)
                last.then_inc(sem("masked"), 1)
                for h in range(2):
                    past(dve, f"lmat{h}", n)
                    src = M[4 + h][:, 0:TP].rearrange("p (t c) -> p t c", t=TT)
                    for m in range(2):
                        last = V.tensor_tensor(la[:, h::2, m, :], src, mlo[:, m:m + 1, :].broadcast_to([P, TT, P]), mult)
                last.then_inc(sem("l_masked"), 1)
                past(dve, "masked", n)
                V.tensor_tensor(at2w[:, :, 1, :], pr[:, :, 0, :], ident[:].unsqueeze(1).broadcast_to([P, 4, P]), add).then_inc(sem("w0_ready"), 1)
            if front:
                done(dve, "w_tanh", i)
                V.tensor_scalar(thw[:], thw[:], LOGW_C, LOGW_C, mult, add).then_inc(sem("lw_ready"), 1)
                done(dve, "a_tanh", i)
                V.tensor_scalar(tha[:], tha[:], 0.5, 0.5, mult, add).then_inc(sem("a_ready"), 1)
            if back:
                past(dve, "at2_mm", n)
                V.tensor_copy(at2w[:, :, 0, :], v4(M[1])).then_inc(sem("at2_copy"), 1)
            if front:
                mix(0, "r", r, U_R)
                self_wait("lw_ready")
                V.tensor_tensor_scan(lp[:], scanm[:], thw[:], 0.0, mult, add).then_inc(sem("lp_ready"), 1)
                self_wait("a_ready")
                V.tensor_scalar(kmod[:], tha[:], par("k_a"), par("om_ka"), mult, add).then_inc(sem("km_part"), 1)
            if back:
                past(dve, "w0_ready", n)
                past(dve, "at4_copy", n)
                for half in range(2):
                    us = slice(2 * half, 2 * half + 2)
                    last = V.tensor_tensor(at4w[:, us, 1, :], M[2 + half][:].rearrange("p (u a c) -> p u a c", u=2, a=2)[:, :, 1, :], at2w[:, us, 1, :], add)
                last.then_inc(sem("w1_ready"), 1)
            if front:
                self_wait("km_part")
                V.tensor_tensor(kmod[:], kmod[:], kx[:], mult).then_inc(sem("kmod_ready"), 1)
                self_wait("lp_ready")
                V.tensor_tensor(lpx[:], lp[:], thw[:], sub).then_inc(sem("lpx_ready"), 1)
            if back:
                past(dve, "w2_mm", n)
                past(dve, "w1_ready", n)
                V.tensor_tensor(w2s[:], v4(M[1]), at4w[:, :, 1, :], add).then_inc(sem("w2_ready"), 1)
            if front:
                mix(2, "v", vx, U_RV)
                self_wait("kmod_ready")
                self_wait("r_mix")
                V.scalar_tensor_tensor(out=rkk[:], in0=r[:], scalar=par("r_k"), in1=kmod[:], op0=mult, op1=mult).then_inc(sem("rkk_ready"), 1)
            if back:
                past(dve, "w3_mm", n)
                past(dve, "w2_ready", n)
                V.tensor_tensor(w3[:], v4(M[2]), w2s[:], add).then_inc(sem("w3_ready"), 1)
            if front:
                done(dve, "kk_root", i)
                V.tensor_scalar(kkn[:], kkn[:], 1e-12, None, ALU.max).then_inc(sem("kk_max"), 1)
                self_wait("kk_max")
                V.reciprocal(kkn[:], kkn[:]).then_inc(sem("kk_inv"), 1)
            if back:
                past(dve, "x0_mm", n)
                V.tensor_copy(x0[:], v4(M[4])).then_inc(sem("x0_copy"), 1)
            if front:
                rotary("q", U_Q, (0, 1), qr)
            if back:
                past(dve, "x0_copy", n)
                past(dve, "z1_mm", n)
                V.tensor_tensor(z1[:], v4(M[5]), x0[:], add).then_inc(sem("z1_ready"), 1)
            if front:
                self_wait("q_rope")
                rotary("k", U_K, (2, 3), kr)
            if back:
                past(dve, "z2_mm", n)
                V.tensor_tensor(z2[:], v4(M[0]), x0[:], add).then_inc(sem("z2_ready"), 1)
            if front:
                self_wait("kk_inv")
                V.tensor_tensor(kk[:], kk0[:], kkn[:], mult).then_inc(sem("kk_norm"), 1)
                self_wait("kk_norm")
                V.tensor_tensor(ba[:], kk[:], tha[:], mult).then_inc(sem("ba_ready"), 1)
            if back:
                past(dve, "z3_mm", n)
                V.tensor_tensor(zf[:], v4(M[1]), x0[:], add).then_inc(sem("zf_ready"), 1)
            if front:
                done(dve, f"proj{U_BON}", i)
                self_wait("v_mix")
                V.tensor_tensor(bonus[:], pj[U_BON % 2][:, 0:T], vx[:], mult).then_inc(sem("bonus_sum"), 1)
            if back:
                past(dve, "q_mm", n)
                V.tensor_tensor(q[:].rearrange(c2, t=TT), M[2][:, 0:TP].rearrange(c2, t=TT), ar[:, :, 1, :], add).then_inc(sem("q_ready"), 1)
                for par_ in range(2):
                    past(dve, f"fg_mm{par_}", n)
                    last = V.tensor_tensor(fts[:, par_::2, :], M[4 + par_][:, 0:TP].rearrange("p (t a c) -> p t a c", t=TT, a=2)[:, :, 0, :],
                                           cst["c_id64"][:].unsqueeze(1).broadcast_to([P, TT, HD]), add)
                last.then_inc(sem("ft_ready"), 1)
            for c in range(NCH):
                if back:
                    if c:
                        past(dve, f"state_mm{c}", n)
                    t, par_ = c // 2, c % 2
                    V.tensor_scalar(zst[c][:], M[4 + par_][:, t * P + HD:(t + 1) * P], epc[:, c:c + 1], None, mult).then_inc(sem(f"state{c}"), 1)
                if front:
                    if c == 0:
                        self_wait("ba_ready")
                        done(dve, "exp_ready", i)
                        V.scalar_tensor_tensor(out=ar[:, :, 0, :], in0=kk[:, 0:TP].rearrange(c2, t=TT), scalar=-1.0,
                                               in1=epx[:, 0:TP].rearrange(c2, t=TT), op0=mult, op1=mult)
                    elif c == 1:
                        V.tensor_tensor(ar[:, :, 1, :], r[:, 0:TP].rearrange(c2, t=TT), ep[:, 0:TP].rearrange(c2, t=TT), mult)
                    elif c == 2:
                        V.tensor_tensor(bt[:], ba[:, 0:TP], en[:, 0:TP], mult)
                    else:
                        V.tensor_tensor(kt[:], kmod[:, 0:TP], en[:, 0:TP], mult).then_inc(sem("abkr_ready"), 1)
            if front:
                done(dve, "sc_mm", i)
                V.tensor_tensor(sc[:], M[4][:, 0:TP + P], retdec[:, bass.ds(i, 1), :].rearrange("p o n -> p (o n)"), mult).then_inc(sem("sc_ready"), 1)
            if back:
                past(dve, "ymean_mm", n)
                V.tensor_tensor(yc[:, 0:TP], ys[:, 0:TP], M[1][:, 0:TP], sub).then_inc(sem("yc_ready"), 1)
            if front:
                done(dve, "kvt_copy", i)
                V.tensor_scalar(vd[:, 0, :], kvt[:, 2, :], dcol[:, 0:1], None, mult)
                V.tensor_scalar(vd[:, 1, :], kvt[:, 3, :], dcol[:, 1:2], None, mult).then_inc(sem("vd_ready"), 1)
                done(dve, "ks8_ready", i)
                V.tensor_tensor(vdiag[:], ks8[:, 1:2, :].broadcast_to([B, B, P]), diag8[:], mult).then_inc(sem("vdiag_ready"), 1)
                done(dve, "gs_tanh", i)
                V.scalar_tensor_tensor(out=sg[:], in0=thg[:], scalar=1.0, in1=pj[U_GS % 2][:, 0:T], op0=add, op1=mult).then_inc(sem("gs_silu"), 1)
            if back:
                past(dve, "y_root", n)
                V.reciprocal(yrs[:, 0:TP], yrs[:, 0:TP]).then_inc(sem("y_inv"), 1)
            if front:
                dve.wait_ge(sem("sin_in"), 16 * (i + 1))
                last_pass(dve, "snew_sent", 16 * i)
                done(dve, "kv_mm", i)
                for half, bank in enumerate((M[0], M[3])):
                    bs = slice(4 * half, 4 * half + 4)
                    last = V.scalar_tensor_tensor(out=snew[:, bs, :], in0=sin_[:, bs, :], scalar=dcol[:, 2:3], in1=v4(bank), op0=mult, op1=add)
                last.then_inc(sem("snew_ready"), 1)
                for m, src in enumerate((r, ep, kmod, vx, kk, ba)):
                    V.tensor_copy(svec[:, bass.ds(i, 1), m, :].rearrange("p o b -> p (o b)"), src[:, TP:T])
            if back:
                past(dve, "y_inv", n)
                V.tensor_tensor(yc[:, 0:TP], yc[:, 0:TP], yrs[:, 0:TP], mult).then_inc(sem("yn"), 1)
                past(dve, "yn", n)
                V.tensor_tensor(yc[:, 0:TP], yc[:, 0:TP], ygate[:], mult).then_inc(sem("yln"), 1)
                past(dve, "yln", n)
                V.tensor_tensor(yc[:, 0:TP], yc[:, 0:TP], ybias[:], add).then_inc(sem("rwkv_out"), 1)
                past(dve, "rwkv_out", n)
                tile = merged[:, bass.ds(n - 1, 1), 0:TP].rearrange("p o t -> p (o t)")
                V.tensor_tensor(tile, tile, yc[:, 0:TP], add)
            if front:
                if back:
                    past(dve, f"state{NCH - 1}", n)
                V.tensor_copy(epc[:], ep[:, C - 1:TP:C])
                done(dve, "gb_tanh", i)
                V.tensor_scalar(ga[:], ga[:], 0.25, 0.25, mult, add)
                V.tensor_scalar(gb[:], gb[:], 0.5, 0.5, mult, add).then_inc(sem("gates_ready"), 1)
                self_wait("gates_ready")
                self_wait("gs_silu")
                V.scalar_tensor_tensor(out=sg[:], in0=sg[:], scalar=par("gn_w"), in1=ga[:], op0=mult, op1=mult).then_inc(sem("retgate_ready"), 1)
                V.tensor_tensor(gg[:], gg[:], gb[:], mult).then_inc(sem("rgate_ready"), 1)
                done(dve, "omean_mm", i)
                V.tensor_tensor(oc[:], os_[:], M[0][:, 0:T], sub).then_inc(sem("oc_ready"), 1)
                self_wait("rgate_ready")
                self_wait("bonus_sum")
                V.tensor_scalar(ygate[:], gg[:, 0:TP], par("lnx_w"), None, mult)
                V.scalar_tensor_tensor(out=ybias[:], in0=bonus[:, 0:TP], scalar=par("lnx_b"), in1=gg[:, 0:TP], op0=add, op1=mult).then_inc(sem("ygate_ready"), 1)
                V.tensor_copy(spost[:, 0, bass.ds(i, 1), :].rearrange("p o b -> p (o b)"), bonus[:, TP:T])
                V.tensor_copy(spost[:, 1, bass.ds(i, 1), :].rearrange("p o b -> p (o b)"), gg[:, TP:T])
                done(dve, "o_root", i)
                V.reciprocal(ors[:], ors[:]).then_inc(sem("o_inv"), 1)
                self_wait("o_inv")
                V.tensor_tensor(oc[:], oc[:], ors[:], mult).then_inc(sem("on"), 1)
                self_wait("on")
                V.tensor_tensor(merged[:, bass.ds(i, 1), 0:TP].rearrange("p o t -> p (o t)"), oc[:, 0:TP], sg[:, 0:TP], mult)
                V.tensor_tensor(spost[:, 2, bass.ds(i, 1), :].rearrange("p o b -> p (o b)"), oc[:, TP:T], sg[:, TP:T], mult).then_inc(sem("ret_out"), 1)

        def sp_pass(sp, i):
            for use, s in slot_of.items():
                settle(sp)
                last_pass(sp, f"proj{use}", i)
                off = {U_RK: O_RK, U_R: O_R, U_RV: O_RV, U_Q: O_Q, U_K: O_K, U_V: O_V, U_GS: O_GS, U_GA: O_GA, U_GB: O_GB}[use]
                sp.dma_start(wslot[s][:], w_in[:, :, bass.ds(i * P + off, P)]).then_inc(sem(f"w_in{s}"), 16)
            last_pass(sp, "snew_ready", i)
            sp.dma_start(sin_[:], a["state_ret"][0].rearrange("b h k v -> k h b v")[:, bass.ds(i, 1), :, :].rearrange("k o b v -> k (o b) v")).then_inc(sem("sin_in"), 16)

        def out_pass(eng, i, n):
            if n is not None:
                settle(eng)
                past(eng, "zt_copy", n)
                eng.dma_start(o["rwkv_p"][0, 0].rearrange("h v k -> v h k")[:, bass.ds(n * 2 - 2, 2), :], zout[:]).then_inc(sem("zout_sent"), 16)
                eng.wait_ge(sem("zout_sent"), 16 * n)
                eng.sem_inc(sem("zout_free"), 1)
            if i is not None:
                settle(eng)
                done(eng, "stp_ready", i)
                eng.dma_start(o["ret_p"][0, 0][bass.ds(i, 1)].rearrange("o k v -> (o k) v"), stp[:]).then_inc(sem("stp_sent"), 16)
                settle(eng)
                done(eng, "snew_ready", i)
                eng.dma_start(o["ret_s"][0].rearrange("b h k v -> k h b v")[:, bass.ds(i, 1), :, :].rearrange("k o b v -> k (o b) v"), snew[:]).then_inc(sem("snew_sent"), 16)

        with nc.Block() as block:

            @block.sync
            def _(sp):
                sp_pass(sp, 0)
                with sp.Fori(1, KT) as i:
                    sp_pass(sp, i)

            @block.gpsimd
            def _(pool):
                for m in mshift:
                    last = nc.gpsimd.memset(m[:, 0:1], 0.0)
                last.then_inc(sem("mshift_zero"), 1)
                pool.sem_inc(sem("zout_free"), 1)
                out_pass(pool, 0, None)
                with pool.Fori(1, KT) as i:
                    out_pass(pool, i, i)
                out_pass(pool, None, KT)
                for nm in ("stp_sent", "snew_sent"):
                    pool.wait_ge(sem(nm), 16 * KT)
                pool.wait_ge(sem("zout_free"), KT + 1)

            @block.scalar
            def _(act):
                act_pass(act, 0, None)
                with act.Fori(1, KT) as i:
                    act_pass(act, i, i)
                act_pass(act, None, KT)

            @block.vector
            def _(dve):
                dve.wait_ge(sem("mshift_zero"), 1)
                dve_pass(dve, 0, None)
                with dve.Fori(1, KT) as i:
                    dve_pass(dve, i, i)
                dve_pass(dve, None, KT)

            @block.tensor
            def _(pe):
                pe_pass(pe, 0, None, wst)
                with pe.Fori(1, KT) as i:
                    pe_pass(pe, i, i, wst)
                pe_pass(pe, None, KT, wst)


def sample_phase(nc, a, o, k, alloc, sem, psum, cst, keep):
    mult, add, sub = ALU.mult, ALU.add, ALU.subtract
    with ExitStack() as ctx:
        sb = {}

        def buf(name, shape):
            return alloc(ctx, sb, name, shape)

        ident, mean64 = cst["c_ident"], cst["c_mean64"]
        merged, svec, spost, parc, eps = (keep[n] for n in ("merged", "svec", "spost", "parc", "eps"))
        NV = 6 * B
        st = buf("st", [P, HD, HD])
        vk = buf("vk", [P, HD, HD])
        prod = buf("prod", [P, HD, HD])
        stok = buf("stok", [NV, D])
        vec = buf("vec", [P, 6, HD])
        sa, y1 = buf("sa", [P, HD]), buf("y1", [P, HD])
        ytok = buf("ytok", [B, D])
        sy, syc, sysq, syr = (buf(n, [P, KT, B]) for n in ("sy", "syc", "sysq", "syr"))
        scr_vec = nc.dram_tensor("scr_vec", [NV, D], F32, kind="Internal").ap()
        scr_y = nc.dram_tensor("scr_y", [P, HD], F32, kind="Internal").ap()

        with nc.Block() as block:

            @block.sync
            def _(sp):
                sp.dma_start(st[:].rearrange("p v k -> p (v k)"), a["state_rwkv"][0].rearrange("b h v k -> (b h) (v k)")).then_inc(sem("st_in"), 16)
                sp.wait_ge(sem("stok_ready"), 2)
                sp.dma_start(scr_vec, stok[:]).then_inc(sem("scr_vec_in"), 16)
                sp.wait_ge(sem("scr_vec_in"), 16)
                sp.dma_start(vec[:], scr_vec.rearrange("(v b) (h c) -> (b h) v c", b=B, c=HD)).then_inc(sem("vec_in"), 16)
                sp.wait_ge(sem("state_new"), 1)
                sp.dma_start(o["rwkv_s"][0].rearrange("b h v k -> (b h) (v k)"), st[:].rearrange("p v k -> p (v k)")).then_inc(sem("rwkv_s_out"), 16)
                sp.wait_ge(sem("y1_ready"), 1)
                sp.dma_start(scr_y, y1[:]).then_inc(sem("scr_y_in"), 16)
                sp.wait_ge(sem("scr_y_in"), 16)
                sp.dma_start(ytok[:], scr_y.rearrange("(b h) c -> b (h c)", b=B)).then_inc(sem("ytok_in"), 16)
                sp.wait_ge(sem("rwkv_s_out"), 16)
                sp.wait_ge(sem("ytok_in"), 16)

            @block.tensor
            def _(pe):
                for kk in range(KT):
                    last = nc.tensor.transpose(psum[kk // 4][0:NV, (kk % 4) * P:(kk % 4 + 1) * P], svec[:, kk].rearrange("p v b -> p (v b)"), ident[:])
                    if kk % 4 == 3:
                        last.then_inc(sem("sv_mm"), 1)
                pe.wait_ge(sem("ytok_in"), 16)
                for kk in range(KT):
                    last = nc.tensor.transpose(psum[2][:, kk * B:(kk + 1) * B], ytok[:, kk * P:(kk + 1) * P], ident[0:B, 0:B])
                last.then_inc(sem("sy_mm"), 1)
                pe.wait_ge(sem("sy_ready"), 1)
                nc.tensor.matmul(psum[3][:, 0:KT * B], mean64[:], sy[:].rearrange("p k b -> p (k b)"), start=True, stop=True).then_inc(sem("symean"), 1)
                pe.wait_ge(sem("sysq_ready"), 1)
                nc.tensor.matmul(psum[4][:, 0:KT * B], mean64[:], sysq[:].rearrange("p k b -> p (k b)"), start=True, stop=True).then_inc(sem("syvar"), 1)

            @block.gpsimd
            def _(pool):
                pool.wait_ge(sem("vec_in"), 16)
                nc.gpsimd.tensor_tensor(vk[:], vec[:, 3, :].unsqueeze(2).broadcast_to([P, HD, HD]),
                                        vec[:, 2, :].unsqueeze(1).broadcast_to([P, HD, HD]), mult).then_inc(sem("vk_ready"), 1)

            @block.scalar
            def _(act):
                act.wait_ge(sem("sv_mm"), 1)
                nc.scalar.copy(stok[:, 0:512], psum[0][0:NV, :]).then_inc(sem("stok_ready"), 1)
                act.wait_ge(sem("sy_mm"), 1)
                nc.scalar.copy(sy[:].rearrange("p k b -> p (k b)"), psum[2][:, 0:KT * B]).then_inc(sem("sy_ready"), 1)
                act.wait_ge(sem("syc_ready"), 1)
                nc.scalar.activation(sysq[:], syc[:], ACT.Square).then_inc(sem("sysq_ready"), 1)
                act.wait_ge(sem("syvar"), 1)
                nc.scalar.activation(syr[:].rearrange("p k b -> p (k b)"), psum[4][:, 0:KT * B], ACT.Sqrt, bias=eps[:, 1:2]).then_inc(sem("syroot"), 1)

            @block.vector
            def _(dve):
                V = nc.vector

                def key(n):
                    return vec[:, n, :].unsqueeze(1).broadcast_to([P, HD, HD])

                step = [0]

                def then(ins):
                    step[0] += 1
                    ins.then_inc(sem("sample_step"), 1)
                    dve.wait_ge(sem("sample_step"), step[0])

                dve.wait_ge(sem("sv_mm"), 2)
                V.tensor_copy(stok[:, 512:1024], psum[1][0:NV, :]).then_inc(sem("stok_ready"), 1)
                dve.wait_ge(sem("st_in"), 16)
                dve.wait_ge(sem("vec_in"), 16)
                then(V.tensor_tensor(prod[:], st[:], key(4), mult))
                V.tensor_reduce(sa[:], prod[:], AX_X, add)
                then(V.tensor_tensor(st[:], st[:], key(1), mult))
                then(V.tensor_tensor(prod[:], sa[:].unsqueeze(2).broadcast_to([P, HD, HD]), key(5), mult))
                then(V.tensor_tensor(st[:], st[:], prod[:], sub))
                dve.wait_ge(sem("vk_ready"), 1)
                V.tensor_tensor(st[:], st[:], vk[:], add).then_inc(sem("state_new"), 1)
                dve.wait_ge(sem("state_new"), 1)
                then(V.tensor_tensor(prod[:], st[:], key(0), mult))
                V.tensor_reduce(y1[:], prod[:], AX_X, add).then_inc(sem("y1_ready"), 1)
                dve.wait_ge(sem("symean"), 1)
                V.tensor_tensor(syc[:].rearrange("p k b -> p (k b)"), sy[:].rearrange("p k b -> p (k b)"), psum[3][:, 0:KT * B], sub).then_inc(sem("syc_ready"), 1)
                dve.wait_ge(sem("syroot"), 1)
                then(V.reciprocal(syr[:], syr[:]))
                then(V.tensor_tensor(syc[:], syc[:], syr[:], mult))

                def chan(n):
                    return parc[:, PX[n], :].unsqueeze(2).broadcast_to([P, KT, B])

                then(V.tensor_tensor(syc[:], syc[:], chan("lnx_w"), mult))
                then(V.tensor_tensor(syc[:], syc[:], chan("lnx_b"), add))
                then(V.tensor_tensor(syc[:], syc[:], spost[:, 0], add))
                then(V.tensor_tensor(syc[:], syc[:], spost[:, 1], mult))
                V.tensor_tensor(merged[:, :, TP:T], syc[:], spost[:, 2], add).then_inc(sem("merged_all"), 1)


def moe_phase(nc, a, o, k, alloc, sem, psum, cst, keep):
    mult, add, sub = ALU.mult, ALU.add, ALU.subtract
    SIZE = [P, P, B]
    with ExitStack() as ctx:
        sb = {}

        def buf(name, shape, dt=F32):
            return alloc(ctx, sb, name, shape, dt)

        ident, tri, ones, slot = (cst["c_" + n] for n in ("ident", "tri", "ones", "slot"))
        merged, gbc, eps = keep["merged"], keep["gbc"], keep["eps"]
        RING = 4
        wg = [buf(f"wg{n}", [P, KT, DE]) for n in range(RING)]
        wu = [buf(f"wu{n}", [P, KT, DE]) for n in range(RING)]
        wd = [buf(f"wd{n}", [P, DE // P, D]) for n in range(RING)]
        wout = [wg[3], wu[3], wd[3], wg[2]]
        x = buf("x", [P, 3, D])
        xn = buf("xn", [P, 3, D])
        xnt = buf("xnt", [P, KT, T])
        stat = buf("mstat", [P, 3, 4])
        rw = buf("rw", [P, KT, NG + NE])
        rb = buf("rb", [P, NG + NE])
        lg = buf("lg", [P, 3, NG + NE])
        gpad = buf("gpad", [P, 3, 8])
        top, topi, topf = buf("topv", [P, 3, 8]), buf("topi", [P, 3, 8], mybir.dt.uint32), buf("topf", [P, 3, 8])
        gmask = buf("gmask", [P, 3, NG])
        gexp, gsum = buf("gexp", [P, 3, NG]), buf("gsum", [P, 3, 4])
        esel, eprod = buf("esel", [P, 3, 8]), buf("eprod", [P, 3, 8, NG])
        tw = buf("tw", [P, 3, 4])
        c8, c8b = buf("c8", [P, 3, 8]), buf("c8b", [P, 3, 8])
        comb = buf("comb", [P, 3, NG, EPG])
        pos = buf("pos", [P, 3, NG])
        cnt = buf("cnt", [P, 4])
        rounds_i = buf("rounds_i", [P, 1], I32)
        pcol, mcol, cg = buf("pcol", [P, 3]), buf("mcol", [P, 3]), buf("cg", [P, 3, EPG])
        G = buf("G", [P, 3, SLOTS])
        GT = buf("GT", [SLOTS, T])
        xg, cb = buf("xg", [P, KT, SLOTS]), buf("cb", [P, EPG, SLOTS])
        th = [buf(f"th{n}", [P, 2, SLOTS]) for n in range(2)]
        hs = [buf(f"hs{n}", [P, 2, SLOTS]) for n in range(2)]
        h = [buf(f"h{n}", [P, 2, SLOTS]) for n in range(2)]
        ysb, yt = buf("ysb", [P, KT, SLOTS]), buf("yt", [SLOTS, D])
        gfin = buf("gfin", [P, D])
        junk = buf("junk", [P, D])
        buf("zeros", [P, 4 * SLOTS])
        hold = buf("hold", [P, 1])
        MB = [psum[4], psum[5]]
        YB = [psum[6], psum[7]]

        def rows(tt):
            return slice(0, SIZE[tt])

        def cols(tt):
            return slice(tt * P, tt * P + SIZE[tt])

        with nc.Block() as block:

            def settle(eng):
                eng.wait_ge(sem("rounds_ready"), 1)

            def load_expert(sp, s, e, n):
                sp.wait_ge(sem(f"slot_free{s}"), n + 1)
                ew = [a[nm][0][bass.ds(e, 1)] for nm in ("expert_w_gate", "expert_w_up", "expert_w_down")]
                sp.dma_start(wg[s][:], ew[0].rearrange("o (k p) f -> p (o k) f", p=P)).then_inc(sem(f"expert_in{s}"), 16)
                sp.dma_start(wu[s][:], ew[1].rearrange("o (k p) f -> p (o k) f", p=P)).then_inc(sem(f"expert_in{s}"), 16)
                sp.dma_start(wd[s][:], ew[2].rearrange("o (k p) f -> p (o k) f", p=P)).then_inc(sem(f"expert_in{s}"), 16)

            @block.sync
            def _(sp):
                sp.dma_start(x[:, 0:2, :], a["x_prompt"][0].rearrange("(t p) d -> p t d", p=P)).then_inc(sem("x2_in"), 16)
                sp.dma_start(x[0:B, 2, :], a["x_sample"].rearrange("b t d -> (b t) d")).then_inc(sem("x2_in"), 16)
                wo = a["w_out"][0].rearrange("(k p) c -> p k c", p=P)
                for n in range(4):
                    sp.dma_start(wout[n][:].rearrange("p a b -> p (a b)").rearrange("p (k c) -> p k c", k=2), wo[:, 2 * n:2 * n + 2, :]).then_inc(sem("wout_in"), 16)
                sp.dma_start(gbc[:], a["norm_ffn"].partition_broadcast(P)).then_inc(sem("gffn_in"), 16)
                sp.dma_start(gfin[:], a["norm_final"].rearrange("(o d) -> o d", o=1).partition_broadcast(P)).then_inc(sem("gfin_in"), 16)
                sp.dma_start(rw[:, :, 0:NG], a["router_group_w"][0].rearrange("(k p) c -> p k c", p=P)).then_inc(sem("rw_in"), 16)
                sp.dma_start(rw[:, :, NG:NG + NE], a["router_expert_w"][0].rearrange("(k p) c -> p k c", p=P)).then_inc(sem("rw_in"), 16)
                sp.dma_start(rb[:, 0:NG], a["router_group_b"].partition_broadcast(P)).then_inc(sem("rw_in"), 16)
                sp.dma_start(rb[:, NG:NG + NE], a["router_expert_b"].partition_broadcast(P)).then_inc(sem("rw_in"), 16)
                with sp.Fori(0, NE // RING) as quad:
                    for s in range(RING):
                        load_expert(sp, s, quad * RING + s, quad)
                sp.wait_ge(sem("rounds_ready"), 1)
                n_rounds = sp.value_load(rounds_i[0:1, 0:1], min_val=1, max_val=3)
                with sp.If(n_rounds > 1):
                    with sp.Fori(1, n_rounds) as rnd:
                        with sp.Fori(0, NE // RING) as quad:
                            for s in range(RING):
                                load_expert(sp, s, quad * RING + s, rnd * (NE // RING) + quad)
                sp.wait_ge(sem("y_final"), 1)
                sp.dma_start(o["y_p"][0].rearrange("(t p) d -> p t d", p=P), xn[:, 0:2, :]).then_inc(sem("y_sent"), 16)
                sp.dma_start(o["y_s"].rearrange("b t d -> (b t) d"), xn[0:B, 2, :]).then_inc(sem("y_sent"), 16)
                sp.wait_ge(sem("y_sent"), 32)

            def loop(eng, group_pre, expert, group_post, round_end=None):
                eng.wait_ge(sem("rounds_ready"), 1)
                n_rounds = eng.value_load(rounds_i[0:1, 0:1], min_val=1, max_val=3)
                with eng.Fori(0, n_rounds) as rnd:
                    with eng.Fori(0, NG) as g:
                        n = rnd * NG + g
                        group_pre(g, n)
                        with eng.Fori(0, EPG // RING) as half:
                            q = n * (EPG // RING) + half
                            expert(half, q)
                        group_post(g, n)
                    if round_end:
                        round_end(rnd)

            @block.tensor
            def _(pe):
                mm = nc.tensor.matmul

                def loose(out, lhsT, rhs, start, stop):
                    return nc.tensor.matmul(out, lhsT, rhs, start=start, stop=stop, skip_group_check=True)

                pe.wait_ge(sem("wout_in"), 64)
                for tt in range(3):
                    for hf in range(2):
                        for kk in range(KT):
                            w = wout[kk // 2][:].rearrange("p a b -> p (a b)")[:, (kk % 2) * D + hf * 512:(kk % 2) * D + hf * 512 + 512]
                            last = mm(psum[2 * tt + hf][rows(tt), :], merged[:, kk, cols(tt)], w, start=(kk == 0), stop=(kk == KT - 1))
                    last.then_inc(sem("wo_mm"), 1)
                for tt in range(3):
                    pe.wait_ge(sem("xn2_ready"), tt + 1)
                for kk in range(KT):
                    if kk >= 2:
                        pe.wait_ge(sem("xnt_copy"), kk - 1)
                    for tt in range(3):
                        last = nc.tensor.transpose(psum[6 + kk % 2][:, cols(tt)], xn[rows(tt), tt, kk * P:(kk + 1) * P], ident[rows(tt), rows(tt)])
                    last.then_inc(sem("xnt_mm"), 1)
                pe.wait_ge(sem("xnt_copy"), KT)
                pe.wait_ge(sem("rw_in"), 64)
                for tt in range(3):
                    for kk in range(KT):
                        last = mm(psum[0][rows(tt), tt * 64:tt * 64 + NG + NE], xnt[:, kk, cols(tt)], rw[:, kk, :], start=(kk == 0), stop=(kk == KT - 1))
                last.then_inc(sem("logit_mm"), 1)
                pe.wait_ge(sem("gmask_ready"), 1)
                for tt in range(3):
                    m = SIZE[tt]
                    for u in range(tt):
                        mm(psum[1][0:m, tt * NG:(tt + 1) * NG], ones[:, 0:m], gmask[:, u, :], start=(u == 0), stop=False)
                    mm(psum[1][0:m, tt * NG:(tt + 1) * NG], tri[0:m, 0:m], gmask[0:m, tt, :], start=(tt == 0), stop=True)
                for tt in range(3):
                    last = mm(psum[1][:, 16:16 + NG], ones[rows(tt), :], gmask[rows(tt), tt, :], start=(tt == 0), stop=(tt == 2))
                last.then_inc(sem("pos_mm"), 1)

                def group_pre(g, n):
                    pe.wait_ge(sem("G_ready"), n + 1)
                    pe.wait_ge(sem("bank_free"), n + 1)
                    for kk in range(KT):
                        for tt in range(3):
                            last = mm(psum[kk // 4][:, (kk % 4) * SLOTS:(kk % 4 + 1) * SLOTS], xn[rows(tt), tt, kk * P:(kk + 1) * P],
                                      G[rows(tt), tt, :], start=(tt == 0), stop=(tt == 2))
                    last.then_inc(sem("xg_mm"), 1)
                    for e in range(EPG):
                        for tt in range(3):
                            last = mm(psum[2 + e // 4][:, (e % 4) * SLOTS:(e % 4 + 1) * SLOTS], cg[rows(tt), tt, e:e + 1].broadcast_to([SIZE[tt], P]),
                                      G[rows(tt), tt, :], start=(tt == 0), stop=(tt == 2))
                    last.then_inc(sem("cb_mm"), 1)
                    pe.wait_ge(sem("xg_copy"), 2 * n + 2)
                    for tt in range(3):
                        last = nc.tensor.transpose(psum[0][0:SLOTS, cols(tt)], G[rows(tt), tt, :], ident[rows(tt), rows(tt)])
                    last.then_inc(sem("gt_mm"), 1)

                def gate_up(s, q):
                    b = MB[s % 2]
                    pe.wait_ge(sem(f"expert_in{s}"), 48 * (q + 1))
                    pe.wait_ge(sem(f"h_bank{s % 2}"), q * 2 + s // 2 + 1)
                    for f in range(4):
                        w = wg[s] if f < 2 else wu[s]
                        for kk in range(KT):
                            last = mm(b[:, f * SLOTS:(f + 1) * SLOTS], w[:, kk, (f % 2) * P:(f % 2 + 1) * P], xg[:, kk, :], start=(kk == 0), stop=(kk == KT - 1))
                    last.then_inc(sem(f"gu_mm{s % 2}"), 1)

                def down(s, q, half):
                    pe.wait_ge(sem(f"h_ready{s % 2}"), q * 2 + s // 2 + 1)
                    for kk in range(KT):
                        for f in range(2):
                            last = loose(YB[kk // 4][:, (kk % 4) * SLOTS:(kk % 4 + 1) * SLOTS], wd[s][:, f, kk * P:(kk + 1) * P], h[s % 2][:, f, :], False, True)
                    last.then_inc(sem(f"slot_free{s}"), 1)
                    return last

                def expert(half, q):
                    gate_up(0, q)
                    gate_up(1, q)
                    down(0, q, half)
                    gate_up(2, q)
                    down(1, q, half)
                    gate_up(3, q)
                    down(2, q, half)
                    down(3, q, half)

                def group_clear(g, n):
                    group_pre(g, n)
                    for b in range(2):
                        loose(YB[b][:, 0:4 * SLOTS], zeros[:, 0:P], zeros[:, 0:4 * SLOTS], True, False)

                def group_post(g, n):
                    loose(YB[1][:, 0:4 * SLOTS], zeros[:, 0:P], zeros[:, 0:4 * SLOTS], False, True).then_inc(sem("ysum_mm"), 1)
                    pe.wait_ge(sem("ysb_copy"), 2 * n + 2)
                    for kk in range(KT):
                        last = nc.tensor.transpose(psum[2 + kk // 4][0:SLOTS, (kk % 4) * P:(kk % 4 + 1) * P], ysb[:, kk, :], ident[:])
                    last.then_inc(sem("yt_mm"), 1)
                    pe.wait_ge(sem("yt_copy"), 2 * n + 2)
                    for tt in range(3):
                        for hf in range(2):
                            bank = psum[(2 * tt + hf) % 4]
                            if tt == 2:
                                pe.wait_ge(sem("scat_add"), n * 6 + hf + 1)
                            mm(bank[rows(tt), :], GT[:, cols(tt)], yt[:, hf * 512:(hf + 1) * 512], start=True, stop=True).then_inc(sem("scat_mm"), 1)

                zeros = sb["zeros"]
                loop(pe, group_clear, expert, group_post)

            @block.scalar
            def _(act):
                A = nc.scalar
                for tt in range(3):
                    act.wait_ge(sem("x1_ready"), tt + 1)
                    if tt:
                        act.wait_ge(sem("x1_sq"), tt)
                    A.activation(junk[rows(tt), :], x[rows(tt), tt, :], ACT.Square, accum_out=stat[rows(tt), tt, 0:1]).then_inc(sem("x1_sq"), 1)
                act.wait_ge(sem("x1_sq"), 3)
                A.activation(stat[:, :, 1:2], stat[:, :, 0:1], ACT.Sqrt, scale=1.0 / D, bias=eps[:, 2:3]).then_inc(sem("x1_root"), 1)
                for kk in range(0, KT, 2):
                    act.wait_ge(sem("xnt_mm"), kk + 1)
                    if kk:
                        act.wait_ge(sem("xnt_copy"), kk)
                    A.copy(xnt[:, kk, :], psum[6 + kk % 2][:, 0:T]).then_inc(sem("xnt_copy"), 1)
                act.wait_ge(sem("gdiff_ready"), 1)
                A.activation(gexp[:], gexp[:], ACT.Exp).then_inc(sem("gexp_ready"), 1)
                act.wait_ge(sem("ediff_ready"), 1)
                A.activation(tw[:, :, 1:2], tw[:, :, 0:1], ACT.Exp).then_inc(sem("eexp_ready"), 1)

                def group_pre(g, n):
                    act.wait_ge(sem("xg_mm"), n + 1)
                    A.copy(xg[:, 0:4, :], psum[0][:, 0:4 * SLOTS].rearrange("p (k s) -> p k s", k=4)).then_inc(sem("xg_copy"), 1)
                    act.wait_ge(sem("cb_mm"), n + 1)
                    A.copy(cb[:, 0:4, :], psum[2][:, 0:4 * SLOTS].rearrange("p (k s) -> p k s", k=4)).then_inc(sem("cb_copy"), 1)
                    act.wait_ge(sem("gt_mm"), n + 1)
                    A.copy(GT[:], psum[0][0:SLOTS, 0:T]).then_inc(sem("gt_copy"), 1)

                def expert(half, q):
                    for s in range(RING):
                        p = s % 2
                        act.wait_ge(sem(f"gu_mm{p}"), q * 2 + s // 2 + 1)
                        act.wait_ge(sem(f"h_bank{p}"), q * 2 + s // 2 + 1)
                        A.activation(th[p][:], MB[p][:, 0:2 * SLOTS].rearrange("p (f s) -> p f s", f=2), ACT.Tanh, scale=0.5).then_inc(sem(f"th_ready{p}"), 1)

                def group_post(g, n):
                    act.wait_ge(sem("ysum_mm"), n + 1)
                    A.copy(ysb[:, 0:4, :], YB[0][:, 0:4 * SLOTS].rearrange("p (k s) -> p k s", k=4)).then_inc(sem("ysb_copy"), 1)
                    act.wait_ge(sem("yt_mm"), n + 1)
                    A.copy(yt[:, 0:512], psum[2][0:SLOTS, :]).then_inc(sem("yt_copy"), 1)

                loop(act, group_pre, expert, group_post)
                act.wait_ge(sem("moe_done"), 1)
                for tt in range(3):
                    if tt:
                        act.wait_ge(sem("x2_sq"), tt)
                    A.activation(junk[rows(tt), :], x[rows(tt), tt, :], ACT.Square, accum_out=stat[rows(tt), tt, 0:1]).then_inc(sem("x2_sq"), 1)
                act.wait_ge(sem("x2_sq"), 3)
                A.activation(stat[:, :, 1:2], stat[:, :, 0:1], ACT.Sqrt, scale=1.0 / D, bias=eps[:, 2:3]).then_inc(sem("x2_root"), 1)

            @block.vector
            def _(dve):
                V = nc.vector
                step = [0]

                def then(ins):
                    step[0] += 1
                    ins.then_inc(sem("router_step"), 1)
                    dve.wait_ge(sem("router_step"), step[0])

                V.memset(sb["zeros"][:], 0.0)
                V.memset(stat[:], 1.0)
                V.memset(gmask[:], 0.0)
                V.memset(cg[:], 0.0)
                V.memset(lg[:], 0.0)
                V.memset(gpad[:], -3.0e38)
                for s in range(2):
                    dve.sem_inc(sem(f"slot_free{s}"), 1)
                    dve.sem_inc(sem(f"h_bank{s}"), 1)
                dve.wait_ge(sem("x2_in"), 32)
                for tt in range(3):
                    dve.wait_ge(sem("wo_mm"), tt + 1)
                    for hf in range(2):
                        hc = slice(hf * 512, (hf + 1) * 512)
                        last = V.tensor_tensor(x[rows(tt), tt, hc], x[rows(tt), tt, hc], psum[2 * tt + hf][rows(tt), :], add)
                    last.then_inc(sem("x1_ready"), 1)
                for s in (2, 3):
                    dve.sem_inc(sem(f"slot_free{s}"), 1)
                dve.wait_ge(sem("x1_root"), 1)
                then(V.reciprocal(stat[:, :, 2:3], stat[:, :, 1:2]))
                dve.wait_ge(sem("gffn_in"), 16)
                for tt in range(3):
                    V.scalar_tensor_tensor(out=xn[rows(tt), tt, :], in0=x[rows(tt), tt, :], scalar=stat[rows(tt), tt, 2:3],
                                           in1=gbc[rows(tt), :], op0=mult, op1=mult).then_inc(sem("xn2_ready"), 1)
                for kk in range(1, KT, 2):
                    dve.wait_ge(sem("xnt_mm"), kk + 1)
                    dve.wait_ge(sem("xnt_copy"), kk)
                    V.tensor_copy(xnt[:, kk, :], psum[6 + kk % 2][:, 0:T]).then_inc(sem("xnt_copy"), 1)
                dve.wait_ge(sem("logit_mm"), 1)
                for tt in range(3):
                    last = V.tensor_tensor(lg[rows(tt), tt, :], psum[0][rows(tt), tt * 64:tt * 64 + NG + NE], rb[rows(tt), :], add)
                then(last)
                then(V.tensor_copy(gpad[:, :, 0:NG], lg[:, :, 0:NG]))
                for tt in range(3):
                    last = V.max(top[:, tt, :], gpad[:, tt, :])
                then(last)
                for tt in range(3):
                    last = V.max_index(topi[:, tt, :], top[:, tt, :], gpad[:, tt, :])
                then(last)
                then(V.tensor_copy(topf[:], topi[:]))
                for tt, m in enumerate(SIZE):
                    last = V.tensor_scalar(gmask[0:m, tt, :], slot[0:m, 0:NG], topf[0:m, tt, 0:1], None, ALU.is_equal)
                last.then_inc(sem("gmask_ready"), 1)
                V.tensor_tensor(gexp[:], lg[:, :, 0:NG], top[:, :, 0:1].broadcast_to([P, 3, NG]), sub).then_inc(sem("gdiff_ready"), 1)
                dve.wait_ge(sem("gmask_ready"), 1)
                then(V.tensor_tensor(eprod[:], lg[:, :, NG:NG + NE].rearrange("p t (g e) -> p t e g", g=NG),
                                     gmask[:].unsqueeze(2).broadcast_to([P, 3, EPG, NG]), mult))
                then(V.tensor_reduce(esel[:], eprod[:], AX_X, add))
                dve.wait_ge(sem("gexp_ready"), 1)
                V.tensor_reduce(gsum[:, :, 0:1], gexp[:], AX_X, add)
                for tt in range(3):
                    last = V.max(top[:, tt, :], esel[:, tt, :])
                then(last)
                for tt in range(3):
                    last = V.max_index(topi[:, tt, :], top[:, tt, :], esel[:, tt, :])
                then(last)
                V.reciprocal(gsum[:, :, 1:2], gsum[:, :, 0:1])
                V.tensor_copy(topf[:], topi[:])
                V.tensor_tensor(tw[:, :, 0:1], top[:, :, 1:2], top[:, :, 0:1], sub).then_inc(sem("ediff_ready"), 1)
                dve.wait_ge(sem("eexp_ready"), 1)
                then(V.tensor_scalar(tw[:, :, 2:3], tw[:, :, 1:2], 1.0, None, add))
                then(V.reciprocal(tw[:, :, 3:4], tw[:, :, 2:3]))
                then(V.tensor_tensor(tw[:, :, 2:3], tw[:, :, 3:4], gsum[:, :, 1:2], mult))
                then(V.tensor_tensor(tw[:, :, 3:4], tw[:, :, 2:3], tw[:, :, 1:2], mult))
                for tt in range(3):
                    V.tensor_scalar(c8[:, tt, :], slot[:, 0:8], topf[:, tt, 0:1], tw[:, tt, 2:3], ALU.is_equal, mult)
                    last = V.tensor_scalar(c8b[:, tt, :], slot[:, 0:8], topf[:, tt, 1:2], tw[:, tt, 3:4], ALU.is_equal, mult)
                then(last)
                then(V.tensor_tensor(c8[:], c8[:], c8b[:], add))
                for tt in range(3):
                    V.tensor_tensor(comb[:, tt], gmask[:, tt, :].unsqueeze(2).broadcast_to([P, NG, EPG]),
                                    c8[:, tt, :].unsqueeze(1).broadcast_to([P, NG, EPG]), mult)
                dve.wait_ge(sem("pos_mm"), 1)
                for tt in range(3):
                    V.tensor_copy(pos[rows(tt), tt, :], psum[1][rows(tt), tt * NG:(tt + 1) * NG])
                then(V.tensor_reduce(cnt[:, 0:1], psum[1][:, 16:16 + NG], AX_X, ALU.max))
                then(V.tensor_scalar(cnt[:, 1:2], cnt[:, 0:1], float(SLOTS), 1.0, ALU.is_gt, add))
                V.tensor_scalar(cnt[:, 2:3], cnt[:, 0:1], float(2 * SLOTS), None, ALU.is_gt).then_inc(sem("cnt_step"), 1)
                dve.wait_ge(sem("cnt_step"), 1)
                V.tensor_tensor(rounds_i[:], cnt[:, 1:2], cnt[:, 2:3], add).then_inc(sem("rounds_ready"), 1)
                dve.sem_inc(sem("bank_free"), 1)

                def group_pre(g, n):
                    V.tensor_copy(pcol[:, 0:2], pos[:, 0:2, bass.ds(g, 1)].rearrange("p t o -> p (t o)"))
                    V.tensor_copy(pcol[0:B, 2:3], pos[0:B, 2, bass.ds(g, 1)])
                    V.tensor_copy(mcol[:], gmask[:, :, bass.ds(g, 1)].rearrange("p t o -> p (t o)"))
                    V.tensor_copy(cg[:], comb[:, :, bass.ds(g, 1), :].rearrange("p t o e -> p t (o e)")).then_inc(sem("cols_ready"), 1)
                    dve.wait_ge(sem("cols_ready"), n + 1)
                    for tt in range(3):
                        last = V.tensor_scalar(G[rows(tt), tt, :], slot[rows(tt), :], pcol[rows(tt), tt:tt + 1], mcol[rows(tt), tt:tt + 1], ALU.is_equal, mult)
                    last.then_inc(sem("G_ready"), 1)
                    dve.wait_ge(sem("xg_mm"), n + 1)
                    V.tensor_copy(xg[:, 4:8, :], psum[1][:, 0:4 * SLOTS].rearrange("p (k s) -> p k s", k=4)).then_inc(sem("xg_copy"), 1)
                    dve.wait_ge(sem("cb_mm"), n + 1)
                    V.tensor_copy(cb[:, 4:8, :], psum[3][:, 0:4 * SLOTS].rearrange("p (k s) -> p k s", k=4)).then_inc(sem("cb_copy"), 1)
                    dve.wait_ge(sem("cb_copy"), 2 * n + 2)
                    V.memset(hold[:], 0.0)

                def expert(half, q):
                    for s in range(RING):
                        p = s % 2
                        turn = q * 2 + s // 2
                        gate = MB[p][:, 0:2 * SLOTS].rearrange("p (f s) -> p f s", f=2)
                        up = MB[p][:, 2 * SLOTS:4 * SLOTS].rearrange("p (f s) -> p f s", f=2)
                        dve.wait_ge(sem(f"th_ready{p}"), turn + 1)
                        V.scalar_tensor_tensor(out=hs[p][:], in0=th[p][:], scalar=1.0, in1=gate, op0=add, op1=mult).then_inc(sem(f"silu{p}"), 1)
                        dve.wait_ge(sem(f"silu{p}"), turn + 1)
                        V.tensor_tensor(th[p][:], hs[p][:], up, mult).then_inc(sem(f"h_bank{p}"), 1)
                        dve.wait_ge(sem(f"h_bank{p}"), turn + 2)
                        V.scalar_tensor_tensor(out=h[p][:], in0=th[p][:], scalar=0.5,
                                               in1=cb[:, bass.ds(half * RING + s, 1), :].broadcast_to([P, 2, SLOTS]),
                                               op0=mult, op1=mult).then_inc(sem(f"h_ready{p}"), 1)

                def group_post(g, n):
                    dve.wait_ge(sem("ysum_mm"), n + 1)
                    V.tensor_copy(ysb[:, 4:8, :], YB[1][:, 0:4 * SLOTS].rearrange("p (k s) -> p k s", k=4)).then_inc(sem("ysb_copy"), 1)
                    dve.wait_ge(sem("yt_mm"), n + 1)
                    V.tensor_copy(yt[:, 512:1024], psum[3][0:SLOTS, :]).then_inc(sem("yt_copy"), 1)
                    for tt in range(3):
                        for hf in range(2):
                            hc = slice(hf * 512, (hf + 1) * 512)
                            dve.wait_ge(sem("scat_mm"), n * 6 + 2 * tt + hf + 1)
                            last = V.tensor_tensor(x[rows(tt), tt, hc], x[rows(tt), tt, hc], psum[(2 * tt + hf) % 4][rows(tt), :], add)
                            last.then_inc(sem("scat_add"), 1)
                    settle(dve)
                    dve.wait_ge(sem("scat_add"), n * 6 + 6)
                    dve.sem_inc(sem("bank_free"), 1)

                def round_end(rnd):
                    for tt in range(3):
                        last = V.tensor_scalar(pos[rows(tt), tt, :], pos[rows(tt), tt, :], -float(SLOTS), None, add)
                    last.then_inc(sem("pos_shifted"), 1)
                    settle(dve)
                    dve.wait_ge(sem("pos_shifted"), rnd + 1)

                loop(dve, group_pre, expert, group_post, round_end)
                dve.sem_inc(sem("moe_done"), 1)
                dve.wait_ge(sem("x2_root"), 1)
                V.reciprocal(stat[:, :, 2:3], stat[:, :, 1:2]).then_inc(sem("x2_inv"), 1)
                dve.wait_ge(sem("x2_inv"), 1)
                dve.wait_ge(sem("gfin_in"), 16)
                for tt in range(3):
                    last = V.scalar_tensor_tensor(out=xn[rows(tt), tt, :], in0=x[rows(tt), tt, :], scalar=stat[rows(tt), tt, 2:3],
                                                  in1=gfin[rows(tt), :], op0=mult, op1=mult)
                last.then_inc(sem("y_final"), 1)


_INS = ['x_prompt', 'x_sample', 'state_ret', 'state_rwkv', 'state_shift', 'norm_mix', 'w_in', 'mu_shift', 'ret_gn_w',
        'rwkv_w0', 'rwkv_w2', 'rwkv_a0', 'rwkv_a2', 'rwkv_g2', 'rwkv_k_k', 'rwkv_k_a', 'rwkv_r_k', 'rwkv_lnx_w',
        'rwkv_lnx_b', 'w_out', 'norm_ffn', 'router_group_w', 'router_group_b', 'router_expert_w', 'router_expert_b',
        'expert_w_gate', 'expert_w_up', 'expert_w_down', 'norm_final']
_OUTS = [("y_p", (1, TP, D)), ("y_s", (B, 1, D)), ("ret_p", (1, 1, HEADS, P, P)), ("rwkv_p", (1, 1, RH, HD, HD)),
         ("shift_p", (1, 1, D)), ("ret_s", (1, B, HEADS, P, P)), ("rwkv_s", (1, B, RH, HD, HD)), ("shift_s", (1, B, D))]


def kernel(**inputs):
    import numpy as _np
    import concourse.bacc as _bacc
    from concourse import mybir as _mybir
    from concourse.bass_utils import run_bass_kernel_spmd as _run

    nc = _bacc.Bacc("TRN2", target_bir_lowering=False, num_devices=1)
    arrays, args, consts, outs = {}, {}, {}, {}
    for name in _INS:
        arr = _np.ascontiguousarray(inputs[name])
        arrays[f"in_{name}_dram"] = arr
        args[name] = nc.dram_tensor(f"in_{name}_dram", arr.shape, _mybir.dt.from_np(arr.dtype), kind="ExternalInput").ap()
    for name, arr in constants().items():
        arrays[f"const_{name}_dram"] = arr
        consts[name] = nc.dram_tensor(f"const_{name}_dram", arr.shape, _mybir.dt.from_np(arr.dtype), kind="ExternalInput").ap()
    for name, shape in _OUTS:
        outs[name] = nc.dram_tensor(f"out_{name}_dram", shape, _mybir.dt.float32, kind="ExternalOutput").ap()
    hybrid_moe_step(nc, args, outs, consts)
    res = _run(nc, [arrays], core_ids=[0]).results[0]
    return tuple(res[f"out_{name}_dram"] for name, _ in _OUTS)
```

```python
from contextlib import ExitStack

import numpy as np

import concourse.bass as bass
from concourse import mybir

ALU = mybir.AluOpType
ACT = mybir.ActivationFunctionType
F32 = mybir.dt.float32
F32R = mybir.dt.float32r
I32 = mybir.dt.int32
AX_X = mybir.AxisListType.X

P = 128
D = 1024
KT = D // P
TP = 256
TT = TP // P
B = 8
T = TP + B
TX = T + B
HEADS = 8
RH = 16
HD = 64
C = 64
NCH = TP // C
PAST = 2048
NG, EPG = 4, 8
NE = NG * EPG
DE = 256
SLOTS = 128
LORA = 64
LORA_G = 160
RMS_EPS, RET_EPS, RWKV_EPS = 1e-6, 1e-5, 64e-5

O_Q, O_K, O_V, O_GS = 0, D, 2 * D, 3 * D
O_SH = 4 * D
O_R, O_RK, O_RV = O_SH, O_SH + D, O_SH + 2 * D
O_LORA = O_SH + 3 * D
N_LORA = 2 * LORA + LORA_G
O_GA = O_LORA + N_LORA
O_GB = O_GA + D
N_IN = O_GB + D
SECTIONS = [O_RK, O_R, O_RV, O_Q, O_K, O_V, O_GS, O_GA, O_GB]

PAR = ["mu_r", "mu_k", "mu_v", "w0", "a0", "k_k", "k_a", "r_k", "lnx_w", "lnx_b", "gn_w"]
NPAR = len(PAR)
DERIVED = ["om_r", "om_k", "om_v", "w0h", "a0h", "om_ka"]
PX = {n: i for i, n in enumerate(PAR + DERIVED)}
NPX = len(PX)
LOGW_C = -0.5 * float(np.exp(-0.5))


def constants():
    out = {}
    half = P // 2
    inv = (10000.0 ** (-np.arange(half, dtype=np.float32) / np.float32(half))).astype(np.float32)
    pos = np.concatenate([np.arange(TP), np.full(B, PAST)]).astype(np.float32)
    ang = (inv[:, None] * pos[None, :]).astype(np.float32).astype(np.float64)
    cos, sin = np.cos(ang), np.sin(ang)
    cs = np.concatenate([cos, cos], 0)
    sn = np.concatenate([sin, -sin], 0)
    scale = P ** -0.5
    out["rope"] = np.stack([cs, sn, cs * scale, sn * scale], 1)
    lg = np.log1p(-np.exp2(-5.0 - np.arange(HEADS)))
    j = np.arange(P)[:, None]
    i0 = np.arange(TP)[None, :]
    dec = np.zeros((P, HEADS, TP + P))
    kd = np.zeros((P, HEADS, 3))
    for h in range(HEADS):
        dec[:, h, :TP] = np.where(i0 >= j, np.exp(np.maximum(i0 - j, 0) * lg[h]), 0)
        i1 = np.arange(P)[None, :]
        dec[:, h, TP:] = np.where(i1 >= j, np.exp(np.maximum(i1 - j, 0) * lg[h]), 0)
        for tt in range(TT):
            kd[:, h, tt] = np.exp((TP - 1 - tt * P - np.arange(P)) * lg[h])
        kd[:, h, 2] = np.exp(lg[h])
    out["retdec"] = dec
    out["retcol"] = kd
    s, t = np.meshgrid(np.arange(P), np.arange(P), indexing="ij")
    same64 = s // C == t // C
    same16 = s // 16 == t // 16
    m = np.zeros((P, 4, P))
    m[:, 0] = same16 & (s < t)
    m[:, 1] = same64 & (s <= t)
    m[:, 2] = same64 & (s < t)
    m[:, 3] = same64 & (s <= t)
    out["mk"] = m
    lo = np.zeros((P, 2, P))
    lo[:, 0] = same16 & (t < s)
    lo[:, 1] = same64 & ~same16 & (t < s)
    out["mlo"] = lo
    out["ident"] = np.eye(P)
    out["one64"] = (s // HD == t // HD).astype(np.float64)
    out["mean64"] = out["one64"] / HD
    out["mean128"] = np.ones((P, P)) / P
    sm = np.ones((P, T))
    sm[:, 0:TP:C] = 0
    sm[:, TP:] = 0
    out["scanm"] = sm
    out["tri"] = (s < t).astype(np.float64)
    out["ones"] = np.ones((P, P))
    out["id64"] = np.concatenate([np.eye(HD), np.eye(HD)], 0)
    out["slot"] = np.tile(np.arange(SLOTS)[None, :], (P, 1)).astype(np.float64)
    d8 = np.zeros((B, B, P))
    for b in range(B):
        d8[b, b] = 1
    out["diag8"] = d8
    return {k: np.ascontiguousarray(v.astype(np.float32)) for k, v in out.items()}


class Semaphores:

    def __init__(self, nc):
        self.nc = nc
        self.named = {}
        self.stack = ExitStack()

    def __call__(self, name):
        if name not in self.named:
            self.named[name] = self.stack.enter_context(self.nc.semaphore(name))
        return self.named[name]

    def next_phase(self):
        handles = list(self.named.values())

        def clear(eng, share):
            for handle in handles[share::5]:
                eng.sem_clear(handle)

        with self.nc.Block() as block:

            @block.gpsimd
            def _(pool):
                clear(pool, 0)

            @block.vector
            def _(dve):
                clear(dve, 1)

            @block.scalar
            def _(act):
                clear(act, 2)

            @block.tensor
            def _(pe):
                clear(pe, 3)

            @block.sync
            def _(sp):
                clear(sp, 4)

        self.named = {}
        self.stack.close()


def hybrid_moe_step(nc, a, o, k):
    w_in = a["w_in"][0].rearrange("(k p) c -> p k c", p=P)

    with ExitStack() as top:
        keep = {}

        def alloc(ctx, table, name, shape, dt=F32):
            table[name] = ctx.enter_context(nc.sbuf_tensor(name, shape, dt))
            return table[name]

        sem = Semaphores(nc)

        psum = [top.enter_context(nc.psum_tensor(f"bank{n}", [P, 512], F32)) for n in range(8)]
        cst = {}
        for n in ("ident", "tri", "ones", "slot"):
            alloc(top, cst, "c_" + n, list(k[n].shape))
        x = alloc(top, keep, "x", [P, 3, D])
        xn = alloc(top, keep, "xn", [P, 3, D])
        stat = alloc(top, keep, "xstat", [P, 3, 4])
        eps = alloc(top, keep, "eps", [P, 4])

        mixer_phase(nc, a, o, k, w_in, alloc, sem, psum, cst, keep)
        sem.next_phase()
        moe_phase(nc, a, o, k, alloc, sem, psum, cst, keep)
        sem.next_phase()


def mixer_phase(nc, a, o, k, w_in, alloc, sem, psum, cst, keep):
    with ExitStack() as ctx:
        sb = {}

        def buf(name, shape):
            return alloc(ctx, sb, name, shape)

        for n in ("one64", "mean64", "mean128", "id64"):
            alloc(ctx, cst, "c_" + n, list(k[n].shape))
        ident, one64, mean64, mean128 = (cst["c_" + n] for n in ("ident", "one64", "mean64", "mean128"))
        eps = keep["eps"]
        gbc = buf("gbc", [P, D])
        merged = buf("merged", [P, KT, T])
        svec = buf("svec", [P, KT, 6, B])
        spost = buf("spost", [P, 3, KT, B])
        parc = buf("parc", [P, NPX, KT])

        room1 = buf("room1", [P, 3 * D + 2 * B * P])
        lowa = room1[:, 0:D]
        g2a = room1[:, D:2 * D]
        g2b = room1[0:LORA_G - P, 2 * D:3 * D]
        sin_ = room1[:, 3 * D:3 * D + B * P].rearrange("p (b v) -> p b v", b=B)
        snew = room1[:, 3 * D + B * P:3 * D + 2 * B * P].rearrange("p (b v) -> p b v", b=B)
        st = room1[:, 0:HD * HD].rearrange("p (v k) -> p v k", v=HD)
        NDEC = HEADS * (TP + P)
        room2 = buf("room2", [P, NDEC + KT * TX])
        retdec = room2[:, 0:NDEC].rearrange("p (h c) -> p h c", h=HEADS)
        xt = room2[:, NDEC:NDEC + KT * TX].rearrange("p (k t) -> p k t", k=KT)
        prod = room2[:, 0:HD * HD].rearrange("p (v k) -> p v k", v=HD)
        NV = 6 * B
        stok = room2[0:NV, HD * HD:HD * HD + D]
        ytok = room2[0:B, HD * HD:HD * HD + D]
        room3 = buf("room3", [P, 4 * T])
        rope = room3[:].rearrange("p (n t) -> p n t", n=4)
        vec = room3[:, 0:6 * HD].rearrange("p (n c) -> p n c", n=6)
        sa, y1 = room3[:, 6 * HD:7 * HD], room3[:, 7 * HD:8 * HD]
        sy, syc, sysq, syr = (room3[:, (8 + n) * HD:(9 + n) * HD].rearrange("p (k b) -> p k b", k=KT) for n in range(4))
        wall = buf("wall", [P, 9, KT * P])
        wslot = [wall[:, n].rearrange("p (k c) -> p k c", k=KT) for n in range(9)]
        xroom = keep["x"][:].rearrange("p t d -> p (t d)")
        pr = xroom[:, 0:16 * P].rearrange("p (u n c) -> p u n c", u=4, n=4)
        la = xroom[:, 16 * P:24 * P].rearrange("p (u n c) -> p u n c", u=4, n=2)
        nroom = keep["xn"][:].rearrange("p t d -> p (t d)")
        at2w, at4w = (nroom[:, n * 8 * P:(n + 1) * 8 * P].rearrange("p (u n c) -> p u n c", u=4, n=2) for n in range(2))
        w2s, w3 = (nroom[:, (4 + n) * 4 * P:(5 + n) * 4 * P].rearrange("p (u c) -> p u c", u=4) for n in range(2))
        retcol = buf("retcol", [P, HEADS, 3])
        mk = buf("mk", [P, 4, P])
        mlo = buf("mlo", [P, 2, P])
        scanm = buf("scanm", [P, T])
        diag8 = buf("diag8", [B, B, P])

        lwa = buf("lwa", [P, T])
        lga = buf("lga", [P, T])
        lgb = buf("lgb", [LORA_G - P, T])
        mulora = buf("mulora", [P, 6])

        def tok(name):
            return buf(name, [P, T])

        pro = ExitStack()
        x_tok = alloc(pro, sb, "x_tok", [P, TT, D])
        xs_tok = alloc(pro, sb, "xs_tok", [2 * B, D])
        sq_junk = alloc(pro, sb, "sq_junk", [P, D])
        stat = alloc(pro, sb, "stat", [P, 3, 4])
        prow = alloc(pro, sb, "prow", [P, P])
        wlora = alloc(pro, sb, "wlora", [P, KT, N_LORA])
        mpro = alloc(pro, sb, "mpro", [P, 3, TX + 1])

        mult, add, sub = ALU.mult, ALU.add, ALU.subtract

        def mm(pe, out, lhsT, rhs, start, stop, loose=False):
            return nc.tensor.matmul(out, lhsT, rhs, start=start, stop=stop, skip_group_check=loose)

        with nc.Block() as block:

            @block.sync
            def _(sp):
                sp.dma_start(sb["x_tok"][:, 0, :], a["x_prompt"][0, 0:P, :]).then_inc(sem("x0_in"), 16)
                sp.dma_start(sb["x_tok"][:, 1, :], a["x_prompt"][0, P:TP, :]).then_inc(sem("x_in"), 16)
                sp.dma_start(sb["xs_tok"][0:B, :], a["x_sample"].rearrange("b t d -> (b t) d")).then_inc(sem("x_in"), 16)
                sp.dma_start(sb["xs_tok"][B:2 * B, :], a["state_shift"][0]).then_inc(sem("x_in"), 16)
                sp.dma_start(gbc[:], a["norm_mix"].partition_broadcast(P)).then_inc(sem("gbc_in"), 16)
                sp.dma_start(wlora[:], w_in[:, :, O_LORA:O_LORA + N_LORA]).then_inc(sem("wlora_in"), 16)
                sp.wait_ge(sem("prow_zero"), 1)
                mu = a["mu_shift"][0:1, :]
                sp.dma_start(prow[0:3 * KT, :], a["mu_shift"][0, 0:3 * D].rearrange("(k c) -> k c", c=P)).then_inc(sem("prow_in"), 16)
                rows = [a[n][0] for n in ("rwkv_w0", "rwkv_a0", "rwkv_k_k", "rwkv_k_a")]
                rows += [a["rwkv_r_k"][0].rearrange("h c -> (h c)")]
                rows += [a[n][0] for n in ("rwkv_lnx_w", "rwkv_lnx_b", "ret_gn_w")]
                for n, row in enumerate(rows, 3):
                    sp.dma_start(prow[n * KT:(n + 1) * KT, :], row.rearrange("(k c) -> k c", c=P)).then_inc(sem("prow_in"), 16)
                lo = NPAR * KT
                sp.dma_start(prow[lo:lo + 1, :], mu[:, 3 * D:3 * D + P]).then_inc(sem("prow_in"), 16)
                sp.dma_start(prow[lo + 1:lo + 2, :], mu[:, 3 * D + P:3 * D + 2 * P]).then_inc(sem("prow_in"), 16)
                sp.dma_start(prow[lo + 2:lo + 3, 0:LORA_G - P], mu[:, 3 * D + 2 * P:3 * D + N_LORA]).then_inc(sem("prow_in"), 16)
                sp.dma_start(lowa[0:LORA, :], a["rwkv_w2"][0]).then_inc(sem("lora_in"), 16)
                sp.dma_start(lowa[LORA:2 * LORA, :], a["rwkv_a2"][0]).then_inc(sem("lora_in"), 16)
                sp.dma_start(g2a, a["rwkv_g2"][0][0:P, :]).then_inc(sem("lora_in"), 16)
                sp.dma_start(g2b, a["rwkv_g2"][0][P:LORA_G, :]).then_inc(sem("lora_in"), 16)
                for n, off in enumerate(SECTIONS):
                    sp.dma_start(wslot[n], w_in[:, :, off:off + P]).then_inc(sem("w_first"), 16)
                sp.wait_ge(sem("xn_ready"), 1)
                sp.dma_start(o["shift_p"][0, 0:1, :], sb["x_tok"][P - 1:P, TT - 1, :]).then_inc(sem("out_done"), 16)
                sp.dma_start(o["shift_s"][0], sb["xs_tok"][0:B, :]).then_inc(sem("out_done"), 16)
                sp.wait_ge(sem("out_done"), 32)
                sp.wait_ge(sem("lora_in"), 64)
                sp.wait_ge(sem("w_first"), 16 * 9)

            @block.scalar
            def _(act):
                for n in ("ident", "one64", "mean64", "mean128", "tri", "ones", "slot", "id64"):
                    act.dma_start(cst["c_" + n][:], k[n]).then_inc(sem("ident_in" if n == "ident" else "const_in"), 16)
                act.wait_ge(sem("eps_ready"), 1)
                act.activation(sq_junk[0:1, 0:1], eps[0:1, 3:4], ACT.Sqrt).then_inc(sem("sq_done"), 1)
                act.wait_ge(sem("stat_zero"), 1)
                act.wait_ge(sem("x0_in"), 16)
                act.wait_ge(sem("sq_done"), 1)
                for t in range(TT):
                    if t == 1:
                        act.wait_ge(sem("x_in"), 48)
                    act.activation(sq_junk[:], sb["x_tok"][:, t, :], ACT.Square, accum_out=stat[:, t, 0:1]).then_inc(sem("sq_done"), 1)
                    act.wait_ge(sem("sq_done"), t + 2)
                act.activation(sq_junk[0:B, :], sb["xs_tok"][0:B, :], ACT.Square, accum_out=stat[0:B, 2, 0:1]).then_inc(sem("sq_done"), 1)
                act.wait_ge(sem("ms_ready"), 1)
                act.activation(stat[:, :, 2:3], stat[:, :, 1:2], ACT.Sqrt).then_inc(sem("rms_ready"), 1)
                for n, t in (("rope", rope), ("retdec", retdec), ("retcol", retcol[:]), ("mk", mk[:]), ("mlo", mlo[:]),
                             ("scanm", scanm[:]), ("diag8", diag8[:])):
                    act.dma_start(t, k[n]).then_inc(sem("const_in"), 16)
                act.activation(sq_junk[0:1, 0:1], eps[0:1, 3:4], ACT.Tanh)
                for kk in range(0, KT, 2):
                    act.wait_ge(sem("xt_mm"), kk + 1)
                    act.copy(xt[:, kk, :], psum[kk][:, 0:TX]).then_inc(sem("xt_act"), 1)
                for n, m in enumerate((P, P, LORA_G - P)):
                    act.wait_ge(sem("lora_mm"), n + 1)
                    act.wait_ge(sem("mulora_ready"), 2)
                    act.activation(mpro[0:m, n, 1:TX + 1], psum[n][0:m, 0:TX], ACT.Copy, scale=mulora[0:m, n:n + 1]).then_inc(sem("lora_mu"), 1)
                act.wait_ge(sem("lora_mix"), 1)
                act.activation(lwa[0:LORA, :], lwa[0:LORA, :], ACT.Tanh)
                act.wait_ge(sem("lora_mix"), 3)
                act.activation(lga[:], lga[:], ACT.Tanh, scale=0.5)
                act.activation(lgb[:], lgb[:], ACT.Tanh, scale=0.5).then_inc(sem("lora_tanh"), 1)
                act.wait_ge(sem("const_in"), 16 * 14)

            @block.vector
            def _(dve):
                nc.vector.memset(prow[:], 0.0).then_inc(sem("prow_zero"), 1)
                nc.vector.memset(stat[:], 1.0).then_inc(sem("stat_zero"), 1)
                nc.vector.memset(mpro[:], 0.0).then_inc(sem("mpro_zero"), 1)
                nc.vector.memset(eps[:, 0:1], RET_EPS)
                nc.vector.memset(eps[:, 1:2], RWKV_EPS)
                nc.vector.memset(eps[:, 2:3], RMS_EPS)
                nc.vector.memset(eps[:, 3:4], 0.0).then_inc(sem("eps_ready"), 1)
                dve.wait_ge(sem("sq_done"), 4)
                nc.vector.tensor_scalar(stat[:, :, 1:2], stat[:, :, 0:1], 1.0 / D, RMS_EPS, mult, add).then_inc(sem("ms_ready"), 1)
                dve.wait_ge(sem("rms_ready"), 1)
                nc.vector.reciprocal(stat[:, :, 3:4], stat[:, :, 2:3]).then_inc(sem("rstd_ready"), 1)
                dve.wait_ge(sem("rstd_ready"), 1)
                dve.wait_ge(sem("gbc_in"), 16)
                for t in range(TT):
                    nc.vector.scalar_tensor_tensor(out=sb["x_tok"][:, t, :], in0=sb["x_tok"][:, t, :], scalar=stat[:, t, 3:4],
                                                   in1=gbc[:], op0=mult, op1=mult)
                nc.vector.scalar_tensor_tensor(out=sb["xs_tok"][0:B, :], in0=sb["xs_tok"][0:B, :], scalar=stat[0:B, 2, 3:4],
                                               in1=gbc[0:B, :], op0=mult, op1=mult).then_inc(sem("xn_ready"), 1)
                for kk in range(1, KT, 2):
                    dve.wait_ge(sem("xt_mm"), kk + 1)
                    nc.vector.tensor_copy(xt[:, kk, :], psum[kk][:, 0:TX]).then_inc(sem("xt_dve"), 1)
                dve.wait_ge(sem("par_mm"), 1)
                nc.vector.tensor_copy(parc[:, 0:NPAR, :], psum[7][:, 0:NPAR * KT].rearrange("p (n k) -> p n k", k=KT)).then_inc(sem("par_c"), 1)
                nc.vector.tensor_copy(mulora[:, 0:3], psum[7][:, NPAR * KT:NPAR * KT + 3]).then_inc(sem("mulora_ready"), 1)
                dve.wait_ge(sem("par_c"), 1)
                dve.wait_ge(sem("mulora_ready"), 1)
                nc.vector.tensor_scalar(mulora[:, 3:6], mulora[:, 0:3], -1.0, 1.0, mult, add).then_inc(sem("mulora_ready"), 1)
                nc.vector.tensor_scalar(parc[:, PX["om_r"]:PX["om_v"] + 1, :], parc[:, PX["mu_r"]:PX["mu_v"] + 1, :], -1.0, 1.0, mult, add)
                nc.vector.tensor_scalar(parc[:, PX["w0h"]:PX["a0h"] + 1, :], parc[:, PX["w0"]:PX["a0"] + 1, :], 0.5, None, mult)
                nc.vector.tensor_scalar(parc[:, PX["om_ka"], :], parc[:, PX["k_a"], :], -1.0, 1.0, mult, add).then_inc(sem("parc_ready"), 1)
                dve.wait_ge(sem("mulora_ready"), 2)
                for n, (m, dst) in enumerate(((P, lwa), (P, lga), (LORA_G - P, lgb))):
                    dve.wait_ge(sem("lora_mu"), n + 1)
                    om = mulora[0:m, 3 + n:4 + n]
                    nc.vector.scalar_tensor_tensor(out=dst[0:m, 0:TP], in0=psum[n][0:m, 0:TP], scalar=om, in1=mpro[0:m, n, 0:TP], op0=mult, op1=add)
                    nc.vector.scalar_tensor_tensor(out=dst[0:m, TP:T], in0=psum[n][0:m, TP:T], scalar=om, in1=mpro[0:m, n, T + 1:TX + 1],
                                                   op0=mult, op1=add).then_inc(sem("lora_mix"), 1)
                dve.wait_ge(sem("lora_tanh"), 1)
                nc.vector.tensor_scalar(lga[:], lga[:], 0.5, 0.5, mult, add)
                nc.vector.tensor_scalar(lgb[:], lgb[:], 0.5, 0.5, mult, add).then_inc(sem("lora_ready"), 1)

            @block.tensor
            def _(pe):
                pe.wait_ge(sem("ident_in"), 16)
                pe.wait_ge(sem("xn_ready"), 1)
                for kk in range(KT):
                    for t in range(TT):
                        nc.tensor.transpose(psum[kk][:, t * P:(t + 1) * P], sb["x_tok"][:, t, kk * P:(kk + 1) * P], ident[:])
                    nc.tensor.transpose(psum[kk][:, TP:TX], sb["xs_tok"][:, kk * P:(kk + 1) * P], ident[0:2 * B, 0:2 * B]).then_inc(sem("xt_mm"), 1)
                pe.wait_ge(sem("xt_dve"), 4)
                pe.wait_ge(sem("prow_in"), 16 * 12)
                nrow = NPAR * KT + 3
                nc.tensor.transpose(psum[7][:, 0:nrow], prow[0:nrow, :], ident[0:nrow, 0:nrow]).then_inc(sem("par_mm"), 1)
                pe.wait_ge(sem("xt_act"), 4)
                pe.wait_ge(sem("wlora_in"), 16)
                for n, m in enumerate((P, P, LORA_G - P)):
                    for kk in range(KT):
                        last = mm(pe, psum[n][0:m, 0:TX], wlora[:, kk, n * P:n * P + m], xt[:, kk, :], kk == 0, kk == KT - 1)
                    last.then_inc(sem("lora_mm"), 1)
        pro.close()
        sem.next_phase()

        pt = buf("pt", [P, NPX])
        dcol = buf("dcol", [P, 3])
        epc = buf("epc", [P, NCH])
        ygate, ybias = buf("ygate", [P, TP]), buf("ybias", [P, TP])
        mshift = [buf(f"mshift{n}", [P, TX + 1]) for n in range(3)]
        r, kx, vx = tok("r"), tok("kx"), tok("vx")
        thw, tha, gg = tok("thw"), tok("tha"), tok("gg")
        kk0, kks, kkn = tok("kk0"), tok("kks"), tok("kkn")
        kk, ba, kmod, lp, lpx = tok("kk"), tok("ba"), tok("kmod"), tok("lp"), tok("lpx")
        ep, en, epx = tok("ep"), tok("en"), tok("epx")
        ar = buf("ar", [P, TT, 2, P])
        bt, kt = buf("bt", [P, TP]), buf("kt", [P, TP])
        rkk, bonus = tok("rkk"), tok("bonus")
        qr, kr, vr = tok("qr"), tok("kr"), tok("vr")
        ta, tb = tok("ta"), tok("tb")
        sg, thg = tok("sg"), kks
        ga, gb = tok("ga"), tok("gb")
        a2 = buf("a2", [P, 4, P])
        a4 = buf("a4", [P, 4, P])
        a8 = buf("a8", [P, 4, P])
        rhs = buf("rhs", [P, 4, 2, HD])
        nt, x0 = buf("nt", [P, 4, P]), buf("x0", [P, 4, P])
        z1, z2, zf = a2, a4, a8
        tmk = buf("tmk", [P, TT, 3, P])
        fts = buf("fts", [P, NCH, HD])
        q = buf("q", [P, TP])
        zst = [buf(f"zst{n}", [P, HD]) for n in range(NCH)]
        zout = buf("zout", [HD, 2, HD])
        ys, yc, ysq, yrs = tok("ys"), tok("yc"), tok("ysq"), tok("yrs")
        kvt = buf("kvt", [P, 4, P])
        vd = buf("vd", [P, TT, P])
        sc = buf("sc", [P, TP + P])
        ks8 = buf("ks8", [B, 2, P])
        vdiag = buf("vdiag", [B, B, P])
        stp = buf("stp", [P, P])
        os_, osq, ors = ys, ysq, yrs
        oc = tok("oc")

        pj = [psum[0], psum[1]]
        M = psum[2:8]

        def v4(x):
            return x[:].rearrange("p (u c) -> p u c", u=4)


        def done(eng, name, i):
            eng.wait_ge(sem(name), i + 1)

        def past(eng, name, n):
            eng.wait_ge(sem(name), n)

        def settle(eng):
            eng.wait_ge(sem("mshift_zero"), 1)

        def last_pass(eng, name, i):
            if not (isinstance(i, int) and i == 0):
                eng.wait_ge(sem(name), i)

        def projected(eng, i, use):
            eng.wait_ge(sem("projected"), i * USES + (use + 1))

        emptied = ["k_mix", "w_tanh", "a_tanh", "r_mix", "v_mix", "kk_root", "q_rope", "k_rope", "g_copy", "bonus_sum",
                   "v_copy", "gs_silu", "ga_tanh", "gb_tanh"]
        U_RK, U_W, U_A, U_R, U_RV, U_KK, U_Q, U_K, U_G, U_BON, U_V, U_GS, U_GA, U_GB = range(14)
        USES = len(emptied)
        slot_of = {use: s for s, use in enumerate((U_RK, U_R, U_RV, U_Q, U_K, U_V, U_GS, U_GA, U_GB))}

        def bank_free(pe, i, use):
            if use >= 2:
                done(pe, emptied[use - 2], i)
            else:
                last_pass(pe, emptied[12 + use], i)

        def project(pe, i, use, half):
            n = slot_of[use]
            if half == 0:
                bank_free(pe, i, use)
                last_pass(pe, f"w_in{n}", 16 * i)
            width = TX if use in (U_RK, U_R, U_RV) else T
            for kk_ in range(half * KT // 2, (half + 1) * KT // 2):
                last = mm(pe, pj[use % 2][:, 0:width], wslot[n][:, kk_, :], xt[:, kk_, 0:width], kk_ == 0, kk_ == KT - 1)
            if half:
                last.then_inc(sem("projected"), 1)

        def pe_pass(pe, i, n, wst):
            front, back = i is not None, n is not None

            def meanwhile(kk_):
                if not front:
                    if kk_ == 0:
                        pe.wait_ge(sem("stok_ready"), 2)
                        pe.wait_ge(sem("ret_out"), KT)
                        pe.wait_ge(sem("wout_in"), 16 * KT)
                        pe.wait_ge(sem("prompt_merged"), KT - 1)
                    w_out_part(pe, 0, [kk_])

            if front:
                project(pe, i, U_RK, 0)
            if back:
                past(pe, "o_sq", n)
                mm(pe, M[3][:, 0:T], mean128[:], osq[:], True, True).then_inc(sem("ovar_mm"), 1)
            if front:
                project(pe, i, U_RK, 1)
            if back:
                past(pe, "abkr_ready", n)
                for t in range(TT):
                    for m, src in enumerate((ar[:, t, 0, :], bt[:, t * P:(t + 1) * P], kt[:, t * P:(t + 1) * P], vx[:, t * P:(t + 1) * P])):
                        last = nc.tensor.transpose(M[4 + t][:, m * P:(m + 1) * P], src, ident[:])
                    last.then_inc(sem("tok_mm"), 1)
                past(pe, "o_root", n)
                for t in range(TT):
                    for h in range(2):
                        u = 2 * t + h
                        hs = slice(HD * h, HD * h + HD)
                        cols = slice(t * P, (t + 1) * P)
                        mm(pe, M[u][:, 0:2 * P], bt[hs, cols], ar[hs, t].rearrange("p a b -> p (a b)"), True, True)
                        mm(pe, M[u][:, 2 * P:4 * P], kt[hs, cols], ar[hs, t].rearrange("p a b -> p (a b)"), True, True).then_inc(sem("prod"), 1)
                for h in range(2):
                    past(pe, f"tok_copy{h}", n)
                    for t in range(TT):
                        hs = slice(HD * h, HD * h + HD)
                        last = mm(pe, M[4 + h][:, t * P:(t + 1) * P], ar[hs, t, 0, :], bt[hs, t * P:(t + 1) * P], True, True)
                    last.then_inc(sem("prod"), 1)
            if front:
                done(pe, "stage_lora", i)
                bank_free(pe, i, U_W)
                mm(pe, pj[1][:, 0:T], wst["w"][0:LORA, :], lwa[0:LORA, :], True, True).then_inc(sem("projected"), 1)
                bank_free(pe, i, U_A)
                mm(pe, pj[0][:, 0:T], wst["w"][LORA:P, :], lwa[LORA:P, :], True, True).then_inc(sem("projected"), 1)
                project(pe, i, U_R, 0)
                project(pe, i, U_R, 1)
            if back:
                past(pe, "masked", n)
                past(pe, "l_masked", n)
                for u in range(4):
                    last = mm(pe, v4(M[0])[:, u, :], pr[:, u, 0, :], la[:, u, 0, :], True, True)
                last.then_inc(sem("a2_mm"), 1)
                for u in range(4):
                    last = mm(pe, v4(M[1])[:, u, :], la[:, u, 0, :], pr[:, u, 0, :], True, True)
                last.then_inc(sem("at2_mm"), 1)
                for u in range(4):
                    h = u % 2
                    last = mm(pe, M[4][:, u * HD:(u + 1) * HD], pr[:, u, 2, :], tmk[:, u // 2, 2, HD * h:HD * h + HD], True, True)
                last.then_inc(sem("lakv_mm"), 1)
            if front:
                project(pe, i, U_RV, 0)
            if back:
                past(pe, "a2_copy", n)
                past(pe, "w0_ready", n)
                past(pe, "at2_copy", n)
                for u in range(4):
                    last = mm(pe, M[2 + u // 2][:, (u % 2) * 2 * P:(u % 2 + 1) * 2 * P], a2[:, u, :], at2w[:, u].rearrange("p a b -> p (a b)"), True, True)
                last.then_inc(sem("at4w1_mm"), 1)
                for u in range(4):
                    last = mm(pe, v4(M[0])[:, u, :], at2w[:, u, 0, :], a2[:, u, :], True, True)
                last.then_inc(sem("a4_mm"), 1)
                meanwhile(0)
            if front:
                project(pe, i, U_RV, 1)
            if back:
                past(pe, "at4_copy", n)
                past(pe, "w1_ready", n)
                past(pe, "a4_copy", n)
                for u in range(4):
                    last = mm(pe, v4(M[5])[:, u, :], at4w[:, u, 0, :], a4[:, u, :], True, True)
                last.then_inc(sem("a8_mm"), 1)
                for u in range(4):
                    last = mm(pe, v4(M[1])[:, u, :], a4[:, u, :], at4w[:, u, 1, :], True, True)
                last.then_inc(sem("w2_mm"), 1)
                meanwhile(1)
            if front:
                bank_free(pe, i, U_KK)
                done(pe, "kk_sq", i)
                mm(pe, pj[1][:, 0:T], one64[:], kks[:], True, True).then_inc(sem("projected"), 1)
                project(pe, i, U_Q, 0)
            if back:
                past(pe, "a8_copy", n)
                past(pe, "w2_ready", n)
                for u in range(4):
                    last = mm(pe, v4(M[2])[:, u, :], a8[:, u, :], w2s[:, u, :], True, True)
                last.then_inc(sem("w3_mm"), 1)
                meanwhile(2)
            if front:
                project(pe, i, U_Q, 1)
            if back:
                past(pe, "w3_ready", n)
                past(pe, "rhs_ready", n)
                for u in range(4):
                    last = mm(pe, v4(M[3])[:, u, :], la[:, u, 1, :], w3[:, u, :], True, True)
                last.then_inc(sem("nt_mm"), 1)
                for u in range(4):
                    last = mm(pe, v4(M[4])[:, u, :], w3[:, u, :], rhs[:, u].rearrange("p a b -> p (a b)"), True, True)
                last.then_inc(sem("x0_mm"), 1)
                meanwhile(3)

            def horner(src, bank, ready):
                past(pe, ready, n)
                for u in range(4):
                    last = mm(pe, v4(bank)[:, u, :], nt[:, u, :], src[:, u, :], True, True)
                last.then_inc(sem("horner_mm"), 1)

            if front:
                project(pe, i, U_K, 0)
            if back:
                past(pe, "nt_copy", n)
                horner(x0, M[5], "x0_copy")
                meanwhile(4)
            if front:
                project(pe, i, U_K, 1)
            if back:
                horner(z1, M[0], "z1_ready")
                meanwhile(5)
            if front:
                bank_free(pe, i, U_G)
                mm(pe, pj[0][:, 0:T], wst["ga"][:], lga[:], True, False)
                mm(pe, pj[0][:, 0:T], wst["gb"][:], lgb[:], False, True).then_inc(sem("projected"), 1)
                bank_free(pe, i, U_BON)
                done(pe, "rkk_ready", i)
                mm(pe, pj[1][:, 0:T], one64[:], rkk[:], True, True).then_inc(sem("projected"), 1)
            if back:
                horner(z2, M[1], "z2_ready")
                meanwhile(6)
            if front:
                project(pe, i, U_V, 0)
            if back:
                past(pe, "zf_ready", n)
                for u in range(4):
                    h, t = u % 2, u // 2
                    hs = slice(HD * h, HD * h + HD)
                    last = mm(pe, M[2][hs, t * P:(t + 1) * P], zf[:, u, 0:HD], pr[:, u, 1, :], True, True, True)
                last.then_inc(sem("q_mm"), 1)
                for par in range(2):
                    ps = slice(C * par, C * par + C)
                    for u in range(4):
                        h, t = u % 2, u // 2
                        hs = slice(HD * h, HD * h + HD)
                        hc = slice(HD * h, HD * h + HD)
                        mm(pe, M[4 + par][hs, t * P:t * P + HD], zf[ps, u, 0:HD], tmk[ps, t, 0, hc], t == 0, False, True)
                        mm(pe, M[4 + par][hs, t * P + HD:(t + 1) * P], tmk[ps, t, 0, hc], zf[ps, u, HD:P], False, False, True)
                        last = mm(pe, M[4 + par][hs, t * P + HD:(t + 1) * P], tmk[ps, t, 1, hc], tmk[ps, t, 2, hc], False, False, True)
                    last.then_inc(sem("fg_mm"), 1)
                for u in range(4):
                    h, t = u % 2, u // 2
                    hs = slice(HD * h, HD * h + HD)
                    mm(pe, M[3][hs, t * P:(t + 1) * P], zf[:, u, HD:P], pr[:, u, 1, :], t == 0, False, True)
                    mm(pe, M[3][hs, t * P:(t + 1) * P], tmk[:, t, 2, HD * h:HD * h + HD], pr[:, u, 3, :], False, False, True)
            if front:
                project(pe, i, U_V, 1)
            for c in range(1, NCH):
                if back:
                    settle(pe)
                    past(pe, f"state{c - 1}", n)
                    if c == 1:
                        past(pe, "q_ready", n)
                        past(pe, "ft_ready", n)
                    t, par = c // 2, c % 2
                    for h in range(2):
                        hs = slice(HD * h, HD * h + HD)
                        last = mm(pe, M[4 + par][hs, t * P + HD:(t + 1) * P], fts[hs, c, :], zst[c - 1][hs, :], False, True, True)
                    last.then_inc(sem("state_mm"), 1)
                    for h in range(2):
                        hs = slice(HD * h, HD * h + HD)
                        last = mm(pe, M[3][hs, c * C:(c + 1) * C], zst[c - 1][hs, :], q[hs, c * C:(c + 1) * C], False, True, True)
                    if c == NCH - 1:
                        last.then_inc(sem("y_mm"), 1)
                if front:
                    project(pe, i, U_GS if c < 3 else U_GA, (c - 1) % 2)
            if back:
                settle(pe)
                past(pe, f"state{NCH - 1}", n)
                nc.tensor.transpose(M[0][0:HD, 0:P], zst[NCH - 1][:], ident[:]).then_inc(sem("zt_mm"), 1)
                past(pe, "y_copy", n)
                mm(pe, M[1][:, 0:TP], mean64[:], ys[:, 0:TP], True, True).then_inc(sem("ymean_mm"), 1)
                past(pe, "zt_copy", n)
            if front:
                done(pe, "q_rope", i)
                done(pe, "k_rope", i)
                mm(pe, M[4][:, 0:TP], kr[:, 0:P], qr[:, 0:TP], True, True)
                mm(pe, M[4][:, TP:TP + P], kr[:, P:TP], qr[:, P:TP], True, True).then_inc(sem("sc_mm"), 1)
                done(pe, "v_copy", i)
                for m, src in enumerate((kr[:, 0:P], kr[:, P:TP], vr[:, 0:P], vr[:, P:TP])):
                    last = nc.tensor.transpose(v4(M[3])[:, m, :], src, ident[:])
                last.then_inc(sem("kvt_mm"), 1)
                nc.tensor.transpose(M[0][0:B, 0:P], kr[:, TP:T], ident[:])
                nc.tensor.transpose(M[0][0:B, P:2 * P], vr[:, TP:T], ident[:]).then_inc(sem("kv8_mm"), 1)
                project(pe, i, U_GA, 1)
            if back:
                past(pe, "y_sq", n)
                mm(pe, M[2][:, 0:TP], mean64[:], ysq[:, 0:TP], True, True).then_inc(sem("yvar_mm"), 1)
            if front:
                done(pe, "sc_ready", i)
                done(pe, "kvt_copy", i)
                mm(pe, M[5][:, 0:TP], kvt[:, 2, :], sc[:, 0:TP], True, False, True)
                mm(pe, M[5][:, P:TP], kvt[:, 3, :], sc[:, TP:TP + P], False, True, True)
                done(pe, "vd_ready", i)
                mm(pe, M[4][:, 0:P], kvt[:, 0, :], vd[:, 0, :], True, False)
                mm(pe, M[4][:, 0:P], kvt[:, 1, :], vd[:, 1, :], False, True).then_inc(sem("stp_mm"), 1)
                done(pe, "vdiag_ready", i)
                vflat = vdiag[:].rearrange("b c d -> b (c d)")
                mm(pe, M[0][:, :], ks8[:, 0, :], vflat[:, 0:512], True, True)
                mm(pe, M[3][:, :], ks8[:, 0, :], vflat[:, 512:1024], True, True).then_inc(sem("kv_mm"), 1)
                project(pe, i, U_GB, 0)
                done(pe, "snew_ready", i)
                for b in range(B):
                    last = mm(pe, M[5][:, TP + b:TP + b + 1], snew[:, b, :], qr[:, TP + b:TP + b + 1], False, True, True)
                last.then_inc(sem("o_mm"), 1)
                project(pe, i, U_GB, 1)
                done(pe, "o_copy", i)
                mm(pe, M[0][:, 0:T], mean128[:], os_[:], True, True).then_inc(sem("omean_mm"), 1)

        wst = {"w": buf("wst_w", [P, P]), "ga": buf("wst_ga", [P, P]), "gb": buf("wst_gb", [LORA_G - P, P])}

        def act_pass(act, i, n):
            A = nc.scalar
            front, back = i is not None, n is not None

            def shifted(m, nm, use):
                projected(act, i, use)
                A.activation(mshift[m][:, 1:TX + 1], pj[use % 2][:, 0:TX], ACT.Copy, scale=pt[:, PX["mu_" + nm]:PX["mu_" + nm] + 1]).then_inc(sem(f"mu_{nm}"), 1)

            if front:
                ci = bass.ts(i, P)
                last_pass(act, "g_copy", i)
                A.copy(wst["w"][:], lowa[:, ci])
                A.copy(wst["ga"][:], g2a[:, ci])
                A.copy(wst["gb"][:], g2b[:, ci]).then_inc(sem("stage_lora"), 1)
            if back:
                past(act, "ovar_mm", n)
                A.activation(ors[:], M[3][:, 0:T], ACT.Sqrt, bias=eps[:, 0:1]).then_inc(sem("o_root"), 1)
            if front:
                done(act, "pt_ready", i)
                shifted(1, "k", U_RK)
            if back:
                for t in range(TT):
                    act.wait_ge(sem("tok_mm"), n * TT + (t + 1 - TT))
                    A.copy(rhs[:, 2 * t:2 * t + 2, 0, :], M[4 + t][:, 0:P].rearrange("p (h c) -> p h c", h=2))
                    A.copy(tmk[:, t], M[4 + t][:, P:4 * P].rearrange("p (n c) -> p n c", n=3)).then_inc(sem(f"tok_copy{t}"), 1)
            if front:
                done(act, "kk0_ready", i)
                A.activation(kks[:], kk0[:], ACT.Square).then_inc(sem("kk_sq"), 1)
                projected(act, i, U_W)
                A.activation(thw[:], pj[1][:, 0:T], ACT.Tanh, scale=0.5, bias=pt[:, PX["w0h"]:PX["w0h"] + 1]).then_inc(sem("w_tanh"), 1)
                projected(act, i, U_A)
                A.activation(tha[:], pj[0][:, 0:T], ACT.Tanh, scale=0.5, bias=pt[:, PX["a0h"]:PX["a0h"] + 1]).then_inc(sem("a_tanh"), 1)
                shifted(0, "r", U_R)
            if back:
                past(act, "a2_mm", n)
                A.copy(a2[:], v4(M[0])).then_inc(sem("a2_copy"), 1)
                past(act, "lakv_mm", n)
                A.copy(rhs[:, :, 1, :], M[4][:, 0:4 * HD].rearrange("p (u c) -> p u c", u=4)).then_inc(sem("rhs_ready"), 1)
                past(act, "at4w1_mm", n)
                for half in range(2):
                    last = A.copy(at4w[:, 2 * half:2 * half + 2, 0, :], M[2 + half][:].rearrange("p (u a c) -> p u a c", u=2, a=2)[:, :, 0, :])
                last.then_inc(sem("at4_copy"), 1)
                past(act, "a4_mm", n)
                A.copy(a4[:], v4(M[0])).then_inc(sem("a4_copy"), 1)
            if front:
                shifted(2, "v", U_RV)
            if back:
                past(act, "a8_mm", n)
                A.copy(a8[:], v4(M[5])).then_inc(sem("a8_copy"), 1)
            if front:
                projected(act, i, U_KK)
                A.activation(kkn[:], pj[1][:, 0:T], ACT.Sqrt).then_inc(sem("kk_root"), 1)
                done(act, "lp_ready", i)
                A.activation(ep[:], lp[:], ACT.Exp)
                A.activation(en[:], lp[:], ACT.Exp, scale=-1.0)
                done(act, "lpx_ready", i)
                A.activation(epx[:], lpx[:], ACT.Exp).then_inc(sem("exp_ready"), 1)
            if back:
                past(act, "nt_mm", n)
                A.copy(nt[:], v4(M[3])).then_inc(sem("nt_copy"), 1)
            if front:
                projected(act, i, U_G)
                A.copy(gg[:], pj[0][:, 0:T]).then_inc(sem("g_copy"), 1)
                projected(act, i, U_V)
                A.copy(vr[:], pj[0][:, 0:T]).then_inc(sem("v_copy"), 1)
                projected(act, i, U_GS)
                A.activation(thg[:], pj[1][:, 0:T], ACT.Tanh, scale=0.5).then_inc(sem("gs_tanh"), 1)
            if back:
                past(act, "y_mm", n)
                A.copy(ys[:, 0:TP], M[3][:, 0:TP]).then_inc(sem("y_copy"), 1)
                past(act, "zt_mm", n)
                act.wait_ge(sem("zout_free"), n)
                A.copy(zout[:], M[0][0:HD, 0:P].rearrange("p (h c) -> p h c", h=2)).then_inc(sem("zt_copy"), 1)
            if front:
                done(act, "kvt_mm", i)
                A.copy(kvt[:], v4(M[3])).then_inc(sem("kvt_copy"), 1)
                done(act, "kv8_mm", i)
                A.copy(ks8[:], M[0][0:B, 0:2 * P].rearrange("p (n c) -> p n c", n=2)).then_inc(sem("ks8_ready"), 1)
            if back:
                past(act, "yc_ready", n)
                A.activation(ysq[:, 0:TP], yc[:, 0:TP], ACT.Square).then_inc(sem("y_sq"), 1)
            if front:
                projected(act, i, U_GA)
                A.activation(ga[:], pj[0][:, 0:T], ACT.Tanh, scale=0.5).then_inc(sem("ga_tanh"), 1)
            if back:
                past(act, "yvar_mm", n)
                A.activation(yrs[:, 0:TP], M[2][:, 0:TP], ACT.Sqrt, bias=eps[:, 1:2]).then_inc(sem("y_root"), 1)
            if front:
                done(act, "stp_mm", i)
                last_pass(act, "stp_sent", i * 16)
                A.copy(stp[:], M[4][:, 0:P]).then_inc(sem("stp_ready"), 1)
                done(act, "o_mm", i)
                A.copy(os_[:], M[5][:, 0:T]).then_inc(sem("o_copy"), 1)
                projected(act, i, U_GB)
                A.activation(gb[:], pj[1][:, 0:T], ACT.Tanh, scale=0.5).then_inc(sem("gb_tanh"), 1)
                done(act, "oc_ready", i)
                A.activation(osq[:], oc[:], ACT.Square).then_inc(sem("o_sq"), 1)

        def dve_pass(dve, i, n):
            V = nc.vector
            front, back = i is not None, n is not None
            c2 = "p (t c) -> p t c"

            def meanwhile(first, last):
                if not front:
                    sample_steps(dve, first, last)

            def par(nm):
                return pt[:, PX[nm]:PX[nm] + 1]

            def self_wait(name):
                done(dve, name, i)

            def mix(m, nm, dst, use):
                done(dve, f"mu_{nm}", i)
                bank = pj[use % 2]
                V.scalar_tensor_tensor(out=dst[:, 0:TP], in0=bank[:, 0:TP], scalar=par("om_" + nm), in1=mshift[m][:, 0:TP], op0=mult, op1=add)
                V.scalar_tensor_tensor(out=dst[:, TP:T], in0=bank[:, TP:T], scalar=par("om_" + nm), in1=mshift[m][:, T + 1:TX + 1],
                                       op0=mult, op1=add).then_inc(sem(f"{nm}_mix"), 1)

            def rotary(nm, use, tabs, dst):
                projected(dve, i, use)
                bank = pj[use % 2]
                hf = P // 2
                V.tensor_tensor(ta[:], bank[:, 0:T], rope[:, tabs[0], :], mult)
                V.tensor_tensor(tb[0:hf, :], bank[hf:P, 0:T], rope[hf:P, tabs[1], :], mult)
                V.tensor_tensor(tb[hf:P, :], bank[0:hf, 0:T], rope[0:hf, tabs[1], :], mult).then_inc(sem("rotary_part"), 1)
                dve.wait_ge(sem("rotary_part"), i * 2 + (1 if nm == "q" else 2))
                V.tensor_tensor(dst[:], ta[:], tb[:], add).then_inc(sem(f"{nm}_rope"), 1)

            if front:
                last_pass(dve, "front_end", i)
                V.tensor_copy(pt[:], parc[:, :, bass.ds(i, 1)].rearrange("p n o -> p (n o)"))
                V.tensor_copy(dcol[:], retcol[:, bass.ds(i, 1), :].rearrange("p o n -> p (o n)")).then_inc(sem("pt_ready"), 1)
                self_wait("pt_ready")
            if back:
                past(dve, "o_root", n)
                V.reciprocal(ors[:], ors[:]).then_inc(sem("o_inv"), 1)
                past(dve, "o_inv", n)
                V.tensor_tensor(oc[:], oc[:], ors[:], mult).then_inc(sem("on"), 1)
                past(dve, "on", n)
                V.tensor_tensor(merged[:, bass.ds(n - 1, 1), 0:TP].rearrange("p o t -> p (o t)"), oc[:, 0:TP], sg[:, 0:TP], mult)
                V.tensor_tensor(spost[:, 2, bass.ds(n - 1, 1), :].rearrange("p o b -> p (o b)"), oc[:, TP:T], sg[:, TP:T], mult).then_inc(sem("ret_out"), 1)
            if front:
                mix(1, "k", kx, U_RK)
                self_wait("k_mix")
                V.tensor_scalar(kk0[:], kx[:], par("k_k"), None, mult).then_inc(sem("kk0_ready"), 1)
            if back:
                for u in range(4):
                    dve.wait_ge(sem("prod"), n * 6 + (u - 5))
                    last = V.tensor_tensor(pr[:, u], v4(M[u]), mk[:], mult)
                last.then_inc(sem("masked"), 1)
                for h in range(2):
                    dve.wait_ge(sem("prod"), n * 6 + (h - 1))
                    src = M[4 + h][:, 0:TP].rearrange("p (t c) -> p t c", t=TT)
                    for m in range(2):
                        last = V.tensor_tensor(la[:, h::2, m, :], src, mlo[:, m:m + 1, :].broadcast_to([P, TT, P]), mult)
                last.then_inc(sem("l_masked"), 1)
                past(dve, "masked", n)
                V.tensor_tensor(at2w[:, :, 1, :], pr[:, :, 0, :], ident[:].unsqueeze(1).broadcast_to([P, 4, P]), add).then_inc(sem("w0_ready"), 1)
            if front:
                done(dve, "w_tanh", i)
                V.tensor_scalar(thw[:], thw[:], LOGW_C, LOGW_C, mult, add).then_inc(sem("lw_ready"), 1)
                done(dve, "a_tanh", i)
                V.tensor_scalar(tha[:], tha[:], 0.5, 0.5, mult, add).then_inc(sem("a_ready"), 1)
            if back:
                past(dve, "at2_mm", n)
                V.tensor_copy(at2w[:, :, 0, :], v4(M[1])).then_inc(sem("at2_copy"), 1)
            if front:
                mix(0, "r", r, U_R)
                self_wait("lw_ready")
                V.tensor_tensor_scan(lp[:], scanm[:], thw[:], 0.0, mult, add).then_inc(sem("lp_ready"), 1)
                self_wait("a_ready")
                V.tensor_scalar(kmod[:], tha[:], par("k_a"), par("om_ka"), mult, add).then_inc(sem("km_part"), 1)
            if back:
                past(dve, "w0_ready", n)
                past(dve, "at4_copy", n)
                for half in range(2):
                    us = slice(2 * half, 2 * half + 2)
                    last = V.tensor_tensor(at4w[:, us, 1, :], M[2 + half][:].rearrange("p (u a c) -> p u a c", u=2, a=2)[:, :, 1, :], at2w[:, us, 1, :], add)
                last.then_inc(sem("w1_ready"), 1)
                meanwhile(0, 1)
            if front:
                self_wait("km_part")
                V.tensor_tensor(kmod[:], kmod[:], kx[:], mult).then_inc(sem("kmod_ready"), 1)
                self_wait("lp_ready")
                V.tensor_tensor(lpx[:], lp[:], thw[:], sub).then_inc(sem("lpx_ready"), 1)
            if front:
                mix(2, "v", vx, U_RV)
            if back:
                past(dve, "w2_mm", n)
                past(dve, "w1_ready", n)
                V.tensor_tensor(w2s, v4(M[1]), at4w[:, :, 1, :], add).then_inc(sem("w2_ready"), 1)
                meanwhile(1, 2)
            if front:
                self_wait("kmod_ready")
                self_wait("r_mix")
                V.scalar_tensor_tensor(out=rkk[:], in0=r[:], scalar=par("r_k"), in1=kmod[:], op0=mult, op1=mult).then_inc(sem("rkk_ready"), 1)
            if back:
                past(dve, "w3_mm", n)
                past(dve, "w2_ready", n)
                V.tensor_tensor(w3, v4(M[2]), w2s, add).then_inc(sem("w3_ready"), 1)
                meanwhile(2, 3)
            if front:
                done(dve, "kk_root", i)
                V.tensor_scalar(kkn[:], kkn[:], 1e-12, None, ALU.max).then_inc(sem("kk_step"), 1)
                dve.wait_ge(sem("kk_step"), i * 3 + 1)
                V.reciprocal(kkn[:], kkn[:]).then_inc(sem("kk_step"), 1)
            if back:
                past(dve, "x0_mm", n)
                V.tensor_copy(x0[:], v4(M[4])).then_inc(sem("x0_copy"), 1)
                meanwhile(3, 4)
            if front:
                rotary("q", U_Q, (0, 1), qr)
            if back:
                past(dve, "x0_copy", n)
                dve.wait_ge(sem("horner_mm"), n * 3 - 2)
                V.tensor_tensor(z1[:], v4(M[5]), x0[:], add).then_inc(sem("z1_ready"), 1)
                meanwhile(4, 5)
            if front:
                self_wait("q_rope")
                rotary("k", U_K, (2, 3), kr)
            if back:
                dve.wait_ge(sem("horner_mm"), n * 3 - 1)
                V.tensor_tensor(z2[:], v4(M[0]), x0[:], add).then_inc(sem("z2_ready"), 1)
                meanwhile(5, 6)
            if front:
                dve.wait_ge(sem("kk_step"), i * 3 + 2)
                V.tensor_tensor(kk[:], kk0[:], kkn[:], mult).then_inc(sem("kk_step"), 1)
                dve.wait_ge(sem("kk_step"), i * 3 + 3)
                V.tensor_tensor(ba[:], kk[:], tha[:], mult).then_inc(sem("ba_ready"), 1)
            if back:
                dve.wait_ge(sem("horner_mm"), n * 3)
                V.tensor_tensor(zf[:], v4(M[1]), x0[:], add).then_inc(sem("zf_ready"), 1)
                meanwhile(6, 7)
            if front:
                projected(dve, i, U_BON)
                self_wait("v_mix")
                V.tensor_tensor(bonus[:], pj[U_BON % 2][:, 0:T], vx[:], mult).then_inc(sem("bonus_sum"), 1)
            if back:
                past(dve, "q_mm", n)
                V.tensor_tensor(q[:].rearrange(c2, t=TT), M[2][:, 0:TP].rearrange(c2, t=TT), ar[:, :, 1, :], add).then_inc(sem("q_ready"), 1)
                for par_ in range(2):
                    dve.wait_ge(sem("fg_mm"), n * 2 + (par_ - 1))
                    last = V.tensor_tensor(fts[:, par_::2, :], M[4 + par_][:, 0:TP].rearrange("p (t a c) -> p t a c", t=TT, a=2)[:, :, 0, :],
                                           cst["c_id64"][:].unsqueeze(1).broadcast_to([P, TT, HD]), add)
                last.then_inc(sem("ft_ready"), 1)
            for c in range(NCH):
                if back:
                    if c:
                        dve.wait_ge(sem("state_mm"), n * (NCH - 1) + (c + 1 - NCH))
                    t, par_ = c // 2, c % 2
                    V.tensor_scalar(zst[c][:], M[4 + par_][:, t * P + HD:(t + 1) * P], epc[:, c:c + 1], None, mult).then_inc(sem(f"state{c}"), 1)
                if front:
                    if c == 0:
                        self_wait("ba_ready")
                        done(dve, "exp_ready", i)
                        V.scalar_tensor_tensor(out=ar[:, :, 0, :], in0=kk[:, 0:TP].rearrange(c2, t=TT), scalar=-1.0,
                                               in1=epx[:, 0:TP].rearrange(c2, t=TT), op0=mult, op1=mult)
                    elif c == 1:
                        V.tensor_tensor(ar[:, :, 1, :], r[:, 0:TP].rearrange(c2, t=TT), ep[:, 0:TP].rearrange(c2, t=TT), mult)
                    elif c == 2:
                        V.tensor_tensor(bt[:], ba[:, 0:TP], en[:, 0:TP], mult)
                    else:
                        V.tensor_tensor(kt[:], kmod[:, 0:TP], en[:, 0:TP], mult).then_inc(sem("abkr_ready"), 1)
            if front:
                done(dve, "sc_mm", i)
                V.tensor_tensor(sc[:], M[4][:, 0:TP + P], retdec[:, bass.ds(i, 1), :].rearrange("p o n -> p (o n)"), mult).then_inc(sem("sc_ready"), 1)
            if back:
                past(dve, "ymean_mm", n)
                V.tensor_tensor(yc[:, 0:TP], ys[:, 0:TP], M[1][:, 0:TP], sub).then_inc(sem("yc_ready"), 1)
                meanwhile(7, 9)
            if front:
                done(dve, "kvt_copy", i)
                V.tensor_scalar(vd[:, 0, :], kvt[:, 2, :], dcol[:, 0:1], None, mult)
                V.tensor_scalar(vd[:, 1, :], kvt[:, 3, :], dcol[:, 1:2], None, mult).then_inc(sem("vd_ready"), 1)
                done(dve, "ks8_ready", i)
                V.tensor_tensor(vdiag[:], ks8[:, 1:2, :].broadcast_to([B, B, P]), diag8[:], mult).then_inc(sem("vdiag_ready"), 1)
                done(dve, "gs_tanh", i)
                V.scalar_tensor_tensor(out=sg[:], in0=thg[:], scalar=1.0, in1=pj[U_GS % 2][:, 0:T], op0=add, op1=mult).then_inc(sem("gs_silu"), 1)
            if back:
                past(dve, "y_root", n)
                V.reciprocal(yrs[:, 0:TP], yrs[:, 0:TP]).then_inc(sem("y_inv"), 1)
            if front:
                dve.wait_ge(sem("sin_in"), 16 * (i + 1))
                last_pass(dve, "snew_sent", 16 * i)
                done(dve, "kv_mm", i)
                for half, bank in enumerate((M[0], M[3])):
                    bs = slice(4 * half, 4 * half + 4)
                    last = V.scalar_tensor_tensor(out=snew[:, bs, :], in0=sin_[:, bs, :], scalar=dcol[:, 2:3], in1=v4(bank), op0=mult, op1=add)
                last.then_inc(sem("snew_ready"), 1)
                for m, src in enumerate((r, ep, kmod, vx, kk, ba)):
                    V.tensor_copy(svec[:, bass.ds(i, 1), m, :].rearrange("p o b -> p (o b)"), src[:, TP:T]).then_inc(sem("svec_part"), 1)
            if back:
                past(dve, "y_inv", n)
                V.tensor_tensor(yc[:, 0:TP], yc[:, 0:TP], yrs[:, 0:TP], mult).then_inc(sem("y_step"), 1)
                dve.wait_ge(sem("y_step"), n * 3 - 2)
                V.tensor_tensor(yc[:, 0:TP], yc[:, 0:TP], ygate[:], mult).then_inc(sem("y_step"), 1)
                dve.wait_ge(sem("y_step"), n * 3 - 1)
                V.tensor_tensor(yc[:, 0:TP], yc[:, 0:TP], ybias[:], add).then_inc(sem("y_step"), 1)
                dve.wait_ge(sem("y_step"), n * 3)
                tile = merged[:, bass.ds(n - 1, 1), 0:TP].rearrange("p o t -> p (o t)")
                V.tensor_tensor(tile, tile, yc[:, 0:TP], add).then_inc(sem("prompt_merged"), 1)
            if front:
                if back:
                    past(dve, f"state{NCH - 1}", n)
                V.tensor_copy(epc[:], ep[:, C - 1:TP:C])
                done(dve, "gb_tanh", i)
                V.tensor_scalar(ga[:], ga[:], 0.25, 0.25, mult, add)
                V.tensor_scalar(gb[:], gb[:], 0.5, 0.5, mult, add).then_inc(sem("gates_ready"), 1)
                self_wait("gates_ready")
                self_wait("gs_silu")
                V.scalar_tensor_tensor(out=sg[:], in0=sg[:], scalar=par("gn_w"), in1=ga[:], op0=mult, op1=mult)
                V.tensor_tensor(gg[:], gg[:], gb[:], mult).then_inc(sem("rgate_ready"), 1)
                done(dve, "omean_mm", i)
                V.tensor_tensor(oc[:], os_[:], M[0][:, 0:T], sub).then_inc(sem("oc_ready"), 1)
                self_wait("rgate_ready")
                self_wait("bonus_sum")
                V.tensor_scalar(ygate[:], gg[:, 0:TP], par("lnx_w"), None, mult)
                V.scalar_tensor_tensor(out=ybias[:], in0=bonus[:, 0:TP], scalar=par("lnx_b"), in1=gg[:, 0:TP], op0=add, op1=mult)
                V.tensor_copy(spost[:, 0, bass.ds(i, 1), :].rearrange("p o b -> p (o b)"), bonus[:, TP:T])
                V.tensor_copy(spost[:, 1, bass.ds(i, 1), :].rearrange("p o b -> p (o b)"), gg[:, TP:T]).then_inc(sem("front_end"), 1)

        def sp_pass(sp, i):
            if not isinstance(i, int):
                for use, s in slot_of.items():
                    settle(sp)
                    past(sp, emptied[use], i)
                    sp.dma_start(wslot[s], w_in[:, :, bass.ds(i * P + SECTIONS[s], P)]).then_inc(sem(f"w_in{s}"), 16)
            last_pass(sp, "snew_ready", i)
            sp.dma_start(sin_, a["state_ret"][0].rearrange("b h k v -> k h b v")[:, bass.ds(i, 1), :, :].rearrange("k o b v -> k (o b) v")).then_inc(sem("sin_in"), 16)

        def out_pass(eng, i, n):
            if n is not None:
                settle(eng)
                past(eng, "zt_copy", n)
                eng.dma_start(o["rwkv_p"][0, 0].rearrange("h v k -> v h k")[:, bass.ds(n * 2 - 2, 2), :], zout[:]).then_inc(sem("zout_sent"), 16)
                eng.wait_ge(sem("zout_sent"), 16 * n)
                eng.sem_inc(sem("zout_free"), 1)
            if i is not None:
                settle(eng)
                done(eng, "stp_ready", i)
                eng.dma_start(o["ret_p"][0, 0][bass.ds(i, 1)].rearrange("o k v -> (o k) v"), stp[:]).then_inc(sem("stp_sent"), 16)
                settle(eng)
                done(eng, "snew_ready", i)
                eng.dma_start(o["ret_s"][0].rearrange("b h k v -> k h b v")[:, bass.ds(i, 1), :, :].rearrange("k o b v -> k (o b) v"), snew).then_inc(sem("snew_sent"), 16)

        scr_vec = nc.dram_tensor("scr_vec", [NV, D], F32, kind="Internal").ap()
        scr_y = nc.dram_tensor("scr_y", [P, HD], F32, kind="Internal").ap()
        SIZE = [P, P, B]

        def w_out_part(pe, tt, kks):
            rows = slice(0, SIZE[tt])
            for kk_ in kks:
                for hf in range(2):
                    last = mm(pe, psum[2 * tt + hf][rows, :], merged[:, kk_, tt * P:tt * P + SIZE[tt]], wall[:, kk_, hf * 512:(hf + 1) * 512],
                              kk_ == 0, kk_ == KT - 1, True)
            return last

        def sp_tail(sp):
            wo = a["w_out"][0].rearrange("(k p) c -> p k c", p=P)
            for use, s in slot_of.items():
                if s < KT:
                    projected(sp, KT - 1, use)
                    sp.dma_start(wall[:, s, :], wo[:, s, :]).then_inc(sem("wout_in"), 16)
            sp.wait_ge(sem("stage_lora"), KT)
            sp.wait_ge(sem("snew_ready"), KT)
            sp.dma_start(st.rearrange("p v k -> p (v k)"), a["state_rwkv"][0].rearrange("b h v k -> (b h) (v k)")).then_inc(sem("st_in"), 16)
            sp.wait_ge(sem("stok_ready"), 2)
            sp.dma_start(scr_vec, stok).then_inc(sem("scr_vec_in"), 16)
            sp.wait_ge(sem("scr_vec_in"), 16)
            sp.dma_start(vec, scr_vec.rearrange("(v b) (h c) -> (b h) v c", b=B, c=HD)).then_inc(sem("vec_in"), 16)
            sp.wait_ge(sem("y_mm"), KT)
            sp.dma_start(keep["x"][:, 0:2, :], a["x_prompt"][0].rearrange("(t p) d -> p t d", p=P)).then_inc(sem("x2_in"), 16)
            sp.dma_start(keep["x"][0:B, 2, :], a["x_sample"].rearrange("b t d -> (b t) d")).then_inc(sem("x2_in"), 16)
            sp.dma_start(gbc[:], a["norm_ffn"].partition_broadcast(P)).then_inc(sem("x2_in"), 16)
            sp.wait_ge(sem("sample_step"), DVE_SLICES * STEPS)
            sp.wait_ge(sem("pool_state"), 1)
            sp.dma_start(scr_y, y1).then_inc(sem("scr_y_in"), 16)
            sp.wait_ge(sem("scr_y_in"), 16)
            sp.dma_start(ytok, scr_y.rearrange("(b h) c -> b (h c)", b=B)).then_inc(sem("ytok_in"), 16)
            sp.dma_start(o["rwkv_s"][0].rearrange("b h v k -> (b h) (v k)"), st.rearrange("p v k -> p (v k)")).then_inc(sem("rwkv_s_out"), 16)
            sp.wait_ge(sem("rwkv_s_out"), 16)
            sp.wait_ge(sem("x2_in"), 48)

        def pe_samples_in(pe):
            pe.wait_ge(sem("svec_part"), 6 * KT)
            pe.wait_ge(sem("gb_tanh"), KT)
            for kk_ in range(KT):
                last = nc.tensor.transpose(psum[kk_ // 4][0:NV, (kk_ % 4) * P:(kk_ % 4 + 1) * P], svec[:, kk_].rearrange("p v b -> p (v b)"), ident[:])
                if kk_ % 4 == 3:
                    last.then_inc(sem("sv_mm"), 1)

        def pe_tail(pe):
            past(pe, "yc_ready", KT)
            w_out_part(pe, 1, range(KT - 1))
            pe.wait_ge(sem("prompt_merged"), KT)
            w_out_part(pe, 0, [KT - 1]).then_inc(sem("wo_mm"), 1)
            w_out_part(pe, 1, [KT - 1]).then_inc(sem("wo_mm"), 1)
            pe.wait_ge(sem("ytok_in"), 16)
            for kk_ in range(KT):
                last = nc.tensor.transpose(psum[6][:, kk_ * B:(kk_ + 1) * B], ytok[:, kk_ * P:(kk_ + 1) * P], ident[0:B, 0:B])
            last.then_inc(sem("sy_mm"), 1)
            pe.wait_ge(sem("sy_ready"), 1)
            mm(pe, psum[7][:, 0:KT * B], mean64[:], sy.rearrange("p k b -> p (k b)"), True, True).then_inc(sem("symean"), 1)
            pe.wait_ge(sem("sysq_ready"), 1)
            mm(pe, psum[6][:, 0:KT * B], mean64[:], sysq.rearrange("p k b -> p (k b)"), True, True).then_inc(sem("syvar"), 1)
            pe.wait_ge(sem("merged_all"), 1)
            w_out_part(pe, 2, range(KT))

        def act_samples_in(act):
            act.wait_ge(sem("sv_mm"), 1)
            projected(act, KT - 1, U_GB)
            nc.scalar.copy(stok[:, 0:512], psum[0][0:NV, :]).then_inc(sem("stok_ready"), 1)

        def act_tail(act):
            act.wait_ge(sem("sy_mm"), 1)
            nc.scalar.copy(sy.rearrange("p k b -> p (k b)"), psum[6][:, 0:KT * B]).then_inc(sem("sy_ready"), 1)
            act.wait_ge(sem("syc_ready"), 1)
            nc.scalar.activation(sysq, syc, ACT.Square).then_inc(sem("sysq_ready"), 1)
            act.wait_ge(sem("syvar"), 1)
            nc.scalar.activation(syr.rearrange("p k b -> p (k b)"), psum[6][:, 0:KT * B], ACT.Sqrt, bias=eps[:, 1:2]).then_inc(sem("syroot"), 1)
            act.wait_ge(sem("wout_in"), 16 * KT)
            act.wait_ge(sem("projected"), KT * USES)
            for tt in range(TT):
                act.wait_ge(sem("x1_ready"), tt + 1)
                if tt:
                    act.wait_ge(sem("x1_sq"), tt)
                nc.scalar.activation(wall[:, KT, :], keep["x"][:, tt, :], ACT.Square, accum_out=keep["xstat"][:, tt, 0:1]).then_inc(sem("x1_sq"), 1)
            act.wait_ge(sem("x1_sq"), TT)
            nc.scalar.activation(keep["xstat"][:, 0:TT, 1:2], keep["xstat"][:, 0:TT, 0:1], ACT.Sqrt, scale=1.0 / D, bias=eps[:, 2:3]).then_inc(sem("x1_root"), 1)

        DVE_SLICES, POOL_SLICES, SLICE, STEPS, HIDDEN = 2, 2, 16, 9, 9

        def state_step(E, part, step):
            vs = slice(part * SLICE, (part + 1) * SLICE)

            def key(m):
                return vec[:, m, :].unsqueeze(1).broadcast_to([P, SLICE, HD])

            def value(v):
                return v[:, vs].unsqueeze(2).broadcast_to([P, SLICE, HD])

            s_, p_ = st[:, vs, :], prod[:, vs, :]
            if step in (0, 7):
                return E.tensor_tensor(p_, s_, key(4 if step == 0 else 0), mult)
            if step in (1, 8):
                return E.tensor_reduce((sa if step == 1 else y1)[:, vs], p_, AX_X, add)
            if step == 2:
                return E.tensor_tensor(s_, s_, key(1), mult)
            if step == 3:
                return E.tensor_tensor(p_, value(sa), key(5), mult)
            if step == 5:
                return E.tensor_tensor(p_, value(vec[:, 3, :]), key(2), mult)
            return E.tensor_tensor(s_, s_, p_, sub if step == 4 else add)

        def sample_steps(dve, first, last):
            for step in range(first, last):
                if step == 0:
                    dve.wait_ge(sem("st_in"), 16)
                    dve.wait_ge(sem("vec_in"), 16)
                    dve.wait_ge(sem("projected"), KT * USES)
                else:
                    dve.wait_ge(sem("sample_step"), step)
                state_step(nc.vector, step // STEPS, step % STEPS).then_inc(sem("sample_step"), 1)

        def pool_tail(pool):
            pool.wait_ge(sem("st_in"), 16)
            pool.wait_ge(sem("vec_in"), 16)
            pool.wait_ge(sem("projected"), KT * USES)
            pool.wait_ge(sem("ret_out"), KT)
            count = 0
            for part in range(DVE_SLICES, DVE_SLICES + POOL_SLICES):
                vs = slice(part * SLICE, (part + 1) * SLICE)
                for step in range(STEPS):
                    if step in (1, 8):
                        half = HD // 2
                        while half:
                            out = (sa if step == 1 else y1)[:, vs].unsqueeze(2) if half == 1 else prod[:, vs, 0:half]
                            nc.gpsimd.tensor_tensor(out, prod[:, vs, 0:half], prod[:, vs, half:2 * half], add).then_inc(sem("pool_step"), 1)
                            count += 1
                            pool.wait_ge(sem("pool_step"), count)
                            half //= 2
                    else:
                        state_step(nc.gpsimd, part, step).then_inc(sem("pool_step"), 1)
                        count += 1
                        pool.wait_ge(sem("pool_step"), count)
            pool.sem_inc(sem("pool_state"), 1)

        def dve_samples_in(dve):
            dve.wait_ge(sem("sv_mm"), 2)
            nc.vector.tensor_copy(stok[:, 512:1024], psum[1][0:NV, :]).then_inc(sem("stok_ready"), 1)

        def dve_tail(dve):
            V = nc.vector
            step = [DVE_SLICES * STEPS]

            def then(ins):
                step[0] += 1
                ins.then_inc(sem("sample_step"), 1)
                dve.wait_ge(sem("sample_step"), step[0])

            sample_steps(dve, HIDDEN, DVE_SLICES * STEPS)
            V.memset(keep["xstat"][:], 1.0)
            dve.wait_ge(sem("x2_in"), 48)
            for tt in range(TT):
                dve.wait_ge(sem("wo_mm"), tt + 1)
                for hf in range(2):
                    hc = slice(hf * 512, (hf + 1) * 512)
                    last = V.tensor_tensor(keep["x"][:, tt, hc], keep["x"][:, tt, hc], psum[2 * tt + hf][:], add)
                last.then_inc(sem("x1_ready"), 1)
            dve.wait_ge(sem("symean"), 1)
            V.tensor_tensor(syc.rearrange("p k b -> p (k b)"), sy.rearrange("p k b -> p (k b)"), psum[7][:, 0:KT * B], sub).then_inc(sem("syc_ready"), 1)
            dve.wait_ge(sem("syroot"), 1)
            then(V.reciprocal(syr, syr))
            then(V.tensor_tensor(syc, syc, syr, mult))

            def chan(m):
                return parc[:, PX[m], :].unsqueeze(2).broadcast_to([P, KT, B])

            then(V.tensor_tensor(syc, syc, chan("lnx_w"), mult))
            then(V.tensor_tensor(syc, syc, chan("lnx_b"), add))
            then(V.tensor_tensor(syc, syc, spost[:, 0], add))
            then(V.tensor_tensor(syc, syc, spost[:, 1], mult))
            V.tensor_tensor(merged[:, :, TP:T], syc, spost[:, 2], add).then_inc(sem("merged_all"), 1)
            stat = keep["xstat"]
            dve.wait_ge(sem("x1_root"), 1)
            then(V.reciprocal(stat[:, 0:TT, 2:3], stat[:, 0:TT, 1:2]))
            for tt in range(TT):
                V.scalar_tensor_tensor(out=keep["xn"][:, tt, :], in0=keep["x"][:, tt, :], scalar=stat[:, tt, 2:3], in1=gbc[:],
                                       op0=mult, op1=mult)

        with nc.Block() as block:

            @block.sync
            def _(sp):
                sp_pass(sp, 0)
                with sp.Fori(1, KT) as i:
                    sp_pass(sp, i)
                sp_tail(sp)

            @block.gpsimd
            def _(pool):
                for m in mshift:
                    last = nc.gpsimd.memset(m[:, 0:1], 0.0)
                last.then_inc(sem("mshift_zero"), 1)
                pool.sem_inc(sem("zout_free"), 1)
                out_pass(pool, 0, None)
                with pool.Fori(1, KT) as i:
                    out_pass(pool, i, i)
                pool_tail(pool)
                out_pass(pool, None, KT)
                for nm in ("stp_sent", "snew_sent"):
                    pool.wait_ge(sem(nm), 16 * KT)
                pool.wait_ge(sem("zout_free"), KT + 1)

            @block.scalar
            def _(act):
                act_pass(act, 0, None)
                with act.Fori(1, KT) as i:
                    act_pass(act, i, i)
                act_samples_in(act)
                act_pass(act, None, KT)
                act_tail(act)

            @block.vector
            def _(dve):
                dve.wait_ge(sem("mshift_zero"), 1)
                dve_pass(dve, 0, None)
                with dve.Fori(1, KT) as i:
                    dve_pass(dve, i, i)
                dve_samples_in(dve)
                dve_pass(dve, None, KT)
                dve_tail(dve)

            @block.tensor
            def _(pe):
                pe_pass(pe, 0, None, wst)
                with pe.Fori(1, KT) as i:
                    pe_pass(pe, i, i, wst)
                pe_samples_in(pe)
                pe_pass(pe, None, KT, wst)
                pe_tail(pe)


def moe_phase(nc, a, o, k, alloc, sem, psum, cst, keep):
    mult, add, sub = ALU.mult, ALU.add, ALU.subtract
    SIZE = [P, P, B]
    with ExitStack() as ctx:
        sb = {}

        def buf(name, shape, dt=F32):
            return alloc(ctx, sb, name, shape, dt)

        ident, tri, ones, slot = (cst["c_" + n] for n in ("ident", "tri", "ones", "slot"))
        x, xn, stat, eps = keep["x"], keep["xn"], keep["xstat"], keep["eps"]
        PIECE = KT * DE
        RING = 8
        ring = buf("ring", [P, RING * PIECE])
        hi_gu, lo_gu = ([buf(f"{nm}{n}", [P, 2 * PIECE], F32R) for n in range(2)] for nm in ("hi_gu", "lo_gu"))
        hi_d, lo_d = ([buf(f"{nm}{n}", [P, PIECE], F32R) for n in range(2)] for nm in ("hi_d", "lo_d"))
        FIRST_LATE = 6
        xnt = ring[:, FIRST_LATE * PIECE:FIRST_LATE * PIECE + KT * T].rearrange("p (k t) -> p k t", k=KT)
        gffn = ring[:, (RING - 1) * PIECE + D:(RING - 1) * PIECE + 2 * D]
        gfin = gffn
        yth, ytl = (hi_gu[1][:, n * D:(n + 1) * D] for n in range(2))
        junk = hi_gu[0][:, 0:D]
        xgh, xgl = (buf(nm, [P, KT, SLOTS], F32R) for nm in ("xgh", "xgl"))
        rw = buf("rw", [P, KT, NG + NE])
        rb = buf("rb", [P, NG + NE])
        lg = buf("lg", [P, 3, NG + NE])
        gpad = buf("gpad", [P, 3, 8])
        top, topi, topf = buf("topv", [P, 3, 8]), buf("topi", [P, 3, 8], mybir.dt.uint32), buf("topf", [P, 3, 8])
        gmask = buf("gmask", [P, 3, NG + 1])
        gexp, gsum = buf("gexp", [P, 3, NG]), buf("gsum", [P, 3, 4])
        esel, eprod = buf("esel", [P, 3, 8]), buf("eprod", [P, 3, 8, NG])
        tw = buf("tw", [P, 3, 4])
        c8, c8b = buf("c8", [P, 3, 8]), buf("c8b", [P, 3, 8])
        comb = buf("comb", [P, 3, NG + 1, EPG])
        pos = buf("pos", [P, 3, NG + 1])
        cnt = buf("cnt", [P, 4])
        rounds_i = buf("rounds_i", [P, 1], I32)
        pcol, mcol, cg = buf("pcol", [P, 3]), buf("mcol", [P, 3]), buf("cg", [P, 3, EPG])
        G = buf("G", [P, 3, SLOTS])
        GT = buf("GT", [SLOTS, 3 * P], F32R)
        cslot = buf("cslot", [SLOTS, EPG])
        th = [buf(f"th{n}", [SLOTS, DE]) for n in range(2)]
        hs = hx = th
        hh = [buf(f"hh{n}", [P, DE // P, SLOTS], F32R) for n in range(2)]
        hl = [buf(f"hl{n}", [P, DE // P, SLOTS], F32R) for n in range(2)]
        MB = [psum[4], psum[5]]
        YB = [psum[6], psum[7]]
        HT = [psum[2], psum[3]]

        def rows(tt):
            return slice(0, SIZE[tt])

        def cols(tt):
            return slice(tt * P, tt * P + SIZE[tt])

        with nc.Block() as block:

            GU0, D0 = EPG, EPG // 2

            def settle(eng):
                eng.wait_ge(sem("rounds_ready"), 1)

            def load_group(sp, g, n, pieces=3 * EPG):
                for j in range(pieces):
                    e, m, k_ = j // 3, j % 3, j % RING
                    e0, m0 = (j - RING) // 3, (j - RING) % 3
                    turn = (e0 + EPG) // 2 - EPG // 2
                    if j >= FIRST_LATE and j < RING:
                        sp.wait_ge(sem("logit_mm"), 1)
                    if m0 < 2:
                        sp.wait_ge(sem(f"lo_gu{e0 % 2}"), n * EPG + (2 * turn + m0 + 1 + GU0))
                    else:
                        sp.wait_ge(sem(f"lo_d{e0 % 2}"), n * (EPG // 2) + (turn + 1 + D0))
                    src = a[("expert_w_gate", "expert_w_up", "expert_w_down")[m]][0][bass.ds(g * EPG + e, 1)]
                    sp.dma_start(ring[:, k_ * PIECE:(k_ + 1) * PIECE].rearrange("p (k f) -> p k f", f=src.shape[-1]),
                                 src.rearrange("o (k p) f -> p (o k) f", p=P)).then_inc(sem(f"piece_in{k_}"), 16)

            @block.sync
            def _(sp):
                sp.dma_start(gffn[0:B, :], a["norm_ffn"].partition_broadcast(B)).then_inc(sem("gffn_in"), 16)
                sp.dma_start(rw[:, :, 0:NG], a["router_group_w"][0].rearrange("(k p) c -> p k c", p=P)).then_inc(sem("rw_in"), 16)
                sp.dma_start(rw[:, :, NG:NG + NE], a["router_expert_w"][0].rearrange("(k p) c -> p k c", p=P)).then_inc(sem("rw_in"), 16)
                sp.dma_start(rb[:, 0:NG], a["router_group_b"].partition_broadcast(P)).then_inc(sem("rw_in"), 16)
                sp.dma_start(rb[:, NG:NG + NE], a["router_expert_b"].partition_broadcast(P)).then_inc(sem("rw_in"), 16)
                with sp.Fori(0, NG) as g:
                    load_group(sp, g, g)
                sp.wait_ge(sem("rounds_ready"), 1)
                n_rounds = sp.value_load(rounds_i[0:1, 0:1], min_val=1, max_val=3)
                with sp.If(n_rounds > 1):
                    with sp.Fori(1, n_rounds) as rnd:
                        with sp.Fori(0, NG) as g:
                            load_group(sp, g, rnd * NG + g)
                load_group(sp, 0, n_rounds * NG, 3)
                sp.wait_ge(sem("lo_d1"), n_rounds * (NG * EPG // 2) + D0)
                sp.dma_start(gfin, a["norm_final"].rearrange("(o d) -> o d", o=1).partition_broadcast(P)).then_inc(sem("gfin_in"), 16)
                for tt in range(TT):
                    sp.wait_ge(sem("y_final"), tt + 1)
                    sp.dma_start(o["y_p"][0].rearrange("(t p) d -> p t d", p=P)[:, tt, :], xn[:, tt, :]).then_inc(sem("y_sent"), 16)
                sp.wait_ge(sem("y_final"), 3)
                sp.dma_start(o["y_s"].rearrange("b t d -> (b t) d"), xn[0:B, 2, :]).then_inc(sem("y_sent"), 16)
                sp.wait_ge(sem("y_sent"), 48)

            def loop(eng, group_pre, experts, group_post, round_start=None, round_end=None):
                eng.wait_ge(sem("rounds_ready"), 1)
                n_rounds = eng.value_load(rounds_i[0:1, 0:1], min_val=1, max_val=3)
                with eng.Fori(0, n_rounds) as rnd:
                    if round_start:
                        round_start(rnd)
                    with eng.Fori(0, NG) as g:
                        n = rnd * NG + g
                        group_pre(g, n)
                        experts(n, n + rnd + 2, g + 1)
                        group_post(n, n + rnd + 2)
                    if round_end:
                        round_end(rnd)

            def pair_turn(n, e):
                return n * (EPG // 2) + e // 2

            @block.tensor
            def _(pe):
                mm = nc.tensor.matmul

                def loose(out, lhsT, rhs, start, stop):
                    return nc.tensor.matmul(out, lhsT, rhs, start=start, stop=stop, skip_group_check=True)

                for kk in range(KT):
                    for tt in range(2):
                        at = (kk % 2) * TP + tt * P
                        last = nc.tensor.transpose(psum[kk // 2][:, at:at + P], xn[:, tt, kk * P:(kk + 1) * P], ident[:])
                    if kk % 2:
                        last.then_inc(sem("xnt_mm"), 1)
                pe.wait_ge(sem("rw_in"), 64)
                for tt in range(3):
                    if tt == 0:
                        pe.wait_ge(sem("xnt_copy"), KT // 2)
                    if tt == 2:
                        pe.wait_ge(sem("xn2_ready"), 1)
                        for kk in range(KT):
                            last = nc.tensor.transpose(psum[6][:, kk * B:(kk + 1) * B], xn[0:B, 2, kk * P:(kk + 1) * P], ident[0:B, 0:B])
                        last.then_inc(sem("xnt_samples_mm"), 1)
                        pe.wait_ge(sem("xnt_samples"), 1)
                    for kk in range(KT):
                        last = mm(psum[0][rows(tt), tt * 64:tt * 64 + NG + NE], xnt[:, kk, cols(tt)], rw[:, kk, :], start=(kk == 0), stop=(kk == KT - 1))
                last.then_inc(sem("logit_mm"), 1)
                pe.wait_ge(sem("gmask_ready"), 1)
                for tt in range(3):
                    m = SIZE[tt]
                    for u in range(tt):
                        mm(psum[1][0:m, tt * NG:(tt + 1) * NG], ones[:, 0:m], gmask[:, u, 0:NG], start=(u == 0), stop=False)
                    mm(psum[1][0:m, tt * NG:(tt + 1) * NG], tri[0:m, 0:m], gmask[0:m, tt, 0:NG], start=(tt == 0), stop=True)
                for tt in range(3):
                    last = mm(psum[1][:, 16:16 + NG], ones[rows(tt), :], gmask[rows(tt), tt, 0:NG], start=(tt == 0), stop=(tt == 2))
                last.then_inc(sem("pos_mm"), 1)

                def gather(n, ahead):
                    pe.wait_ge(sem("G_ready"), ahead)
                    for kk in range(KT):
                        for tt in range(3):
                            last = mm(psum[kk // 4][:, (kk % 4) * SLOTS:(kk % 4 + 1) * SLOTS], xn[rows(tt), tt, kk * P:(kk + 1) * P],
                                      G[rows(tt), tt, :], start=(tt == 0), stop=(tt == 2))
                    last.then_inc(sem("xg_mm"), 1)

                def round_start(rnd):
                    gather(0, rnd * (NG + 1) + 1)

                def group_pre(g, n):
                    for tt in range(3):
                        mm(HT[1][:, 0:EPG], G[rows(tt), tt, :], cg[rows(tt), tt, :], start=(tt == 0), stop=(tt == 2))
                    for tt in range(3):
                        last = nc.tensor.transpose(HT[0][:, cols(tt)], G[rows(tt), tt, :], ident[rows(tt), rows(tt)])
                    last.then_inc(sem("gt_mm"), 1)

                def gate_up(n, e, half, ahead):
                    p = e % 2
                    if half == 0:
                        if e == 0:
                            pe.wait_ge(sem("xg_low"), 2 * ahead - 2)
                        pe.wait_ge(sem(f"hi_gu_done{p}"), pair_turn(n, e) * 2 + 2)
                        if e < 2:
                            pe.wait_ge(sem("scat_add"), n * 6 + (3 + e))
                        pe.wait_ge(sem(f"h_full{p}"), pair_turn(n, e) + 1)
                    else:
                        pe.wait_ge(sem(f"lo_gu{p}"), pair_turn(n, e) * 2 + (2 + GU0))
                    for step in range(half * 12, half * 12 + 12):
                        m, kk = step // KT, step % KT
                        w, v = ((hi_gu, xgh), (hi_gu, xgl), (lo_gu, xgh))[m]
                        last = mm(MB[p][:, :], v[:, kk, :], w[p][:].rearrange("p (m k f) -> p m k f", m=2, k=KT)[:, :, kk, :],
                                  start=(step == 0), stop=(step == 3 * KT - 1))
                    if half:
                        last.then_inc(sem(f"gu_mm{p}"), 1)

                def turn_h(n, e):
                    p = e % 2
                    pe.wait_ge(sem(f"h_full{p}"), pair_turn(n, e) + 2)
                    for f in range(DE // P):
                        last = nc.tensor.transpose(HT[p][:, f * SLOTS:(f + 1) * SLOTS], hx[p][:, f * P:(f + 1) * P], ident[:])
                    last.then_inc(sem(f"ht_mm{p}"), 1)

                def down(n, e):
                    p = e % 2
                    pe.wait_ge(sem(f"h_ready{p}"), pair_turn(n, e) + 1)
                    pe.wait_ge(sem(f"lo_d{p}"), pair_turn(n, e) + (1 + D0))
                    for hf in range(2):
                        for f in range(DE // P):
                            for m, (w, v) in enumerate(((hi_d, hh), (hi_d, hl), (lo_d, hh))):
                                at = f * D + hf * 512
                                last = loose(YB[hf][:, :], v[p][:, f, :], w[p][:, at:at + 512], e == 0 and f == 0 and m == 0,
                                             e == EPG - 1 and f == DE // P - 1 and m == 2)
                        if e == EPG - 1 and hf == 0:
                            last.then_inc(sem("y_first"), 1)
                    last.then_inc(sem(f"down_mm{p}"), 1)

                def experts(n, ahead, following):
                    for e in range(EPG):
                        gate_up(n, e, 0, ahead)
                        if e:
                            turn_h(n, e - 1)
                        gate_up(n, e, 1, ahead)
                        if e:
                            down(n, e - 1)
                    turn_h(n, EPG - 1)
                    gather(n, ahead)
                    down(n, EPG - 1)

                def group_post(n, ahead):
                    pe.wait_ge(sem("yt_low"), 2 * n + 2)
                    for tt in range(3):
                        for hf in range(2):
                            bank = psum[2 + 2 * tt + hf]
                            hc = slice(hf * 512, (hf + 1) * 512)
                            mm(bank[:, :], GT[:, tt * P:(tt + 1) * P], yth[:, hc], start=True, stop=False)
                            mm(bank[:, :], GT[:, tt * P:(tt + 1) * P], ytl[:, hc], start=False, stop=True).then_inc(sem("scat_mm"), 1)
                    settle(pe)
                    pe.wait_ge(sem("scat_add"), n * 6 + (2 + 6))
                    pe.wait_ge(sem("xg_low"), 2 * ahead)

                loop(pe, group_pre, experts, group_post, round_start)

            @block.gpsimd
            def _(pool):
                for s in range(2):
                    pool.sem_inc(sem(f"lo_d{s}"), D0)
                def experts(n, ahead, following):
                    for e in range(EPG):
                        p, k_ = e % 2, (3 * e + 2) % RING
                        pool.wait_ge(sem(f"hi_d_done{p}"), pair_turn(n, e) + 1)
                        nc.gpsimd.tensor_tensor(lo_d[p][:], ring[:, k_ * PIECE:(k_ + 1) * PIECE], hi_d[p][:].bitcast(F32), sub).then_inc(sem(f"lo_d{p}"), 1)

                for m in range(2):
                    at = slice(m * PIECE, (m + 1) * PIECE)
                    pool.wait_ge(sem("hi_gu_done0"), m + 1)
                    nc.gpsimd.tensor_tensor(lo_gu[0][:, at], ring[:, at], hi_gu[0][:, at].bitcast(F32), sub).then_inc(sem("lo_gu0"), 1)

                loop(pool, lambda g, n: None, experts, lambda n, ahead: None)

            @block.scalar
            def _(act):
                A = nc.scalar
                act.wait_ge(sem("x1_ready"), 1)
                A.activation(junk[0:B, :], x[0:B, 2, :], ACT.Square, accum_out=stat[0:B, 2, 0:1]).then_inc(sem("x1_sq"), 1)
                act.wait_ge(sem("x1_sq"), 1)
                A.activation(stat[0:B, 2, 1:2], stat[0:B, 2, 0:1], ACT.Sqrt, scale=1.0 / D, bias=eps[0:B, 2:3]).then_inc(sem("x1_root"), 1)
                for b in (2, 3):
                    act.wait_ge(sem("xnt_mm"), b + 1)
                    A.copy(xnt[:, 2 * b:2 * b + 2, 0:TP], psum[b][:].rearrange("p (k t) -> p k t", k=2)).then_inc(sem("xnt_copy"), 1)
                def piece(n, e, m):
                    j = 3 * e + m
                    act.wait_ge(sem(f"piece_in{j % RING}"), 16 * (n * (3 * EPG // RING) + (j // RING + 1)))
                    return ring[:, (j % RING) * PIECE:(j % RING + 1) * PIECE]

                def high_gu(n, e):
                    p = e % 2
                    act.wait_ge(sem(f"gu_mm{p}"), pair_turn(n, e) + 1)
                    for m in range(2):
                        A.copy(hi_gu[p][:, m * PIECE:(m + 1) * PIECE], piece(n, e, m)).then_inc(sem(f"hi_gu_done{p}"), 1)

                def high_d(n, e):
                    p = e % 2
                    act.wait_ge(sem(f"down_mm{p}"), pair_turn(n, e) + 1)
                    A.copy(hi_d[p][:], piece(n, e, 2)).then_inc(sem(f"hi_d_done{p}"), 1)

                high_gu(0, 0)
                high_d(0, 0)
                act.wait_ge(sem("gdiff_ready"), 1)
                A.activation(gexp[:], gexp[:], ACT.Exp).then_inc(sem("gexp_ready"), 1)
                act.wait_ge(sem("ediff_ready"), 1)
                A.activation(tw[:, :, 1:2], tw[:, :, 0:1], ACT.Exp).then_inc(sem("eexp_ready"), 1)

                def gate(n, e):
                    p = e % 2
                    act.wait_ge(sem(f"gu_mm{p}"), pair_turn(n, e) + 2)
                    act.wait_ge(sem(f"h_full{p}"), pair_turn(n, e) + 1)
                    A.activation(th[p][:], MB[p][:, 0:DE], ACT.Tanh, scale=0.5).then_inc(sem(f"th_ready{p}"), 1)

                def high_h(n, e):
                    p = e % 2
                    act.wait_ge(sem(f"down_mm{p}"), pair_turn(n, e) + 1)
                    act.wait_ge(sem(f"ht_mm{p}"), pair_turn(n, e) + 1)
                    A.copy(hh[p][:], HT[p][:, 0:2 * SLOTS].rearrange("p (f s) -> p f s", f=2)).then_inc(sem(f"hh_ready{p}"), 1)

                def high_x(ahead):
                    act.wait_ge(sem("xg_mm"), ahead)
                    for hf in range(2):
                        A.copy(xgh[:, 4 * hf:4 * hf + 4, :], psum[hf][:].rearrange("p (k s) -> p k s", k=4)).then_inc(sem("xg_high"), 1)

                def round_start(rnd):
                    high_x(rnd * (NG + 1) + 1)

                def group_pre(g, n):
                    act.wait_ge(sem("gt_mm"), n + 1)
                    A.copy(GT[:, 0:T], HT[0][:, 0:T]).then_inc(sem("gt_copy"), 1)
                    high_gu(n, 1)
                    high_d(n, 1)

                def experts(n, ahead, following):
                    for e in range(EPG):
                        gate(n, e)
                        if e + 2 <= EPG:
                            high_gu(n, e + 2)
                        if e:
                            high_d(n, e + 1)
                        high_h(n, e)
                    high_x(ahead)

                def group_post(n, ahead):
                    for hf in range(2):
                        if hf == 0:
                            act.wait_ge(sem("y_first"), n + 1)
                        else:
                            act.wait_ge(sem("down_mm1"), n * (EPG // 2) + (EPG // 2 + 1))
                        A.copy(yth[:, hf * 512:(hf + 1) * 512], YB[hf][:, :]).then_inc(sem("yt_high"), 1)

                loop(act, group_pre, experts, group_post, round_start)
                act.wait_ge(sem("moe_done"), 1)
                for tt in range(3):
                    A.activation(junk[rows(tt), :], x[rows(tt), tt, :], ACT.Square, accum_out=stat[rows(tt), tt, 0:1]).then_inc(sem("x2_sq"), 1)
                    act.wait_ge(sem("x2_sq"), tt + 1)
                    A.activation(stat[rows(tt), tt, 1:2], stat[rows(tt), tt, 0:1], ACT.Sqrt, scale=1.0 / D, bias=eps[rows(tt), 2:3]).then_inc(sem("x2_root"), 1)

            @block.vector
            def _(dve):
                V = nc.vector
                step = [0]

                def then(ins):
                    step[0] += 1
                    ins.then_inc(sem("router_step"), 1)
                    dve.wait_ge(sem("router_step"), step[0])

                for hf in range(2):
                    hc = slice(hf * 512, (hf + 1) * 512)
                    last = V.tensor_tensor(x[0:B, 2, hc], x[0:B, 2, hc], psum[4 + hf][0:B, :], add)
                last.then_inc(sem("x1_ready"), 1)
                V.memset(gmask[:], 0.0)
                V.memset(cg[:], 0.0)
                V.memset(pos[:], 0.0)
                V.memset(comb[:], 0.0)
                V.tensor_scalar(GT[:, T:], ident[0:SLOTS, 0:3 * P - T], 0.0, None, mult)
                V.memset(lg[:], 0.0)
                V.memset(gpad[:], -3.0e38)
                for b in (0, 1):
                    dve.wait_ge(sem("xnt_mm"), b + 1)
                    V.tensor_copy(xnt[:, 2 * b:2 * b + 2, 0:TP], psum[b][:].rearrange("p (k t) -> p k t", k=2)).then_inc(sem("xnt_copy"), 1)
                dve.wait_ge(sem("x1_root"), 1)
                then(V.reciprocal(stat[0:B, 2, 2:3], stat[0:B, 2, 1:2]))
                dve.wait_ge(sem("gffn_in"), 16)
                V.scalar_tensor_tensor(out=xn[0:B, 2, :], in0=x[0:B, 2, :], scalar=stat[0:B, 2, 2:3],
                                       in1=gffn[0:B, :], op0=mult, op1=mult).then_inc(sem("xn2_ready"), 1)
                dve.sem_inc(sem("scat_add"), 6)
                for s in range(2):
                    dve.sem_inc(sem(f"lo_gu{s}"), GU0)
                    dve.sem_inc(sem(f"down_mm{s}"), 1)
                    dve.sem_inc(sem(f"h_full{s}"), 1)
                    dve.sem_inc(sem(f"gu_mm{s}"), 1)
                dve.wait_ge(sem("xnt_samples_mm"), 1)
                V.tensor_copy(xnt[:, :, TP:T], psum[6][:, 0:KT * B].rearrange("p (k b) -> p k b", k=KT)).then_inc(sem("xnt_samples"), 1)
                def low_gu(n, e, parts=(0, 1)):
                    p = e % 2
                    for m in parts:
                        k_ = (3 * e + m) % RING
                        at = slice(m * PIECE, (m + 1) * PIECE)
                        dve.wait_ge(sem(f"hi_gu_done{p}"), pair_turn(n, e) * 2 + (m + 1))
                        V.tensor_tensor(lo_gu[p][:, at], ring[:, k_ * PIECE:(k_ + 1) * PIECE], hi_gu[p][:, at].bitcast(F32), sub).then_inc(sem(f"lo_gu{p}"), 1)

                dve.wait_ge(sem("logit_mm"), 1)
                for tt in range(3):
                    last = V.tensor_tensor(lg[rows(tt), tt, :], psum[0][rows(tt), tt * 64:tt * 64 + NG + NE], rb[rows(tt), :], add)
                then(last)
                then(V.tensor_copy(gpad[:, :, 0:NG], lg[:, :, 0:NG]))
                for tt in range(3):
                    last = V.max(top[:, tt, :], gpad[:, tt, :])
                then(last)
                for tt in range(3):
                    last = V.max_index(topi[:, tt, :], top[:, tt, :], gpad[:, tt, :])
                then(last)
                then(V.tensor_copy(topf[:], topi[:]))
                for tt, m in enumerate(SIZE):
                    last = V.tensor_scalar(gmask[0:m, tt, 0:NG], slot[0:m, 0:NG], topf[0:m, tt, 0:1], None, ALU.is_equal)
                last.then_inc(sem("gmask_ready"), 1)
                V.tensor_tensor(gexp[:], lg[:, :, 0:NG], top[:, :, 0:1].broadcast_to([P, 3, NG]), sub).then_inc(sem("gdiff_ready"), 1)
                dve.wait_ge(sem("gmask_ready"), 1)
                then(V.tensor_tensor(eprod[:], lg[:, :, NG:NG + NE].rearrange("p t (g e) -> p t e g", g=NG),
                                     gmask[:, :, 0:NG].unsqueeze(2).broadcast_to([P, 3, EPG, NG]), mult))
                then(V.tensor_reduce(esel[:], eprod[:], AX_X, add))
                dve.wait_ge(sem("gexp_ready"), 1)
                V.tensor_reduce(gsum[:, :, 0:1], gexp[:], AX_X, add)
                for tt in range(3):
                    last = V.max(top[:, tt, :], esel[:, tt, :])
                then(last)
                for tt in range(3):
                    last = V.max_index(topi[:, tt, :], top[:, tt, :], esel[:, tt, :])
                then(last)
                V.reciprocal(gsum[:, :, 1:2], gsum[:, :, 0:1])
                V.tensor_copy(topf[:], topi[:])
                V.tensor_tensor(tw[:, :, 0:1], top[:, :, 1:2], top[:, :, 0:1], sub).then_inc(sem("ediff_ready"), 1)
                dve.wait_ge(sem("eexp_ready"), 1)
                then(V.tensor_scalar(tw[:, :, 2:3], tw[:, :, 1:2], 1.0, None, add))
                then(V.reciprocal(tw[:, :, 3:4], tw[:, :, 2:3]))
                then(V.tensor_tensor(tw[:, :, 2:3], tw[:, :, 3:4], gsum[:, :, 1:2], mult))
                then(V.tensor_tensor(tw[:, :, 3:4], tw[:, :, 2:3], tw[:, :, 1:2], mult))
                for tt in range(3):
                    V.tensor_scalar(c8[:, tt, :], slot[:, 0:8], topf[:, tt, 0:1], tw[:, tt, 2:3], ALU.is_equal, mult)
                    last = V.tensor_scalar(c8b[:, tt, :], slot[:, 0:8], topf[:, tt, 1:2], tw[:, tt, 3:4], ALU.is_equal, mult)
                then(last)
                then(V.tensor_tensor(c8[:], c8[:], c8b[:], add))
                for tt in range(3):
                    V.tensor_tensor(comb[:, tt, 0:NG], gmask[:, tt, 0:NG].unsqueeze(2).broadcast_to([P, NG, EPG]),
                                    c8[:, tt, :].unsqueeze(1).broadcast_to([P, NG, EPG]), mult)
                dve.wait_ge(sem("pos_mm"), 1)
                for tt in range(3):
                    V.tensor_copy(pos[rows(tt), tt, 0:NG], psum[1][rows(tt), tt * NG:(tt + 1) * NG])
                then(V.tensor_reduce(cnt[:, 0:1], psum[1][:, 16:16 + NG], AX_X, ALU.max))
                then(V.tensor_scalar(cnt[:, 1:2], cnt[:, 0:1], float(SLOTS), 1.0, ALU.is_gt, add))
                V.tensor_scalar(cnt[:, 2:3], cnt[:, 0:1], float(2 * SLOTS), None, ALU.is_gt).then_inc(sem("cnt_step"), 1)
                dve.wait_ge(sem("cnt_step"), 1)
                V.tensor_tensor(rounds_i[:], cnt[:, 1:2], cnt[:, 2:3], add).then_inc(sem("rounds_ready"), 1)

                def one_hot(g, ahead):
                    V.tensor_copy(pcol[:, 0:2], pos[:, 0:2, bass.ds(g, 1)].rearrange("p t o -> p (t o)"))
                    V.tensor_copy(pcol[0:B, 2:3], pos[0:B, 2, bass.ds(g, 1)])
                    V.tensor_copy(mcol[:], gmask[:, :, bass.ds(g, 1)].rearrange("p t o -> p (t o)"))
                    V.tensor_copy(cg[:], comb[:, :, bass.ds(g, 1), :].rearrange("p t o e -> p t (o e)")).then_inc(sem("cols_ready"), 1)
                    dve.wait_ge(sem("cols_ready"), ahead)
                    for tt in range(3):
                        last = V.tensor_scalar(G[rows(tt), tt, :], slot[rows(tt), :], pcol[rows(tt), tt:tt + 1], mcol[rows(tt), tt:tt + 1], ALU.is_equal, mult)
                    last.then_inc(sem("G_ready"), 1)

                def low_x(ahead):
                    for hf in range(2):
                        dve.wait_ge(sem("xg_high"), 2 * ahead + (hf - 1))
                        hk = slice(4 * hf, 4 * hf + 4)
                        V.tensor_tensor(xgl[:, hk, :], psum[hf][:].rearrange("p (k s) -> p k s", k=4), xgh[:, hk, :].bitcast(F32), sub).then_inc(sem("xg_low"), 1)

                def round_start(rnd):
                    one_hot(0, rnd * (NG + 1) + 1)
                    low_x(rnd * (NG + 1) + 1)

                def group_pre(g, n):
                    dve.wait_ge(sem("gt_mm"), n + 1)
                    V.tensor_scalar(cslot[:], HT[1][:, 0:EPG], 0.5, None, mult).then_inc(sem("cslot_ready"), 1)
                    low_gu(n, 1)

                def experts(n, ahead, following):
                    dve.wait_ge(sem("cslot_ready"), n + 1)
                    for e in range(EPG):
                        p = e % 2
                        turn = pair_turn(n, e)
                        dve.wait_ge(sem(f"th_ready{p}"), turn + 1)
                        V.scalar_tensor_tensor(out=hs[p][:], in0=th[p][:], scalar=1.0, in1=MB[p][:, 0:DE], op0=add, op1=mult).then_inc(sem(f"silu{p}"), 1)
                        dve.wait_ge(sem(f"silu{p}"), turn + 1)
                        V.scalar_tensor_tensor(out=hx[p][:], in0=hs[p][:], scalar=cslot[:, e:e + 1], in1=MB[p][:, DE:2 * DE],
                                               op0=mult, op1=mult).then_inc(sem(f"h_full{p}"), 1)
                        if e + 2 <= EPG:
                            low_gu(n, e + 2, (0,) if e == 0 else (0, 1))
                        dve.wait_ge(sem(f"hh_ready{p}"), turn + 1)
                        V.tensor_tensor(hl[p][:], HT[p][:, 0:2 * SLOTS].rearrange("p (f s) -> p f s", f=2), hh[p][:].bitcast(F32), sub).then_inc(sem(f"h_ready{p}"), 1)
                        if e == 0:
                            low_gu(n, 2, (1,))
                        if e == 2:
                            one_hot(following, ahead)
                    low_x(ahead)

                def group_post(n, ahead):
                    for hf in range(2):
                        hc = slice(hf * 512, (hf + 1) * 512)
                        dve.wait_ge(sem("yt_high"), 2 * n + (hf + 1))
                        V.tensor_tensor(ytl[:, hc], YB[hf][:, :], yth[:, hc].bitcast(F32), sub).then_inc(sem("yt_low"), 1)
                    for tt in range(3):
                        for hf in range(2):
                            hc = slice(hf * 512, (hf + 1) * 512)
                            dve.wait_ge(sem("scat_mm"), n * 6 + 2 * tt + hf + 1)
                            last = V.tensor_tensor(x[rows(tt), tt, hc], x[rows(tt), tt, hc], psum[2 + 2 * tt + hf][rows(tt), :], add)
                            last.then_inc(sem("scat_add"), 1)
    
                def round_end(rnd):
                    for tt in range(3):
                        last = V.tensor_scalar(pos[rows(tt), tt, :], pos[rows(tt), tt, :], -float(SLOTS), None, add)
                    last.then_inc(sem("pos_shifted"), 1)
                    settle(dve)
                    dve.wait_ge(sem("pos_shifted"), rnd + 1)

                loop(dve, group_pre, experts, group_post, round_start, round_end)
                dve.sem_inc(sem("moe_done"), 1)
                dve.wait_ge(sem("gfin_in"), 16)
                for tt in range(3):
                    dve.wait_ge(sem("x2_root"), tt + 1)
                    V.reciprocal(stat[rows(tt), tt, 2:3], stat[rows(tt), tt, 1:2]).then_inc(sem("x2_inv"), 1)
                    dve.wait_ge(sem("x2_inv"), tt + 1)
                    V.scalar_tensor_tensor(out=xn[rows(tt), tt, :], in0=x[rows(tt), tt, :], scalar=stat[rows(tt), tt, 2:3],
                                           in1=gfin[rows(tt), :], op0=mult, op1=mult).then_inc(sem("y_final"), 1)


_INS = ['x_prompt', 'x_sample', 'state_ret', 'state_rwkv', 'state_shift', 'norm_mix', 'w_in', 'mu_shift', 'ret_gn_w',
        'rwkv_w0', 'rwkv_w2', 'rwkv_a0', 'rwkv_a2', 'rwkv_g2', 'rwkv_k_k', 'rwkv_k_a', 'rwkv_r_k', 'rwkv_lnx_w',
        'rwkv_lnx_b', 'w_out', 'norm_ffn', 'router_group_w', 'router_group_b', 'router_expert_w', 'router_expert_b',
        'expert_w_gate', 'expert_w_up', 'expert_w_down', 'norm_final']
_OUTS = [("y_p", (1, TP, D)), ("y_s", (B, 1, D)), ("ret_p", (1, 1, HEADS, P, P)), ("rwkv_p", (1, 1, RH, HD, HD)),
         ("shift_p", (1, 1, D)), ("ret_s", (1, B, HEADS, P, P)), ("rwkv_s", (1, B, RH, HD, HD)), ("shift_s", (1, B, D))]


def kernel(**inputs):
    import numpy as _np
    import concourse.bacc as _bacc
    from concourse import mybir as _mybir
    from concourse.bass_utils import run_bass_kernel_spmd as _run

    nc = _bacc.Bacc("TRN2", target_bir_lowering=False, num_devices=1)
    arrays, args, consts, outs = {}, {}, {}, {}
    for name in _INS:
        arr = _np.ascontiguousarray(inputs[name])
        arrays[f"in_{name}_dram"] = arr
        args[name] = nc.dram_tensor(f"in_{name}_dram", arr.shape, _mybir.dt.from_np(arr.dtype), kind="ExternalInput").ap()
    for name, arr in constants().items():
        arrays[f"const_{name}_dram"] = arr
        consts[name] = nc.dram_tensor(f"const_{name}_dram", arr.shape, _mybir.dt.from_np(arr.dtype), kind="ExternalInput").ap()
    for name, shape in _OUTS:
        outs[name] = nc.dram_tensor(f"out_{name}_dram", shape, _mybir.dt.float32, kind="ExternalOutput").ap()
    hybrid_moe_step(nc, args, outs, consts)
    res = _run(nc, [arrays], core_ids=[0]).results[0]
    return tuple(res[f"out_{name}_dram"] for name, _ in _OUTS)
```
